# Optimizing a Trainium2 kernel written in Bass

```python
import math
import jax, jax.numpy as jnp
from jax import lax
import numpy as np

D_MODEL = 1024
BATCH = 1
SEQ = 512
DEPTH = 1

CHUNK = 64
Q_BLOCK = 128
PLE_DIM = 256
D_MIX = D_MODEL
D_ATTN = D_MIX // 2
D_CONV = D_MIX - D_ATTN
N_HEADS_A = 4
HEAD_DIM_V = D_ATTN // N_HEADS_A
HEAD_DIM_QK = HEAD_DIM_V // 2
CONV_WIDTH = 3
N_IN_PARTS = 8
D_IN = 4 * D_ATTN + 4 * D_CONV
EPS = 1e-6
SUBLN_EPS = 1e-5


def rms_norm(x, gain, eps=EPS):
    xf = x.astype(jnp.float32)
    y = xf * lax.rsqrt(jnp.mean(xf * xf, axis=-1, keepdims=True) + eps)
    return (y * gain.astype(jnp.float32)).astype(x.dtype)

def alibi_slopes(n_heads):
    return jnp.exp2(-8.0 * jnp.arange(1, n_heads + 1, dtype=jnp.float32) / n_heads)

def diff_attention(q, k, v, lam, slopes):
    seq = q.shape[1]
    scale = HEAD_DIM_QK ** -0.5
    outs = []
    for q0 in range(0, seq, Q_BLOCK):
        k_end = q0 + Q_BLOCK
        t = jnp.arange(q0, k_end)
        s = jnp.arange(k_end)
        scores = jnp.einsum('bqhmd,bkhmd->bhmqk', q[:, q0:k_end], k[:, :k_end]).astype(jnp.float32) * scale
        dist = jnp.abs(t[:, None] - s[None, :]).astype(jnp.float32)
        allowed = (s[None, :] // CHUNK) <= (t[:, None] // CHUNK)
        bias = jnp.where(allowed[None], -slopes[:, None, None] * dist[None], -jnp.inf)
        probs = jax.nn.softmax(scores + bias[None, :, None], axis=-1)
        weights = probs[:, :, 0] - lam * probs[:, :, 1]
        outs.append(jnp.einsum('bhqk,bkhd->bqhd', weights.astype(v.dtype), v[:, :k_end]))
    return jnp.concatenate(outs, axis=1)

def first_inputs(seed: int = 0) -> dict:
    key = jax.random.key(seed)
    ks = jax.random.split(key, 16)
    f32 = jnp.float32
    x = jax.random.normal(ks[0], (BATCH, SEQ, D_MODEL), f32)
    p = jax.random.normal(ks[1], (DEPTH, BATCH, SEQ, PLE_DIM), f32)
    pre_norm_gain = 1.0 + 0.02 * jax.random.normal(ks[2], (DEPTH, D_MODEL), f32)
    w_in = jax.random.normal(ks[3], (DEPTH, D_MODEL, D_IN), f32) * D_MODEL ** -0.5
    lambda_q1 = 0.1 * jax.random.normal(ks[4], (DEPTH, HEAD_DIM_QK), f32)
    lambda_k1 = 0.1 * jax.random.normal(ks[5], (DEPTH, HEAD_DIM_QK), f32)
    lambda_q2 = 0.1 * jax.random.normal(ks[6], (DEPTH, HEAD_DIM_QK), f32)
    lambda_k2 = 0.1 * jax.random.normal(ks[7], (DEPTH, HEAD_DIM_QK), f32)
    subln_gain = 1.0 + 0.02 * jax.random.normal(ks[8], (DEPTH, HEAD_DIM_V), f32)
    conv_w = jax.random.normal(ks[9], (DEPTH, CONV_WIDTH, D_CONV), f32) * CONV_WIDTH ** -0.5
    w_out = jax.random.normal(ks[10], (DEPTH, D_MIX, D_MODEL), f32) * D_MIX ** -0.5
    post_norm_gain = 1.0 + 0.02 * jax.random.normal(ks[11], (DEPTH, D_MODEL), f32)
    w_ple_proj = jax.random.normal(ks[12], (DEPTH, PLE_DIM, D_MODEL), f32) * PLE_DIM ** -0.5
    ple_norm_gain = 1.0 + 0.02 * jax.random.normal(ks[13], (DEPTH, D_MODEL), f32)
    w_ple_gate = jax.random.normal(ks[14], (DEPTH, D_MODEL, D_MODEL), f32) * D_MODEL ** -0.5
    return {"x": x, "p": p, "pre_norm_gain": pre_norm_gain, "w_in": w_in,
            "lambda_q1": lambda_q1, "lambda_k1": lambda_k1, "lambda_q2": lambda_q2,
            "lambda_k2": lambda_k2, "subln_gain": subln_gain, "conv_w": conv_w,
            "w_out": w_out, "post_norm_gain": post_norm_gain, "w_ple_proj": w_ple_proj,
            "ple_norm_gain": ple_norm_gain, "w_ple_gate": w_ple_gate}

def first_block(x, p, pre_norm_gain, w_in, lambda_q1, lambda_k1, lambda_q2, lambda_k2,
              subln_gain, conv_w, w_out, post_norm_gain, w_ple_proj, ple_norm_gain, w_ple_gate):
    bsz, seq, _ = x.shape
    slopes = alibi_slopes(N_HEADS_A)
    for i in range(DEPTH):
        lambda_init = 0.8 - 0.6 * math.exp(-0.3 * i)
        h = rms_norm(x, pre_norm_gain[i])
        proj = h @ w_in[i]
        q, k, v, z_a, b_gate, c_gate, u, z_c = jnp.split(proj, N_IN_PARTS, axis=-1)

        q = q.reshape(bsz, seq, N_HEADS_A, 2, HEAD_DIM_QK)
        k = k.reshape(bsz, seq, N_HEADS_A, 2, HEAD_DIM_QK)
        v = v.reshape(bsz, seq, N_HEADS_A, HEAD_DIM_V)
        lam = (jnp.exp(jnp.sum((lambda_q1[i] * lambda_k1[i]).astype(jnp.float32)))
               - jnp.exp(jnp.sum((lambda_q2[i] * lambda_k2[i]).astype(jnp.float32)))
               + lambda_init)
        attn = diff_attention(q, k, v, lam, slopes)
        attn = rms_norm(attn, subln_gain[i], SUBLN_EPS) * (1.0 - lambda_init)
        attn = attn.reshape(bsz, seq, D_ATTN) * jax.nn.silu(z_a)

        g = c_gate * u
        g_pad = jnp.pad(g, ((0, 0), (CONV_WIDTH - 1, 0), (0, 0)))
        conv = conv_w[i, 0] * g_pad[:, 0:seq]
        for j in range(1, CONV_WIDTH):
            conv = conv + conv_w[i, j] * g_pad[:, j:j + seq]
        conv_out = b_gate * conv * jax.nn.silu(z_c)

        mixed = jnp.concatenate([attn, conv_out], axis=-1) @ w_out[i]
        x = x + rms_norm(mixed, post_norm_gain[i])

        e = rms_norm(p[i] @ w_ple_proj[i], ple_norm_gain[i])
        x = x + jax.nn.sigmoid(x @ w_ple_gate[i]) * e
    return x


N_META = 16

MLA_HEADS = 8
MLA_Q_RANK = 384
MLA_KV_RANK = 256
MLA_NOPE = 128
MLA_ROPE = 64
MLA_V = 128
ROPE_HALF = MLA_ROPE // 2
ROPE_THETA = 10000.0

GLA_HEADS = 4
GLA_DK = D_MODEL // 2
GLA_DV = D_MODEL
GLA_HK = GLA_DK // GLA_HEADS
GLA_HV = GLA_DV // GLA_HEADS
GLA_GATE_RANK = 16
GLA_TAU = 16.0
GLA_CHUNK = 16

PEER_HEADS = 8
PEER_NKEYS = 128
PEER_EXPERTS = PEER_NKEYS * PEER_NKEYS
PEER_QDIM = 256
PEER_HALF = PEER_QDIM // 2
PEER_TOPK = 16
PEER_BLOCK = 16

SPLITS = (MLA_Q_RANK, MLA_KV_RANK, MLA_ROPE, GLA_DK, GLA_DK, GLA_DV, GLA_GATE_RANK, GLA_DV, D_MODEL, D_MODEL)
D_IN_2 = MLA_Q_RANK + MLA_KV_RANK + MLA_ROPE + 2 * GLA_DK + GLA_DV + GLA_GATE_RANK + GLA_DV + 2 * D_MODEL


def rmsnorm(x, g):
    x32 = x.astype(jnp.float32)
    y = x32 * lax.rsqrt(jnp.mean(x32 * x32, axis=-1, keepdims=True) + EPS)
    return (y * g.astype(jnp.float32)).astype(x.dtype)

def rope_tables(n):
    inv_freq = ROPE_THETA ** (-jnp.arange(ROPE_HALF, dtype=jnp.float32) / ROPE_HALF)
    ang = jnp.arange(n, dtype=jnp.float32)[:, None] * inv_freq[None, :]
    return jnp.cos(ang), jnp.sin(ang)

def rope(x, cos, sin):
    x32 = x.astype(jnp.float32)
    x1, x2 = x32[..., :ROPE_HALF], x32[..., ROPE_HALF:]
    return jnp.concatenate([x1 * cos - x2 * sin, x2 * cos + x1 * sin], axis=-1).astype(x.dtype)

def mla_branch(c_q, c_kv, k_pe, q_norm, w_uq, kv_norm, w_ukv, qn_nope, qn_pe, kn_nope, kn_pe, cos, sin, cid):
    B, L, _ = c_q.shape
    q = (rmsnorm(c_q, q_norm) @ w_uq).reshape(B, L, MLA_HEADS, MLA_NOPE + MLA_ROPE)
    kv = (rmsnorm(c_kv, kv_norm) @ w_ukv).reshape(B, L, MLA_HEADS, MLA_NOPE + MLA_V)
    q_nope = rmsnorm(q[..., :MLA_NOPE], qn_nope)
    q_pe = rope(rmsnorm(q[..., MLA_NOPE:], qn_pe), cos[:, None, :], sin[:, None, :])
    k_nope = rmsnorm(kv[..., :MLA_NOPE], kn_nope)
    v = kv[..., MLA_NOPE:]
    k_pe = rope(rmsnorm(k_pe, kn_pe), cos, sin)
    scale = (MLA_NOPE + MLA_ROPE) ** -0.5
    lp = cid.shape[0]
    nb = lp // Q_BLOCK
    pad = ((0, 0), (0, lp - L), (0, 0), (0, 0))
    qn_b = jnp.pad(q_nope, pad).reshape(B, nb, Q_BLOCK, MLA_HEADS, MLA_NOPE).transpose(1, 0, 2, 3, 4)
    qp_b = jnp.pad(q_pe, pad).reshape(B, nb, Q_BLOCK, MLA_HEADS, MLA_ROPE).transpose(1, 0, 2, 3, 4)
    cq_b = cid.reshape(nb, Q_BLOCK)
    cid_k = cid[:L]

    def attend(blk):
        qn, qp, cq = blk
        s = (jnp.einsum('bqhd,bkhd->bhqk', qn, k_nope) + jnp.einsum('bqhd,bkd->bhqk', qp, k_pe)).astype(jnp.float32) * scale
        mask = cid_k[None, :] <= cq[:, None]
        s = jnp.where(mask, s, -jnp.inf)
        w = jax.nn.softmax(s, axis=-1).astype(v.dtype)
        return jnp.einsum('bhqk,bkhd->bqhd', w, v)

    out = lax.map(attend, (qn_b, qp_b, cq_b))
    out = out.transpose(1, 0, 2, 3, 4).reshape(B, lp, MLA_HEADS * MLA_V)
    return out[:, :L]

def gla_branch(gq, gk, gv, ga, gg, w_a2, b_a, g_norm):
    B, L, _ = gq.shape
    nc = L // GLA_CHUNK
    q = gq.reshape(B, L, GLA_HEADS, GLA_HK) * (GLA_HK ** -0.5)
    k = gk.reshape(B, L, GLA_HEADS, GLA_HK)
    v = gv.reshape(B, L, GLA_HEADS, GLA_HV)
    log_a = jax.nn.log_sigmoid((ga @ w_a2 + b_a).astype(jnp.float32)) / GLA_TAU
    log_a = log_a.reshape(B, L, GLA_HEADS, GLA_HK)

    def to_chunks(t):
        return t.reshape(B, nc, GLA_CHUNK, GLA_HEADS, t.shape[-1]).transpose(1, 0, 3, 2, 4).astype(jnp.float32)

    tri = jnp.tril(jnp.ones((GLA_CHUNK, GLA_CHUNK), dtype=bool))

    def step(S, inp):
        qc, kc, vc, lac = inp
        bcum = jnp.cumsum(lac, axis=2)
        o_inter = jnp.einsum('bhcd,bhde->bhce', qc * jnp.exp(bcum), S)
        diff = bcum[:, :, :, None, :] - bcum[:, :, None, :, :]
        decay = jnp.exp(jnp.where(tri[None, None, :, :, None], diff, -jnp.inf))
        A = jnp.einsum('bhid,bhjd,bhijd->bhij', qc, kc, decay)
        o_intra = jnp.einsum('bhij,bhje->bhie', A, vc)
        b_last = bcum[:, :, -1]
        k_dec = kc * jnp.exp(b_last[:, :, None, :] - bcum)
        S = jnp.exp(b_last)[..., None] * S + jnp.einsum('bhcd,bhce->bhde', k_dec, vc)
        return S, o_inter + o_intra

    S0 = jnp.zeros((B, GLA_HEADS, GLA_HK, GLA_HV), jnp.float32)
    _, o = lax.scan(step, S0, (to_chunks(q), to_chunks(k), to_chunks(v), to_chunks(log_a)))
    o = o.transpose(1, 0, 3, 2, 4).reshape(B, L, GLA_HEADS, GLA_HV).astype(gq.dtype)
    o = rmsnorm(o, g_norm).reshape(B, L, GLA_DV)
    return o * jax.nn.silu(gg)

def peer_ffn(h, w_q, sub_keys, u_tab, v_tab):
    B, L, D = h.shape
    q = (h @ w_q).reshape(B, L, PEER_HEADS, 2, PEER_HALF)
    s = jnp.einsum('blhpd,pnd->blhpn', q, sub_keys).astype(jnp.float32)
    top_s, top_i = lax.top_k(s, PEER_TOPK)
    cand_s = top_s[..., 0, :, None] + top_s[..., 1, None, :]
    cand_i = top_i[..., 0, :, None] * PEER_NKEYS + top_i[..., 1, None, :]
    best_s, best_pos = lax.top_k(cand_s.reshape(B, L, PEER_HEADS, PEER_TOPK * PEER_TOPK), PEER_TOPK)
    idx = jnp.take_along_axis(cand_i.reshape(B, L, PEER_HEADS, PEER_TOPK * PEER_TOPK), best_pos, axis=-1)
    gate = jax.nn.softmax(best_s, axis=-1)
    nb = L // PEER_BLOCK

    def blocks(t):
        return t.reshape((B, nb, PEER_BLOCK) + t.shape[2:]).swapaxes(0, 1)

    def expert_block(inp):
        hb, ib, gb = inp
        u = u_tab[ib]
        act = jax.nn.gelu(jnp.einsum('bpd,bphkd->bphk', hb, u).astype(jnp.float32), approximate=False)
        coef = (act * gb).astype(hb.dtype)
        return jnp.einsum('bphk,bphkd->bpd', coef, v_tab[ib])

    out = lax.map(expert_block, (blocks(h), blocks(idx), blocks(gate)))
    return out.swapaxes(0, 1).reshape(B, L, D)

def second_inputs(seed: int = 0) -> dict:
    key = jax.random.key(seed)
    ks = jax.random.split(key, 24)
    f32 = jnp.float32

    def nrm(k, shape, fan_in):
        return jax.random.normal(k, shape, f32) * (fan_in ** -0.5)

    def gain(k, shape):
        return 1.0 + 0.02 * jax.random.normal(k, shape, f32)

    return {
        "x": jax.random.normal(ks[0], (BATCH, SEQ, D_MODEL), f32),
        "meta": jax.random.normal(ks[1], (N_META, D_MODEL), f32),
        "norm_mix": gain(ks[2], (DEPTH, D_MODEL)),
        "w_in": nrm(ks[3], (DEPTH, D_MODEL, D_IN_2), D_MODEL),
        "mla_q_norm": gain(ks[4], (DEPTH, MLA_Q_RANK)),
        "mla_w_uq": nrm(ks[5], (DEPTH, MLA_Q_RANK, MLA_HEADS * (MLA_NOPE + MLA_ROPE)), MLA_Q_RANK),
        "mla_kv_norm": gain(ks[6], (DEPTH, MLA_KV_RANK)),
        "mla_w_ukv": nrm(ks[7], (DEPTH, MLA_KV_RANK, MLA_HEADS * (MLA_NOPE + MLA_V)), MLA_KV_RANK),
        "qn_nope": gain(ks[8], (DEPTH, MLA_NOPE)),
        "qn_pe": gain(ks[9], (DEPTH, MLA_ROPE)),
        "kn_nope": gain(ks[10], (DEPTH, MLA_NOPE)),
        "kn_pe": gain(ks[11], (DEPTH, MLA_ROPE)),
        "gla_w_a2": nrm(ks[12], (DEPTH, GLA_GATE_RANK, GLA_DK), GLA_GATE_RANK),
        "gla_b_a": 0.1 * jax.random.normal(ks[13], (DEPTH, GLA_DK), f32),
        "gla_norm": gain(ks[14], (DEPTH, GLA_HV)),
        "w_o_mla": nrm(ks[15], (DEPTH, MLA_HEADS * MLA_V, D_MODEL), MLA_HEADS * MLA_V),
        "w_o_gla": nrm(ks[16], (DEPTH, GLA_DV, D_MODEL), GLA_DV),
        "w_out": nrm(ks[17], (DEPTH, D_MODEL, D_MODEL), D_MODEL),
        "norm_ffn": gain(ks[18], (DEPTH, D_MODEL)),
        "peer_w_q": nrm(ks[19], (DEPTH, D_MODEL, PEER_HEADS * PEER_QDIM), D_MODEL),
        "peer_keys": nrm(ks[20], (DEPTH, 2, PEER_NKEYS, PEER_HALF), PEER_HALF),
        "peer_u": nrm(ks[21], (DEPTH, PEER_EXPERTS, D_MODEL), D_MODEL),
        "peer_v": nrm(ks[22], (DEPTH, PEER_EXPERTS, D_MODEL), PEER_HEADS),
    }

def second_block(x, meta, norm_mix, w_in, mla_q_norm, mla_w_uq, mla_kv_norm, mla_w_ukv, qn_nope, qn_pe, kn_nope, kn_pe, gla_w_a2, gla_b_a, gla_norm, w_o_mla, w_o_gla, w_out, norm_ffn, peer_w_q, peer_keys, peer_u, peer_v):
    B = x.shape[0]
    h = jnp.concatenate([jnp.broadcast_to(meta.astype(x.dtype)[None], (B, N_META, D_MODEL)), x], axis=1)
    L = h.shape[1]
    lp = -(-L // Q_BLOCK) * Q_BLOCK
    pos = jnp.arange(lp)
    cid = jnp.where(pos < N_META, 0, 1 + (pos - N_META) // CHUNK)
    cos, sin = rope_tables(L)
    offsets = [int(o) for o in np.cumsum(SPLITS)[:-1]]
    for l in range(DEPTH):
        n = rmsnorm(h, norm_mix[l])
        parts = jnp.split(n @ w_in[l], offsets, axis=-1)
        c_q, c_kv, k_pe, gq, gk, gv, ga, gg, gate_a, gate_b = parts
        y_a = mla_branch(c_q, c_kv, k_pe, mla_q_norm[l], mla_w_uq[l], mla_kv_norm[l], mla_w_ukv[l], qn_nope[l], qn_pe[l], kn_nope[l], kn_pe[l], cos, sin, cid)
        y_b = gla_branch(gq, gk, gv, ga, gg, gla_w_a2[l], gla_b_a[l], gla_norm[l])
        mix = jax.nn.sigmoid(gate_a) * (y_a @ w_o_mla[l]) + jax.nn.sigmoid(gate_b) * (y_b @ w_o_gla[l])
        h = h + mix @ w_out[l]
        h = h + peer_ffn(rmsnorm(h, norm_ffn[l]), peer_w_q[l], peer_keys[l], peer_u[l], peer_v[l])
    return h[:, N_META:]


def setup_inputs(seed=0):
    out = dict(first_inputs(seed))
    for name, value in second_inputs(seed + 1).items():
        if name != "x":
            out[name + "_2"] = value
    return out


def reference(
    x, p, pre_norm_gain, w_in, lambda_q1, lambda_k1, lambda_q2, lambda_k2, subln_gain, conv_w,
    w_out, post_norm_gain, w_ple_proj, ple_norm_gain, w_ple_gate, meta_2, norm_mix_2, w_in_2,
    mla_q_norm_2, mla_w_uq_2, mla_kv_norm_2, mla_w_ukv_2, qn_nope_2, qn_pe_2, kn_nope_2,
    kn_pe_2, gla_w_a2_2, gla_b_a_2, gla_norm_2, w_o_mla_2, w_o_gla_2, w_out_2, norm_ffn_2,
    peer_w_q_2, peer_keys_2, peer_u_2, peer_v_2,
):
    x = first_block(
        x, p, pre_norm_gain, w_in, lambda_q1, lambda_k1, lambda_q2, lambda_k2, subln_gain,
        conv_w, w_out, post_norm_gain, w_ple_proj, ple_norm_gain, w_ple_gate,
    )
    return second_block(
        x, meta_2, norm_mix_2, w_in_2, mla_q_norm_2, mla_w_uq_2, mla_kv_norm_2, mla_w_ukv_2,
        qn_nope_2, qn_pe_2, kn_nope_2, kn_pe_2, gla_w_a2_2, gla_b_a_2, gla_norm_2, w_o_mla_2,
        w_o_gla_2, w_out_2, norm_ffn_2, peer_w_q_2, peer_keys_2, peer_u_2, peer_v_2,
    )


_drawn_inputs = setup_inputs


def setup_inputs(seed=0):
    import zlib

    import numpy as np

    out = dict(_drawn_inputs(seed))
    spreads = {}
    factors = {'lambda_k1': 2.709,
     'lambda_q2': 2.903,
     'subln_gain': 3.712,
     'post_norm_gain': 2.822,
     'ple_norm_gain': 4.058,
     'norm_mix_2': 3.971,
     'mla_q_norm_2': 8.0,
     'mla_kv_norm_2': 8.0,
     'qn_nope_2': 8.0,
     'qn_pe_2': 8.0,
     'kn_nope_2': 8.0,
     'kn_pe_2': 8.0,
     'gla_b_a_2': 3.8,
     'gla_norm_2': 22.13,
     'norm_ffn_2': 25.768}
    for name, (base, spread) in spreads.items():
        noise = np.random.default_rng([zlib.crc32(name.encode()), seed]).standard_normal(out[name].shape)
        drawn = base * np.exp(spread * noise) if base else spread * noise
        out[name] = __import__('jax').numpy.asarray(drawn.astype(out[name].dtype))
    for name, factor in factors.items():
        out[name] = (out[name] * factor).astype(out[name].dtype)
    return out
```

```python
from contextlib import ExitStack

import numpy as np

import concourse.bass as bass
from concourse import mybir

F32 = mybir.dt.float32
U32 = mybir.dt.uint32
ALU = mybir.AluOpType
ACT = mybir.ActivationFunctionType
AX_X = mybir.AxisListType.X

P = 128
D = 1024
KD = D // P
T = 512
TT = T // P
META = 16
TM = T + META
CHUNK = 64
NEG = -1e30

HA = 4
DQK = 64
SCALE_A = DQK ** -0.5
SLOPES = [2.0 ** (-8.0 * (h + 1) / HA) for h in range(HA)]
LAMBDA_INIT = 0.8 - 0.6
HM = 8
ROPE = 64
SCALE_M = (128 + ROPE) ** -0.5
HG = 4
HK = 128
HV = 256
TAU = 16.0
LEVELS = [64, 32, 16, 8, 4, 2, 1]
HP = 8
NKEYS = 128
TOPK = 16
ENTRIES = HP * TOPK
NE = NKEYS * NKEYS
EG = 4
GROUPS = NKEYS // EG
HALF = 64

EPS = 1e-6
SUBLN_EPS = 1e-5

CONST = {}
_at = 0
for _name, _n in (("ident", P), ("ones", P), ("heads64", P), ("rot", P), ("iota", P), ("dist", T),
                  ("levels", 8 * P), ("reset", TM), ("cos", TM), ("sin", TM)):
    CONST[_name] = (_at, _n)
    _at += _n
NCONST = _at

VEC = {}
_at = 0
for _name, _n in (("pre", 8), ("mix", 8), ("subln", 1), ("conv", 12), ("post", 8), ("ple", 8), ("qnorm", 3),
                  ("kvnorm", 2), ("qn", 1), ("kn", 1), ("qp", 1), ("kp", 1), ("ba", 4), ("gnorm", 2),
                  ("ffn", 8), ("lam", 4), ("eps", 1), ("subeps", 1)):
    VEC[_name] = (_at, _n)
    _at += _n
NVEC = _at

WEIGHTS = [("q", 8, 512), ("k", 8, 512), ("v", 8, 512), ("c", 8, 512), ("u", 8, 512), ("zc", 8, 512), ("b", 8, 512),
           ("za", 8, 512), ("wo0", 8, 512), ("wo1", 8, 512), ("ple", 2, 1024), ("pg0", 8, 512), ("pg1", 8, 512),
           ("cq", 8, 384), ("ckv", 8, 384), ("uqn", 3, 1024), ("uqp", 3, 512), ("ukv", 2, 2048),
           ("gq", 8, 512), ("gk", 8, 512), ("ga", 8, 16), ("gv0", 8, 512), ("gv1", 8, 512),
           ("gg0", 8, 512), ("gg1", 8, 512), ("ta0", 8, 512), ("oa0", 8, 512), ("ta1", 8, 512), ("oa1", 8, 512),
           ("tb0", 8, 512), ("ob0", 8, 512), ("tb1", 8, 512), ("ob1", 8, 512), ("w20", 8, 512), ("w21", 8, 512),
           ("pq0", 8, 512), ("pq1", 8, 512), ("pq2", 8, 512), ("pq3", 8, 512)]
WSLOT = 4096
NW = 3
WN = {w[0]: n for n, w in enumerate(WEIGHTS)}
WAT = {}
_at = 0
for _name, _k, _n in WEIGHTS:
    WAT[_name] = _at
    _at += _k * _n
NWTOT = _at

UNITS_A = [(h, i) for h in range(HA) for i in range(TT)]
UNITS_M = [(h, i) for h in range(HM) for i in range(TT)]


PARTS = [f"qn{m}" for m in range(4)] + [f"qp{m}" for m in range(2)] + [f"kn{h}" for h in range(HM)]


def psum_jobs():
    jobs = [("lam",), ("ss", "n1")]
    for g in ("q", "k", "v"):
        jobs += [(g, 0), (g, 1)]
    side = [(g, m) for g in ("c", "u", "zc", "b", "za") for m in (0, 1)]
    jobs.append(("S", 0))
    for u in range(len(UNITS_A)):
        if u + 1 < len(UNITS_A):
            jobs.append(("S", u + 1))
        if side:
            jobs.append(side.pop(0))
        jobs += [("T", u), ("O", u)]
    jobs += [("ss", "sl0"), ("ss", "sl1")]
    jobs += [("wo", m) for m in range(4)] + [("ple", m) for m in range(4)] + [("ss", "post"), ("ss", "ple")]
    jobs += [("pg", m) for m in range(4)]
    jobs.append(("ss", "mix"))
    jobs += [("cq", 0), ("cq", 1), ("ckv", 0), ("ckv", 1), ("kpe", 0)]
    jobs += [("ss", "cq"), ("ss", "ckv"), ("ss", "kpe"), ("rot", "kpe")]
    for n, name in enumerate(PARTS):
        jobs.append(({"qn": "uqn", "qp": "uqp", "kn": "kn"}[name[0:2]], int(name[2:])))
        if n >= 1:
            jobs.append(("ss", PARTS[n - 1]))
        if n >= 3 and PARTS[n - 3][0:2] == "qp":
            jobs.append(("rot", int(PARTS[n - 3][2:])))
    jobs.append(("ss", PARTS[-1]))
    jobs += [("mv", t) for t in range(TT + 1)]
    jobs.append(("MS", 0))
    for u in range(len(UNITS_M)):
        if u + 1 < len(UNITS_M):
            jobs.append(("MS", u + 1))
        jobs += [("MT", u), ("MO", u)]
    jobs += [("gq", 0), ("gq", 1)] + [("gk", h) for h in range(HG)] + [("ga", 0)]
    jobs += [("gv", g, m) for g in (0, 1) for m in (0, 1, 2)]
    for h in range(HG):
        jobs += [("z", h)] + [("lev", h, n) for n in range(8)] + [("kd", h)]
        jobs += [("st", h, c) for c in range(TT)] + [("go", h)]
    jobs += [("ss", f"g{h}") for h in range(HG)]
    jobs += [("gg", h) for h in range(HG)]
    for side_ab in "ab":
        for m in range(4):
            jobs += [("t" + side_ab, m), ("o" + side_ab, m)]
    jobs += [("w2", m) for m in range(4)]
    jobs.append(("ss", "ffn"))
    jobs += [("pq", m) for m in range(8)]
    for t in range(TT):
        jobs += [("ps", t, 0), ("ps", t, 1), ("tr", t)]
    return {key: n for n, key in enumerate(jobs)}


JOB = psum_jobs()
NPAIR = 4

LAST = {"q": ("q", 1), "k": ("k", 1), "v": ("v", 1), "c": ("c", 1), "u": ("u", 1), "zc": ("zc", 1), "b": ("b", 1),
        "za": ("za", 1), "wo0": ("wo", 1), "wo1": ("wo", 3), "ple": ("ple", 3), "pg0": ("pg", 1), "pg1": ("pg", 3),
        "cq": ("cq", 1), "ckv": ("kpe", 0), "uqn": ("uqn", 3), "uqp": ("uqp", 1), "ukv": ("mv", TT),
        "gq": ("gq", 1), "gk": ("gk", HG - 1), "ga": ("ga", 0), "gv0": ("gv", 0, 2), "gv1": ("gv", 1, 2),
        "gg0": ("gg", 1), "gg1": ("gg", 3), "ta0": ("ta", 1), "ta1": ("ta", 3), "tb0": ("tb", 1), "tb1": ("tb", 3),
        "oa0": ("oa", 1), "oa1": ("oa", 3), "ob0": ("ob", 1), "ob1": ("ob", 3), "w20": ("w2", 1), "w21": ("w2", 3),
        "pq0": ("pq", 1), "pq1": ("pq", 3), "pq2": ("pq", 5), "pq3": ("pq", 7)}

NORMS = ([("n1", D, True), ("sl0", 128, False), ("sl1", 128, False), ("post", D, True), ("ple", D, True),
          ("mix", D, True), ("cq", 384, True), ("ckv", 256, False), ("kpe", 64, False)]
         + [(f"qn{m}", 128, False) for m in range(4)] + [(f"qp{m}", 64, False) for m in range(2)]
         + [(f"kn{h}", 128, False) for h in range(HM)] + [(f"g{h}", 256, False) for h in range(HG)]
         + [("ffn", D, True)])
NORM = {n[0]: k for k, n in enumerate(NORMS)}


def build(nc, A):
    ctx = ExitStack()
    with ctx:
        def sb(name, shape, dt=F32):
            return ctx.enter_context(nc.sbuf_tensor(name, shape, dt))

        def sem(name):
            return ctx.enter_context(nc.semaphore(name))

        wring = sb("wring", [P, NW * WSLOT])
        cst = sb("cst", [P, NCONST])
        vec = sb("vec", [P, NVEC])
        resid = sb("resid", [P, KD, TM])
        normed_x = sb("normed_x", [P, KD, TM])
        sqbuf = sb("sqbuf", [P, KD * TM])
        rt = sb("rt", [P, 2, 1056])
        small = sb("small", [P, 320])
        AREA = 21560
        area = sb("area", [P, AREA])
        ps = ctx.enter_context(nc.psum_tensor("ps", [P, 8, 512], F32))

        def C(name, a=0, b=None):
            at, n = CONST[name]
            return cst[:, at + a:at + (n if b is None else b)]

        def V(name, i=0):
            at, _ = VEC[name]
            return vec[:, at + i:at + i + 1]

        def view(start, *dims):
            n = int(np.prod(dims))
            assert start + n <= AREA, (start, dims)
            flat = area[:, start:start + n]
            if len(dims) == 1:
                return flat
            if len(dims) == 2:
                return flat.rearrange("p (a b) -> p a b", a=dims[0])
            return flat.rearrange("p (a b c) -> p a b c", a=dims[0], b=dims[1])

        xs = resid[:, :, 0:T]
        hs = normed_x[:, :, 0:T]
        small_sq = [sqbuf[:, 0:1056], sqbuf[:, 1056:2112]]
        sq_hi = sqbuf[:, 2112:4224]

        qT = view(0, 4, T)
        kT = view(2048, 4, T)
        v_tok = view(4096, TT, 512)
        zaT = view(6144, 4, T)
        gT = view(8192, 4, T + 2)
        szT = view(10248, 4, T)
        mixin = view(12296, KD, T)
        probs = view(16392, 2, 2, 512)
        weights_p = view(18440, 2, 512)
        pT_sb = view(19464, 2, 512)
        pin = view(20488, 2, T)
        cT = sqbuf[:, 2112:4160].rearrange("p (a b) -> p a b", a=4)
        mixedT = view(0, KD, T)
        eT = view(4096, KD, T)
        sgT = view(8192, KD, T)
        qn = view(0, HM, T)
        qp = view(4096, 4, T)
        kn = view(6144, HM, TM)
        mv = view(10368, TT, 1024)
        mvm = view(14464, 1024)
        ya = view(15488, HM, T)
        cq = view(15488, 3, T)
        ckv = view(17024, 2, TM)
        mpt = view(19584, 2, 640)
        mp = sq_hi[:, 0:1056].rearrange("p (a b) -> p a b", a=2)
        kp = sq_hi[:, 1056:1056 + TM]
        rot_tmp = view(19584, 1056)
        gq = view(0, HG, T)
        gk = view(2048, HG, TM)
        gv = view(4160, TT, 1024)
        gvm = view(8256, 1024)
        oT = view(9280, KD, T)
        la = view(13376, TM)
        bc = view(13904, TM)
        dec = view(14432, 8)
        gaT = view(14448, TM)
        wl = sqbuf[:, 2112:2112 + TM]
        ql = sqbuf[:, 2640:2640 + T]
        kl = sqbuf[:, 3152:3152 + TM]
        attT = sqbuf[:, 3680:3680 + T]
        state = view(19584, TT, HV)
        kdt = view(20608, TT + 1, P)
        qb = view(14976, T)
        gate_s = view(0, 2, 2, T)
        mixT = view(4096, KD, T)
        mix_tmp = view(2048, 2, T)
        pq = view(0, 16, T)
        sc = view(8192, 16, P)
        cand = view(12288, HP, 256)
        onehot = view(14592, ENTRIES, TOPK)
        onehot2 = view(16640, ENTRIES, TOPK)
        topv = view(18688, 16, TOPK)
        topi = view(18944, 16, TOPK)
        best = view(19200, HP, TOPK)
        ent = view(19328, 3, P)
        bsum = view(19712, HP)
        topi_u = view(19728, 16, TOPK).bitcast(U32)
        bpos_u = view(19984, HP, TOPK).bitcast(U32)
        bi_u = view(20112, ENTRIES).bitcast(U32)
        bj_u = view(20240, ENTRIES).bitcast(U32)
        bi = view(20368, ENTRIES)
        bj = view(20496, ENTRIES)
        entT = sqbuf[:, 0:3 * T].rearrange("p (a b) -> p a b", a=3)
        oneA = sqbuf[:, 1536:1536 + 1024].rearrange("p (a b) -> p a b", a=8)
        oneB = sqbuf[:, 2560:2560 + 1024].rearrange("p (a b) -> p a b", a=8)
        stage = view(0, 2, 8192)
        uslot = [wring[:, 0:4096], wring[:, 4096:8192]]
        vslot = [wring[:, 8192:12288], area[:, 0:4096]]
        gslot = [view(4096, EG, T), view(6144, EG, T)]
        coef = [view(8192, EG, T), view(10240, EG, T)]

        wa2_sb = C("dist")[0:16, :]
        keys_sb = sb("keys_sb", [P, 2, P])

        consts_in = sem("consts_in")
        x_in = sem("x_in")
        p_in = sem("p_in")
        keys_in = sem("keys_in")
        w_in = [sem(f"w_in{i}") for i in range(NW)]
        filled = [sem(f"filled{i}") for i in range(NPAIR)]
        emptied = [sem(f"emptied{i}") for i in range(NPAIR)]
        squared = sem("squared")
        normed = sem("normed")
        dve_step = sem("dve_step")
        act_step = sem("act_step")
        lam_ready = sem("lam_ready")
        stats_ready = sem("stats_ready")
        exp_done = sem("exp_done")
        probs_ready = sem("probs_ready")
        mixin_ready = sem("mixin_ready")
        x1_ready = sem("x1_ready")
        x2_ready = sem("x2_ready")
        roped = sem("roped")
        neg_max = sem("neg_max")
        mprobs = sem("mprobs")
        zbias = sem("zbias")
        log_decay = sem("log_decay")
        cumulated = sem("cumulated")
        level_diff = sem("level_diff")
        level_exp = sem("level_exp")
        level_qk = sem("level_qk")
        kd_diff = sem("kd_diff")
        kd_exp = sem("kd_exp")
        kd_ready = sem("kd_ready")
        decays = sem("decays")
        qb_ready = sem("qb_ready")
        mixed = sem("mixed")
        gated = sem("gated")
        soft_diff = sem("soft_diff")
        soft_exp = sem("soft_exp")
        entries = sem("entries")
        hot = sem("hot")
        spread = sem("spread")
        copied = sem("copied")
        stored = [sem(f"stored{i}") for i in range(2)]
        u_in = [sem(f"u_in{i}") for i in range(2)]
        v_in = [sem(f"v_in{i}") for i in range(2)]
        g_in = [sem(f"g_in{i}") for i in range(2)]
        pre_done = sem("pre_done")
        gelu_done = sem("gelu_done")
        coef_done = sem("coef_done")
        out_done = sem("out_done")
        added = sem("added")
        out_stored = sem("out_stored")

        def pair(key):
            n = JOB[key] % NPAIR
            return ps[:, 2 * n:2 * n + 2, :]

        def flat(key):
            return pair(key).rearrange("p a b -> p (a b)")

        def when_filled(eng, key):
            eng.wait_ge(filled[JOB[key] % NPAIR], JOB[key] // NPAIR + 1)

        def when_emptied(eng, key):
            eng.wait_ge(emptied[JOB[key] % NPAIR], JOB[key] // NPAIR + 1)

        def fills(ins, key):
            ins.then_inc(filled[JOB[key] % NPAIR], 1)

        def empties(ins, key):
            ins.then_inc(emptied[JOB[key] % NPAIR], 1)

        def W(name):
            g = WN[name]
            _, k, n = WEIGHTS[g]
            at = (g % NW) * WSLOT
            return wring[:, at:at + k * n].rearrange("p (k n) -> p k n", k=k)

        def norm_sq(name):
            k = NORM[name]
            return sqbuf if NORMS[k][2] else small_sq[k % 2]

        block = ctx.enter_context(nc.Block())

        @block.sync
        def _(sp):
            sp.dma_start(cst[:, :], A["consts"]).then_inc(consts_in, 16)
            sp.dma_start(vec[:, :], A["vecs"]).then_inc(consts_in, 16)
            sp.dma_start(xs, A["xT"]).then_inc(x_in, 16)
            sp.dma_start(resid[:, :, T:TM], A["metaT"]).then_inc(x_in, 16)
            for g, (name, k, n) in enumerate(WEIGHTS):
                if g >= NW:
                    when_filled(sp, LAST[WEIGHTS[g - NW][0]])
                at = (g % NW) * WSLOT
                sp.dma_start(wring[:, at:at + k * n],
                             A["weights"][:, WAT[name]:WAT[name] + k * n]).then_inc(w_in[g % NW], 16)
                if g == NW:
                    sp.dma_start(pin, A["pT"]).then_inc(p_in, 16)
                    sp.dma_start(keys_sb[:, :, :], A["keysT"]).then_inc(keys_in, 16)
                if name == "pg1":
                    when_emptied(sp, ("S", len(UNITS_A) - 1))
                    sp.dma_start(wa2_sb, A["wa2"]).then_inc(keys_in, 16)
            when_filled(sp, ("pq", 7))

            def load_u(g, s):
                sp.dma_start(uslot[s], A["uT"][bass.ds(g, 1), :, :].rearrange("g p n -> p (g n)")).then_inc(u_in[s], 16)

            def load_gates(g, s):
                sp.dma_start(gslot[s], A["gates"][:, bass.ds(g, 1), :].rearrange("p g (j t) -> p (g j) t", j=EG)
                             ).then_inc(g_in[s], 16)

            def load_v(g, s):
                sp.dma_start(vslot[s], A["vT"][bass.ds(g, 1), :, :].rearrange("g p n -> p (g n)")).then_inc(v_in[s], 16)

            load_u(0, 0)
            load_u(1, 1)
            load_v(0, 0)
            for n in range(T // HALF):
                sp.wait_ge(copied, (n + 1) * (HALF // 4))
                sp.dma_start(A["gates"].rearrange("p g (j t) -> p (g j) t", j=EG)[:, :, n * HALF:(n + 1) * HALF],
                             stage[:, n % 2, :].rearrange("p (j t) -> p j t", t=HALF)).then_inc(stored[n % 2], 16)
            for i in range(2):
                sp.wait_ge(stored[i], 8 * (T // HALF))
            load_gates(0, 0)
            load_gates(1, 1)
            load_v(1, 1)
            with sp.Fori(0, GROUPS // 2 - 1) as it:
                for s in range(2):
                    sp.wait_ge(pre_done, 8 * it + EG * (s + 1))
                    load_u(2 * it + 2 + s, s)
                    sp.wait_ge(coef_done, 8 * it + EG * (s + 1))
                    load_gates(2 * it + 2 + s, s)
                    sp.wait_ge(out_done, 16 * it + KD * (s + 1))
                    load_v(2 * it + 2 + s, s)
            for k in range(KD):
                sp.wait_ge(added, KD * (GROUPS - 1) + k + 1)
                sp.dma_start(A["out"][k * P:(k + 1) * P, :], resid[:, k, 0:T]).then_inc(out_stored, 16)
            sp.wait_ge(out_stored, 16 * KD)

        @block.tensor
        def _(pe):
            def claim(key):
                if JOB[key] >= NPAIR:
                    n = JOB[key] - NPAIR
                    pe.wait_ge(emptied[n % NPAIR], n // NPAIR + 1)

            def arrived(name):
                g = WN[name]
                pe.wait_ge(w_in[g % NW], 16 * (g // NW + 1))

            def project(key, name, tiles, src, k_tiles, width=T, col0=0):
                claim(key)
                arrived(name)
                out = flat(key)
                w = W(name)
                for a, m in enumerate(tiles):
                    for k in range(k_tiles):
                        mm = pe.matmul(out[:, a * 512:a * 512 + T], w[:, k, col0 + m * P:col0 + (m + 1) * P],
                                       src[:, k, 0:T], start=(k == 0), stop=(k == k_tiles - 1))
                    if width == TM:
                        for k in range(k_tiles):
                            mm = pe.matmul(out[:, T:TM], w[:, k, col0 + m * P:col0 + (m + 1) * P],
                                           src[:, k, T:TM], start=(k == 0), stop=(k == k_tiles - 1))
                fills(mm, key)

            def tokens(key, name, tiles, src, k_tiles, col0, width):
                claim(key)
                arrived(name)
                out = flat(key)
                w = W(name)
                at = 0
                for t in tiles:
                    n = P if t < TT else META
                    for c in range(0, width, 512):
                        for k in range(k_tiles):
                            mm = pe.matmul(out[0:n, at:at + 512], src[:, k, t * P:t * P + n],
                                           w[:, k, col0 + c:col0 + c + 512], start=(k == 0), stop=(k == k_tiles - 1))
                        at += 512
                fills(mm, key)

            def sums(name, ones, groups, width=T):
                key = ("ss", name)
                claim(key)
                pe.wait_ge(squared, NORM[name] + 1)
                sq = norm_sq(name)
                out = flat(key)
                for a, starts in enumerate(groups):
                    for n, c in enumerate(starts):
                        mm = pe.matmul(out[:, a * 512:a * 512 + T], ones, sq[:, c:c + T],
                                       start=(n == 0), stop=(n == len(starts) - 1))
                    if width == TM:
                        for n, c in enumerate(starts):
                            mm = pe.matmul(out[:, T:TM], ones, sq[:, c + T:c + TM],
                                           start=(n == 0), stop=(n == len(starts) - 1))
                fills(mm, key)

            ident, ones, heads64 = C("ident"), C("ones"), C("heads64")

            pe.wait_ge(consts_in, 32)
            pe.wait_ge(lam_ready, 1)
            claim(("lam",))
            fills(pe.matmul(flat(("lam",))[:, 0:2], ones, small[:, 0:2], start=True, stop=True), ("lam",))
            sums("n1", ones, [[k * T for k in range(KD)]])
            pe.wait_ge(normed, NORM["n1"] + 1)
            for g in ("q", "k"):
                for m in (0, 1):
                    project((g, m), g, (2 * m, 2 * m + 1), hs, KD)
            for m in (0, 1):
                tokens(("v", m), "v", (2 * m, 2 * m + 1), hs, KD, 0, 512)

            def scores_a(u):
                h, i = UNITS_A[u]
                key = ("S", u)
                claim(key)
                if u == 0:
                    when_emptied(pe, ("k", 1))
                for m in range(2):
                    mm = pe.matmul(pair(key)[:, m, 0:(i + 1) * P], qT[64 * m:64 * m + 64, h, i * P:(i + 1) * P],
                                   kT[64 * m:64 * m + 64, h, 0:(i + 1) * P], start=True, stop=True)
                fills(mm, key)

            side = [(g, m) for g in ("c", "u", "zc", "b", "za") for m in (0, 1)]
            scores_a(0)
            for u, (h, i) in enumerate(UNITS_A):
                if u + 1 < len(UNITS_A):
                    scores_a(u + 1)
                if side:
                    g, m = side.pop(0)
                    project((g, m), g, (2 * m, 2 * m + 1), hs, KD)
                claim(("T", u))
                pe.wait_ge(probs_ready, u + 1)
                for b in range(i + 1):
                    mm = pe.transpose(flat(("T", u))[:, b * P:(b + 1) * P], weights_p[:, u % 2, b * P:(b + 1) * P], ident)
                fills(mm, ("T", u))
                claim(("O", u))
                when_emptied(pe, ("T", u))
                for b in range(i + 1):
                    mm = pe.matmul(flat(("O", u))[:, 0:P], v_tok[:, b, h * P:(h + 1) * P],
                                   pT_sb[:, u % 2, b * P:(b + 1) * P], start=(b == 0), stop=(b == i))
                fills(mm, ("O", u))
            for n in range(2):
                sums(f"sl{n}", ones, [[0], [T]])
            pe.wait_ge(mixin_ready, 2)
            for m in range(4):
                project(("wo", m), f"wo{m // 2}", (2 * (m % 2), 2 * (m % 2) + 1), mixin, KD)
            pe.wait_ge(p_in, 16)
            for m in range(4):
                project(("ple", m), "ple", (2 * m, 2 * m + 1), pin, 2)
            sums("post", ones, [[k * T for k in range(KD)]])
            sums("ple", ones, [[k * T for k in range(KD)]])
            pe.wait_ge(x1_ready, 1)
            for m in range(4):
                project(("pg", m), f"pg{m // 2}", (2 * (m % 2), 2 * (m % 2) + 1), xs, KD)

            sums("mix", ones, [[k * TM for k in range(KD)]], TM)
            pe.wait_ge(normed, NORM["mix"] + 1)
            project(("cq", 0), "cq", (0, 1), hs, KD)
            project(("cq", 1), "cq", (2,), hs, KD)
            project(("ckv", 0), "ckv", (0,), normed_x, KD, TM)
            project(("ckv", 1), "ckv", (1,), normed_x, KD, TM)
            project(("kpe", 0), "ckv", (2,), normed_x, KD, TM)
            sums("cq", ones, [[0, T, 2 * T]])
            sums("ckv", ones, [[0, TM]], TM)
            sums("kpe", heads64, [[0]], TM)
            claim(("rot", "kpe"))
            pe.wait_ge(normed, NORM["kpe"] + 1)
            pe.matmul(flat(("rot", "kpe"))[:, 0:T], C("rot"), kp[:, 0:T], start=True, stop=True)
            fills(pe.matmul(flat(("rot", "kpe"))[:, T:TM], C("rot"), kp[:, T:TM], start=True, stop=True), ("rot", "kpe"))
            def project_part(name):
                kind, m = name[0:2], int(name[2:])
                if kind == "qn":
                    if m == 0:
                        pe.wait_ge(normed, NORM["cq"] + 1)
                    project(("uqn", m), "uqn", (2 * m, 2 * m + 1), cq, 3)
                elif kind == "qp":
                    project(("uqp", m), "uqp", (2 * m, 2 * m + 1), cq, 3)
                else:
                    if m == 0:
                        pe.wait_ge(normed, NORM["ckv"] + 1)
                    project(("kn", m), "ukv", (m,), ckv, 2, TM)

            def sum_part(name):
                kind = name[0:2]
                if kind == "qn":
                    sums(name, ones, [[0], [T]])
                elif kind == "qp":
                    sums(name, heads64, [[0], [T]])
                else:
                    sums(name, ones, [[0]], TM)

            for n, name in enumerate(PARTS):
                project_part(name)
                if n >= 1:
                    sum_part(PARTS[n - 1])
                if n >= 3 and PARTS[n - 3][0:2] == "qp":
                    m = int(PARTS[n - 3][2:])
                    claim(("rot", m))
                    pe.wait_ge(normed, NORM[f"qp{m}"] + 1)
                    for a in range(2):
                        mm = pe.matmul(pair(("rot", m))[:, a, :], C("rot"), qp[:, 2 * m + a, :], start=True, stop=True)
                    fills(mm, ("rot", m))
            sum_part(PARTS[-1])
            for t in range(TT + 1):
                tokens(("mv", t), "ukv", (t,), ckv, 2, 1024, 1024)

            def scores_m(u):
                h, i = UNITS_M[u]
                key = ("MS", u)
                claim(key)
                if u == 0:
                    pe.wait_ge(normed, NORM["kn7"] + 1)
                    pe.wait_ge(roped, 3)
                nk = (i + 1) * P
                r = 64 * (h % 2)
                out = flat(key)
                for at, a, n in ((0, 0, nk), (nk, T, META)):
                    pe.matmul(out[:, at:at + n], qn[:, h, i * P:(i + 1) * P], kn[:, h, a:a + n], start=True, stop=False)
                    mm = pe.matmul(out[:, at:at + n], qp[r:r + 64, h // 2, i * P:(i + 1) * P], kp[r:r + 64, a:a + n],
                                   start=False, stop=True)
                fills(mm, key)

            scores_m(0)
            for u, (h, i) in enumerate(UNITS_M):
                if u + 1 < len(UNITS_M):
                    scores_m(u + 1)
                nk = (i + 1) * P
                claim(("MT", u))
                pe.wait_ge(mprobs, u + 1)
                for b in range(i + 1):
                    pe.transpose(flat(("MT", u))[:, b * P:(b + 1) * P], mp[:, u % 2, b * P:(b + 1) * P], ident)
                fills(pe.transpose(flat(("MT", u))[0:META, 512:640], mp[:, u % 2, nk:nk + META], ident), ("MT", u))
                claim(("MO", u))
                when_emptied(pe, ("MT", u))
                for b in range(i + 1):
                    pe.matmul(flat(("MO", u))[:, 0:P], mv[:, b, h * P:(h + 1) * P], mpt[:, u % 2, b * P:(b + 1) * P],
                              start=(b == 0), stop=False)
                fills(pe.matmul(flat(("MO", u))[:, 0:P], mvm[0:META, h * P:(h + 1) * P], mpt[0:META, u % 2, 512:640],
                                start=False, stop=True), ("MO", u))

            for m in range(2):
                project(("gq", m), "gq", (2 * m, 2 * m + 1), hs, KD)
            for h in range(HG):
                project(("gk", h), "gk", (h,), normed_x, KD, TM)
            claim(("ga", 0))
            arrived("ga")
            for a, n in ((0, T), (T, META)):
                for k in range(KD):
                    mm = pe.matmul(flat(("ga", 0))[0:16, a:a + n], W("ga")[:, k, :], normed_x[:, k, a:a + n],
                                   start=(k == 0), stop=(k == KD - 1))
            fills(mm, ("ga", 0))
            for g in (0, 1):
                for m in (0, 1):
                    tokens(("gv", g, m), f"gv{g}", (2 * m, 2 * m + 1), normed_x, KD, 0, 512)
                tokens(("gv", g, 2), f"gv{g}", (TT,), normed_x, KD, 0, 512)
            pe.wait_ge(keys_in, 32)
            when_emptied(pe, ("gv", 1, 2))
            for h in range(HG):
                claim(("z", h))
                if h == 0:
                    when_emptied(pe, ("ga", 0))
                for a, n in ((0, T), (T, META)):
                    mm = pe.matmul(flat(("z", h))[:, a:a + n], wa2_sb[:, h * P:(h + 1) * P], gaT[0:16, a:a + n],
                                   start=True, stop=True)
                fills(mm, ("z", h))
                for n in range(8):
                    key = ("lev", h, n)
                    claim(key)
                    if n:
                        pe.wait_ge(level_qk, 7 * h + n)
                    for c in range(TT):
                        lhs = gk[:, h, c * P:(c + 1) * P] if n == 0 else kl[:, c * P:(c + 1) * P]
                        rhs = gq[:, h, c * P:(c + 1) * P] if n == 0 else ql[:, c * P:(c + 1) * P]
                        mm = pe.matmul(flat(key)[:, c * P:(c + 1) * P], lhs, rhs, start=True, stop=True)
                    fills(mm, key)
                claim(("kd", h))
                pe.wait_ge(kd_ready, h + 1)
                for c in range(TT):
                    pe.transpose(flat(("kd", h))[:, c * P:(c + 1) * P], kl[:, c * P:(c + 1) * P], ident)
                fills(pe.transpose(flat(("kd", h))[0:META, 512:640], kl[:, T:TM], ident), ("kd", h))
                when_emptied(pe, ("kd", h))
                for c in range(TT):
                    key = ("st", h, c)
                    claim(key)
                    if c == 0:
                        mm = pe.matmul(flat(key)[:, 0:HV], kdt[0:META, TT, :], gvm[0:META, h * HV:(h + 1) * HV],
                                       start=True, stop=True)
                    else:
                        mm = pe.matmul(flat(key)[:, 0:HV], kdt[:, c - 1, :], gv[:, c - 1, h * HV:(h + 1) * HV],
                                       start=True, stop=True)
                    fills(mm, key)
                key = ("go", h)
                claim(key)
                when_emptied(pe, ("lev", h, 7))
                pe.wait_ge(qb_ready, h + 1)
                when_emptied(pe, ("st", h, TT - 1))
                for e in range(2):
                    for c in range(TT):
                        pe.matmul(pair(key)[:, e, c * P:(c + 1) * P], gv[:, c, h * HV + e * P:h * HV + (e + 1) * P],
                                  attT[:, c * P:(c + 1) * P], start=True, stop=False)
                        mm = pe.matmul(pair(key)[:, e, c * P:(c + 1) * P], state[:, c, e * P:(e + 1) * P],
                                       qb[:, c * P:(c + 1) * P], start=False, stop=True)
                fills(mm, key)
            for h in range(HG):
                sums(f"g{h}", ones, [[0, T]])
            for h in range(HG):
                project(("gg", h), f"gg{h // 2}", (2 * (h % 2), 2 * (h % 2) + 1), hs, KD)
            for s, src in (("a", ya), ("b", oT)):
                for m in range(4):
                    tiles = (2 * (m % 2), 2 * (m % 2) + 1)
                    project(("t" + s, m), f"t{s}{m // 2}", tiles, hs, KD)
                    if s == "b" and m == 0:
                        pe.wait_ge(gated, HG)
                    project(("o" + s, m), f"o{s}{m // 2}", tiles, src, KD)
            pe.wait_ge(mixed, 4)
            for m in range(4):
                project(("w2", m), f"w2{m // 2}", (2 * (m % 2), 2 * (m % 2) + 1), mixT, KD)

            sums("ffn", ones, [[k * T for k in range(KD)]])
            pe.wait_ge(normed, NORM["ffn"] + 1)
            for m in range(8):
                project(("pq", m), f"pq{m // 2}", (2 * (m % 2), 2 * (m % 2) + 1), hs, KD)
            when_emptied(pe, ("pq", 7))
            when_emptied(pe, ("pq", 6))
            for t in range(TT):
                for half in range(2):
                    key = ("ps", t, half)
                    claim(key)
                    for j in range(8):
                        f = 8 * half + j
                        mm = pe.matmul(flat(key)[:, j * P:(j + 1) * P], pq[:, f, t * P:(t + 1) * P],
                                       keys_sb[:, f % 2, :], start=True, stop=True)
                    fills(mm, key)
                key = ("tr", t)
                claim(key)
                pe.wait_ge(entries, t + 1)
                for j in range(3):
                    mm = pe.transpose(flat(key)[:, j * P:(j + 1) * P], ent[:, j, :], ident)
                fills(mm, key)

            for key in (("ps", TT - 1, 0), ("ps", TT - 1, 1), ("tr", TT - 1), ("tr", TT - 2)):
                when_emptied(pe, key)

            def spread_tokens(step):
                for half in range(2):
                    pe.wait_ge(hot, 2 * step + half + 1)
                    at_least(pe, copied, 2 * step + half - 1)
                    for j in range(4):
                        mm = pe.matmul(ps[:, half, j * P:(j + 1) * P], oneA[:, 4 * half + j, :],
                                       oneB[:, 4 * half + j, :], start=True, stop=True)
                    mm.then_inc(spread, 1)

            spread_tokens(0)
            with pe.Fori(1, T // 8) as step:
                spread_tokens(step)
            pe.wait_ge(copied, 2 * (T // 8))

            def pre(g, s, turn):
                pe.wait_ge(u_in[s], 16 * turn)
                u = uslot[s].rearrange("p (k n) -> p k n", k=KD)
                for j in range(EG):
                    at_least(pe, gelu_done, EG * g - EG + j + 1)
                    for k in range(KD):
                        mm = pe.matmul(ps[:, j, :], u[:, k, j * P:(j + 1) * P], hs[:, k, :],
                                       start=(k == 0), stop=(k == KD - 1))
                    mm.then_inc(pre_done, 1)

            def combine(g, s, turn):
                pe.wait_ge(v_in[s], 16 * turn)
                pe.wait_ge(coef_done, EG * g + EG)
                v = vslot[s].rearrange("p (j d) -> p j d", j=EG)
                for m in range(KD):
                    at_least(pe, added, KD * g + m - 3)
                    for j in range(EG):
                        mm = pe.matmul(ps[:, 4 + m % 4, :], v[:, j, m * P:(m + 1) * P], coef[s][:, j, :],
                                       start=(j == 0), stop=(j == EG - 1))
                    mm.then_inc(out_done, 1)

            def two_groups(it, last=False):
                pre(2 * it + 1, 1, it + 1)
                combine(2 * it, 0, it + 1)
                if not last:
                    pre(2 * it + 2, 0, it + 2)
                combine(2 * it + 1, 1, it + 1)

            pre(0, 0, 1)
            two_groups(0)
            with pe.Fori(1, GROUPS // 2 - 1) as it:
                two_groups(it)
            two_groups(GROUPS // 2 - 1, last=True)

        @block.scalar
        def _(act):
            steps = [0]

            def link(ins):
                steps[0] += 1
                ins.then_inc(act_step, 1)
                act.wait_ge(act_step, steps[0])

            def copy_out(key, dst, src, func=ACT.Copy, scale=1.0):
                when_filled(act, key)
                empties(act.activation(dst, src, func, scale=scale), key)

            def square(name, dst, src):
                k = NORM[name]
                back = 1 if (NORMS[k][2] or NORMS[k - 1][2]) else 2
                if k >= back:
                    when_filled(act, ("ss", NORMS[k - back][0]))
                act.activation(dst, src, ACT.Square).then_inc(squared, 1)

            def root(name, width, eps="eps"):
                k = NORM[name]
                if k >= 2:
                    act.wait_ge(normed, k - 1)
                when_filled(act, ("ss", name))
                empties(act.activation(rt[:, k % 2, 0:width], flat(("ss", name))[:, 0:width], ACT.Sqrt,
                                       bias=V(eps), scale=1.0 / NORMS[k][1]), ("ss", name))

            sq_x = sqbuf[:, 0:KD * T].rearrange("p (k t) -> p k t", k=KD)

            act.wait_ge(x_in, 32)
            act.wait_ge(consts_in, 32)
            square("n1", sq_x, xs)
            copy_out(("lam",), small[:, 2:4], flat(("lam",))[:, 0:2], ACT.Exp)
            root("n1", T)
            for m in range(2):
                copy_out(("q", m), qT[:, 2 * m:2 * m + 2, :], pair(("q", m)))
            for m in range(2):
                copy_out(("k", m), kT[:, 2 * m:2 * m + 2, :], pair(("k", m)))
            for m in range(2):
                copy_out(("v", m), v_tok[:, 2 * m:2 * m + 2, :], pair(("v", m)))

            def exps_a(u):
                h, i = UNITS_A[u]
                nk = (i + 1) * P
                st = small[:, 16 + 16 * (u % 2):32 + 16 * (u % 2)]
                act.wait_ge(stats_ready, u + 1)
                for m in range(2):
                    e = act.activation(probs[:, u % 2, m, 0:nk], probs[:, u % 2, m, 0:nk], ACT.Exp,
                                       bias=st[:, 2 + m:3 + m], scale=SCALE_A, accum_out=st[:, 4 + m:5 + m])
                e.then_inc(exp_done, 1)

            side = [(g, m) for g in ("c", "u", "zc", "b", "za") for m in (0, 1)]
            exps_a(0)
            for u, (h, i) in enumerate(UNITS_A):
                if u + 1 < len(UNITS_A):
                    exps_a(u + 1)
                if side:
                    g, m = side.pop(0)
                    if g == "c":
                        copy_out((g, m), cT[:, 2 * m:2 * m + 2, :], pair((g, m)))
                    if g == "zc":
                        copy_out((g, m), szT[:, 2 * m:2 * m + 2, :], pair((g, m)), ACT.Silu)
                    if g == "za":
                        copy_out((g, m), zaT[:, 2 * m:2 * m + 2, :], pair((g, m)), ACT.Silu)
                nk = (i + 1) * P
                if u >= 2:
                    when_filled(act, ("O", u - 2))
                copy_out(("T", u), pT_sb[:, u % 2, 0:nk], flat(("T", u))[:, 0:nk])
                copy_out(("O", u), mixin[:, h, i * P:(i + 1) * P], flat(("O", u))[:, 0:P])
            when_emptied(act, ("O", len(UNITS_A) - 1))
            for n in range(2):
                square(f"sl{n}", small_sq[NORM[f"sl{n}"] % 2][:, 0:1024].rearrange("p (a b) -> p a b", a=2),
                       mixin[:, 2 * n:2 * n + 2, :])
            for n in range(2):
                root(f"sl{n}", 1024, "subeps")
            for m in range(4):
                copy_out(("wo", m), mixedT[:, 2 * m:2 * m + 2, :], pair(("wo", m)))
            when_emptied(act, ("wo", 3))
            square("post", sq_x, mixedT)
            for m in range(4):
                copy_out(("ple", m), eT[:, 2 * m:2 * m + 2, :], pair(("ple", m)))
            root("post", T)
            when_emptied(act, ("ple", 3))
            square("ple", sq_x, eT)
            root("ple", T)
            for m in range(4):
                copy_out(("pg", m), sgT[:, 2 * m:2 * m + 2, :], pair(("pg", m)), ACT.Sigmoid)

            act.wait_ge(x2_ready, 1)
            square("mix", sqbuf[:, :].rearrange("p (k t) -> p k t", k=KD), resid[:, :, :])
            root("mix", TM)
            copy_out(("cq", 0), cq[:, 0:2, :], pair(("cq", 0)))
            copy_out(("cq", 1), cq[:, 2, :], flat(("cq", 1))[:, 0:T])
            when_emptied(act, ("cq", 1))
            square("cq", sqbuf[:, 0:3 * T].rearrange("p (k t) -> p k t", k=3), cq)
            for k in range(2):
                copy_out(("ckv", k), ckv[:, k, :], flat(("ckv", k))[:, 0:TM])
            copy_out(("kpe", 0), kp, flat(("kpe", 0))[:, 0:TM])
            root("cq", T)
            when_emptied(act, ("kpe", 0))
            square("ckv", norm_sq("ckv")[:, 0:2 * TM].rearrange("p (k t) -> p k t", k=2), ckv)
            square("kpe", norm_sq("kpe")[:, 0:TM], kp)
            root("ckv", TM)
            root("kpe", TM)

            def raw_part(name):
                kind, m = name[0:2], int(name[2:])
                sq = norm_sq(name)
                if kind == "kn":
                    key = ("kn", m)
                    copy_out(key, kn[:, m, :], flat(key)[:, 0:TM])
                    when_emptied(act, key)
                    square(name, sq[:, 0:TM], kn[:, m, :])
                else:
                    key, dst = (("uqn", m), qn) if kind == "qn" else (("uqp", m), qp)
                    copy_out(key, dst[:, 2 * m:2 * m + 2, :], pair(key))
                    when_emptied(act, key)
                    square(name, sq[:, 0:1024].rearrange("p (a b) -> p a b", a=2), dst[:, 2 * m:2 * m + 2, :])

            for n, name in enumerate(PARTS):
                raw_part(name)
                if n >= 1:
                    root(PARTS[n - 1], TM if PARTS[n - 1][0:2] == "kn" else 1024)
            root(PARTS[-1], TM)
            for t in range(TT + 1):
                if t < TT:
                    copy_out(("mv", t), mv[:, t, :], flat(("mv", t)))
                else:
                    copy_out(("mv", t), mvm[0:META, :], flat(("mv", t))[0:META, :])

            def exps_m(u):
                h, i = UNITS_M[u]
                n = (i + 1) * P + META
                st = small[:, 64 + 8 * (u % 2):72 + 8 * (u % 2)]
                act.wait_ge(neg_max, u + 1)
                if u >= 2:
                    when_filled(act, ("MT", u - 2))
                empties(act.activation(mp[:, u % 2, 0:n], flat(("MS", u))[:, 0:n], ACT.Exp, bias=st[:, 1:2],
                                       scale=SCALE_M, accum_out=st[:, 2:3]), ("MS", u))

            exps_m(0)
            for u, (h, i) in enumerate(UNITS_M):
                if u + 1 < len(UNITS_M):
                    exps_m(u + 1)
                nk = (i + 1) * P
                key = ("MT", u)
                when_filled(act, key)
                if u >= 2:
                    when_filled(act, ("MO", u - 2))
                act.activation(mpt[0:META, u % 2, 512:640], flat(key)[0:META, 512:640], ACT.Copy)
                empties(act.activation(mpt[:, u % 2, 0:nk], flat(key)[:, 0:nk], ACT.Copy), key)
                copy_out(("MO", u), ya[:, h, i * P:(i + 1) * P], flat(("MO", u))[:, 0:P])

            for m in range(2):
                copy_out(("gq", m), gq[:, 2 * m:2 * m + 2, :], pair(("gq", m)), scale=HK ** -0.5)
            for h in range(HG):
                copy_out(("gk", h), gk[:, h, :], flat(("gk", h))[:, 0:TM])
            copy_out(("ga", 0), gaT[0:16, :], flat(("ga", 0))[0:16, 0:TM])
            for g in (0, 1):
                for m in (0, 1):
                    copy_out(("gv", g, m), gv[:, 2 * m:2 * m + 2, 512 * g:512 * g + 512], pair(("gv", g, m)))
                copy_out(("gv", g, 2), gvm[0:META, 512 * g:512 * g + 512], flat(("gv", g, 2))[0:META, 0:512])
            for h in range(HG):
                key = ("z", h)
                when_filled(act, key)
                if h:
                    act.wait_ge(kd_ready, h)
                act.activation(la, flat(key)[:, 0:TM], ACT.Identity, bias=V("ba", h))
                empties(act.activation(bc, flat(key)[:, 0:TM], ACT.Abs, bias=V("ba", h)), key)
                when_emptied(act, key)
                link(act.activation(bc, bc, ACT.Exp, scale=-1.0))
                act.activation(bc, bc, ACT.Ln, bias=C("ones", 0, 1)).then_inc(zbias, 1)
                act.wait_ge(cumulated, h + 1)
                if h:
                    when_filled(act, ("go", h - 1))
                act.activation(qb, bc[:, 0:T], ACT.Exp, scale=1 / TAU)
                act.activation(dec[:, 0:TT], bc[:, 0:T].rearrange("p (c t) -> p c t", t=P)[:, :, P - 1], ACT.Exp,
                               scale=1 / TAU).then_inc(decays, 1)
                for n, s in enumerate(LEVELS):
                    act.wait_ge(level_diff, 7 * h + n + 1)
                    w = wl[:, 0:T].rearrange("p (b x s) -> p b x s", x=2, s=s)
                    act.activation(w[:, :, 0, :], w[:, :, 0, :], ACT.Exp, scale=-1 / TAU)
                    act.activation(w[:, :, 1, :], w[:, :, 1, :], ACT.Exp, scale=1 / TAU).then_inc(level_exp, 1)
                act.wait_ge(kd_diff, h + 1)
                act.activation(kl, kl, ACT.Exp, scale=1 / TAU).then_inc(kd_exp, 1)
                key = ("kd", h)
                when_filled(act, key)
                if h:
                    when_filled(act, ("st", h - 1, TT - 1))
                act.activation(kdt[0:META, TT, :], flat(key)[0:META, 512:640], ACT.Copy)
                empties(act.activation(kdt[:, 0:TT, :].rearrange("p a b -> p (a b)"), flat(key)[:, 0:T], ACT.Copy), key)
                copy_out(("go", h), oT[:, 2 * h:2 * h + 2, :], pair(("go", h)))
            when_emptied(act, ("go", HG - 1))
            for h in range(HG):
                square(f"g{h}", norm_sq(f"g{h}")[:, 0:1024].rearrange("p (a b) -> p a b", a=2),
                       oT[:, 2 * h:2 * h + 2, :])
                if h >= 1:
                    root(f"g{h - 1}", T)
            root(f"g{HG - 1}", T)

            def gate(key, func, k, before):
                when_filled(act, key)
                if before is not None:
                    before()
                empties(act.activation(gate_s[:, k % 2, :, :], pair(key), func), key)

            for h in range(HG):
                gate(("gg", h), ACT.Silu, h, (lambda: act.wait_ge(gated, h - 1)) if h >= 2 else None)
            for m in range(4):
                gate(("ta", m), ACT.Sigmoid, m,
                     (lambda: act.wait_ge(gated, HG)) if m < 2 else (lambda: when_emptied(act, ("oa", m - 2))))
            for m in range(4):
                gate(("tb", m), ACT.Sigmoid, m,
                     lambda: when_emptied(act, ("oa", m + 2) if m < 2 else ("ob", m - 2)))

            when_emptied(act, ("w2", 3))
            square("ffn", sq_x, xs)
            root("ffn", T)
            for m in range(8):
                copy_out(("pq", m), pq[:, 2 * m:2 * m + 2, :], pair(("pq", m)))
            for t in range(TT):
                if t:
                    act.wait_ge(entries, t)
                for half in range(2):
                    key = ("ps", t, half)
                    copy_out(key, sc[:, 8 * half:8 * half + 8, :].rearrange("p a b -> p (a b)"), flat(key))
                act.wait_ge(soft_diff, t + 1)
                act.activation(ent[:, 2, :], ent[:, 2, :], ACT.Exp).then_inc(soft_exp, 1)
                copy_out(("tr", t), entT[:, :, t * P:(t + 1) * P],
                         flat(("tr", t))[:, 0:3 * P].rearrange("p (a b) -> p a b", a=3))

            def copy_tokens(n, i):
                dst = stage[:, n % 2, :].rearrange("p (j t) -> p t j", t=HALF)
                for half in range(2):
                    act.wait_ge(spread, 2 * (8 * n + i) + half + 1)
                    act.activation(dst[:, bass.ds(8 * i + 4 * half, 4), :],
                                   ps[:, half, :].rearrange("p (t j) -> p t j", t=4), ACT.Copy).then_inc(copied, 1)

            for n in range(T // HALF):
                if n >= 2:
                    act.wait_ge(stored[n % 2], 16 * (n // 2))
                with act.Fori(0, HALF // 8) as i:
                    copy_tokens(n, i)
            for i in range(2):
                act.wait_ge(stored[i], 8 * (T // HALF))

            def gelus(g, s):
                at_least(act, out_done, KD * g - KD)
                for j in range(EG):
                    act.wait_ge(pre_done, EG * g + j + 1)
                    act.activation(coef[s][:, j, :], ps[:, j, :], ACT.Gelu).then_inc(gelu_done, 1)

            gelus(0, 0)
            gelus(1, 1)
            with act.Fori(1, GROUPS // 2) as it:
                gelus(2 * it, 0)
                gelus(2 * it + 1, 1)

        @block.vector
        def _(dve):
            steps = [0]

            def link(ins):
                steps[0] += 1
                ins.then_inc(dve_step, 1)
                dve.wait_ge(dve_step, steps[0])

            def inverse(name, width):
                when_emptied(dve, ("ss", name))
                r = rt[:, NORM[name] % 2, 0:width]
                link(dve.reciprocal(r, r))
                return r

            def scale_by(dst, src, gain, r, last=None):
                ins = dve.scalar_tensor_tensor(dst, src, gain, r, ALU.mult, ALU.mult)
                if last:
                    ins.then_inc(normed, 1)

            def big_norm(name, gain, dst, src, width=T):
                r = inverse(name, width)
                for k in range(KD):
                    scale_by(dst[:, k, 0:width], src[:, k, 0:width], V(gain, k), r, k == KD - 1)
                dve.wait_ge(normed, NORM[name] + 1)

            dve.wait_ge(consts_in, 32)
            dve.tensor_tensor(small[:, 0:2], vec[:, VEC["lam"][0]:VEC["lam"][0] + 2],
                              vec[:, VEC["lam"][0] + 2:VEC["lam"][0] + 4], ALU.mult).then_inc(lam_ready, 1)
            dve.memset(gT[:, :, 0:2], 0.0)
            when_emptied(dve, ("lam",))
            link(dve.scalar_tensor_tensor(small[:, 4:5], small[:, 3:4], -LAMBDA_INIT, small[:, 2:3],
                                          ALU.add, ALU.subtract))
            dve.wait_ge(x_in, 32)
            big_norm("n1", "pre", normed_x, resid)

            def stats_a(u):
                h, i = UNITS_A[u]
                nk = (i + 1) * P
                st = small[:, 16 + 16 * (u % 2):32 + 16 * (u % 2)]
                key = ("S", u)
                when_filled(dve, key)
                for m in range(2):
                    ins = dve.scalar_tensor_tensor(probs[:, u % 2, m, 0:nk], C("dist", T - nk, T), -SLOPES[h] / SCALE_A,
                                                   pair(key)[:, m, 0:nk], ALU.mult, ALU.add)
                empties(ins, key)
                when_emptied(dve, key)
                link(dve.tensor_reduce(st[:, 0:2], probs[:, u % 2, :, 0:nk], AX_X, ALU.max))
                dve.tensor_scalar(st[:, 2:4], st[:, 0:2], -SCALE_A, None, ALU.mult).then_inc(stats_ready, 1)

            def combine_a(u):
                h, i = UNITS_A[u]
                nk = (i + 1) * P
                st = small[:, 16 + 16 * (u % 2):32 + 16 * (u % 2)]
                dve.wait_ge(exp_done, u + 1)
                if u >= 2:
                    when_filled(dve, ("T", u - 2))
                link(dve.reciprocal(st[:, 6:8], st[:, 4:6]))
                link(dve.tensor_scalar(weights_p[:, u % 2, 0:nk], probs[:, u % 2, 1, 0:nk], st[:, 7:8], small[:, 4:5],
                                       ALU.mult, ALU.mult))
                dve.scalar_tensor_tensor(weights_p[:, u % 2, 0:nk], probs[:, u % 2, 0, 0:nk], st[:, 6:7],
                                         weights_p[:, u % 2, 0:nk], ALU.mult, ALU.add).then_inc(probs_ready, 1)

            def conv_part(m):
                for a in (2 * m, 2 * m + 1):
                    dst = mixin[:, 4 + a, :]
                    link(dve.tensor_scalar(dst, gT[:, a, 0:T], V("conv", a), None, ALU.mult))
                    link(dve.scalar_tensor_tensor(dst, gT[:, a, 1:T + 1], V("conv", 4 + a), dst, ALU.mult, ALU.add))
                    link(dve.scalar_tensor_tensor(dst, gT[:, a, 2:T + 2], V("conv", 8 + a), dst, ALU.mult, ALU.add))

            side = [(g, m) for g in ("c", "u", "zc", "b", "za") for m in (0, 1)]
            stats_a(0)
            for u in range(len(UNITS_A)):
                if u + 1 < len(UNITS_A):
                    stats_a(u + 1)
                combine_a(u)
                if side:
                    g, m = side.pop(0)
                    if g == "u":
                        when_filled(dve, (g, m))
                        when_emptied(dve, ("c", m))
                        empties(dve.tensor_tensor(gT[:, 2 * m:2 * m + 2, 2:T + 2], cT[:, 2 * m:2 * m + 2, :],
                                                  pair((g, m)), ALU.mult), (g, m))
                    if g == "zc":
                        when_emptied(dve, ("u", m))
                        conv_part(m)
                    if g == "b":
                        when_filled(dve, (g, m))
                        when_emptied(dve, ("zc", m))
                        sz = szT[:, 2 * m:2 * m + 2, :]
                        empties(dve.tensor_tensor(sz, sz, pair((g, m)), ALU.mult), (g, m))
                        when_emptied(dve, (g, m))
                        mx = mixin[:, 4 + 2 * m:6 + 2 * m, :]
                        dve.tensor_tensor(mx, mx, sz, ALU.mult)
            for n in range(2):
                r = inverse(f"sl{n}", 1024).rearrange("p (a b) -> p a b", a=2)
                mx = mixin[:, 2 * n:2 * n + 2, :]
                scale_by(mx, mx, V("subln"), r, True)
                dve.wait_ge(normed, NORM[f"sl{n}"] + 1)
                when_emptied(dve, ("za", n))
                dve.scalar_tensor_tensor(mx, mx, 1.0 - LAMBDA_INIT, zaT[:, 2 * n:2 * n + 2, :],
                                         ALU.mult, ALU.mult).then_inc(mixin_ready, 1)
            big_norm("post", "post", mixedT, mixedT)
            dve.tensor_tensor(xs, xs, mixedT, ALU.add).then_inc(x1_ready, 1)
            big_norm("ple", "ple", eT, eT)
            dve.wait_ge(x1_ready, 1)
            for m in range(4):
                when_emptied(dve, ("pg", m))
                sg = sgT[:, 2 * m:2 * m + 2, :]
                link(dve.tensor_tensor(sg, sg, eT[:, 2 * m:2 * m + 2, :], ALU.mult))
                when_filled(dve, ("pg", 3))
                x = resid[:, 2 * m:2 * m + 2, 0:T]
                ins = dve.tensor_tensor(x, x, sg, ALU.add)
            ins.then_inc(x2_ready, 1)

            dve.wait_ge(x2_ready, 1)
            big_norm("mix", "mix", normed_x, resid, TM)
            r = inverse("cq", T)
            for k in range(3):
                scale_by(cq[:, k, :], cq[:, k, :], V("qnorm", k), r, k == 2)
            r = inverse("ckv", TM)
            for k in range(2):
                scale_by(ckv[:, k, :], ckv[:, k, :], V("kvnorm", k), r, k == 1)
            scale_by(kp, kp, V("kp"), inverse("kpe", TM), True)

            def rope(key, dst, turned, cos, sin, tmp):
                when_filled(dve, key)
                empties(dve.tensor_tensor(tmp, turned, sin, ALU.mult), key)
                link(dve.tensor_tensor(dst, dst, cos, ALU.mult))
                when_emptied(dve, key)
                dve.tensor_tensor(dst, dst, tmp, ALU.add).then_inc(roped, 1)

            rope(("rot", "kpe"), kp, flat(("rot", "kpe"))[:, 0:TM], C("cos"), C("sin"), rot_tmp[:, 0:TM])
            for n, name in enumerate(PARTS):
                kind, m = name[0:2], int(name[2:])
                if kind == "kn":
                    scale_by(kn[:, m, :], kn[:, m, :], V("kn"), inverse(name, TM), True)
                else:
                    dst = (qn if kind == "qn" else qp)[:, 2 * m:2 * m + 2, :]
                    scale_by(dst, dst, V(kind), inverse(name, 1024).rearrange("p (a b) -> p a b", a=2), True)
                if n >= 2 and PARTS[n - 2][0:2] == "qp":
                    b = int(PARTS[n - 2][2:])
                    rope(("rot", b), qp[:, 2 * b:2 * b + 2, :], pair(("rot", b)),
                         C("cos", 0, T).unsqueeze(1).to_broadcast([P, 2, T]),
                         C("sin", 0, T).unsqueeze(1).to_broadcast([P, 2, T]),
                         rot_tmp[:, 0:1024].rearrange("p (a b) -> p a b", a=2))

            def stats_m(u):
                h, i = UNITS_M[u]
                nk = (i + 1) * P
                st = small[:, 64 + 8 * (u % 2):72 + 8 * (u % 2)]
                key = ("MS", u)
                when_filled(dve, key)
                link(dve.memset(flat(key)[0:CHUNK, nk - CHUNK:nk], NEG))
                link(dve.tensor_reduce(st[:, 0:1], flat(key)[:, 0:nk + META], AX_X, ALU.max))
                dve.tensor_scalar(st[:, 1:2], st[:, 0:1], -SCALE_M, None, ALU.mult).then_inc(neg_max, 1)

            stats_m(0)
            for u, (h, i) in enumerate(UNITS_M):
                if u + 1 < len(UNITS_M):
                    stats_m(u + 1)
                n = (i + 1) * P + META
                st = small[:, 64 + 8 * (u % 2):72 + 8 * (u % 2)]
                when_emptied(dve, ("MS", u))
                link(dve.reciprocal(st[:, 3:4], st[:, 2:3]))
                dve.tensor_scalar(mp[:, u % 2, 0:n], mp[:, u % 2, 0:n], st[:, 3:4], None, ALU.mult).then_inc(mprobs, 1)

            bx = bc[:, 0:T]

            def level_difference(h, n):
                s = LEVELS[n - 1]
                b = bx.rearrange("p (b x) -> p b x", x=2 * s)
                mid = b[:, :, s - 1:s].to_broadcast([P, T // (2 * s), 2 * s])
                dve.tensor_tensor(wl[:, 0:T].rearrange("p (b x) -> p b x", x=2 * s), b, mid,
                                  ALU.subtract).then_inc(level_diff, 1)

            att = attT.rearrange("p (c t) -> p c t", c=TT)

            def mask(n):
                return C("levels", n * P, (n + 1) * P).unsqueeze(1).to_broadcast([P, TT, P])

            def choose(h, n):
                key = ("lev", h, n)
                when_filled(dve, key)
                src = flat(key)[:, 0:T].rearrange("p (c t) -> p c t", c=TT)
                if n == 0:
                    if h:
                        when_filled(dve, ("go", h - 1))
                    empties(dve.tensor_tensor(att, src, mask(0), ALU.mult), key)
                else:
                    when_emptied(dve, ("lev", h, n - 1))
                    empties(dve.copy_predicated(att, mask(n).bitcast(U32), src), key)

            when_emptied(dve, ("gk", HG - 1))
            for h in range(HG):
                dve.wait_ge(zbias, h + 1)
                link(dve.scalar_tensor_tensor(la, la, 0.0, bc, ALU.min, ALU.subtract))
                dve.tensor_tensor_scan(bc, C("reset"), la, 0.0, ALU.mult, ALU.add).then_inc(cumulated, 1)
                dve.wait_ge(cumulated, h + 1)
                if h:
                    when_filled(dve, ("kd", h - 1))
                level_difference(h, 1)
                choose(h, 0)
                dve.wait_ge(decays, h + 1)
                dve.tensor_tensor(qb, qb, gq[:, h, :], ALU.mult).then_inc(qb_ready, 1)
                for n in range(1, 8):
                    dve.wait_ge(level_exp, 7 * h + n)
                    if n > 1:
                        when_filled(dve, ("lev", h, n - 1))
                    dve.tensor_tensor(ql, gq[:, h, :], wl[:, 0:T], ALU.mult)
                    dve.tensor_tensor(kl[:, 0:T], gk[:, h, 0:T], wl[:, 0:T], ALU.mult).then_inc(level_qk, 1)
                    dve.wait_ge(level_qk, 7 * h + n)
                    if n < 7:
                        level_difference(h, n + 1)
                    if n > 1:
                        choose(h, n - 1)
                when_filled(dve, ("lev", h, 7))
                b4 = bx.rearrange("p (c t) -> p c t", c=TT)
                dve.tensor_tensor(kl[:, 0:T].rearrange("p (c t) -> p c t", c=TT),
                                  b4[:, :, P - 1:P].to_broadcast([P, TT, P]), b4, ALU.subtract)
                dve.tensor_tensor(kl[:, T:TM], bc[:, TM - 1:TM].to_broadcast([P, META]), bc[:, T:TM],
                                  ALU.subtract).then_inc(kd_diff, 1)
                choose(h, 7)
                dve.wait_ge(kd_exp, h + 1)
                dve.tensor_tensor(kl, kl, gk[:, h, :], ALU.mult).then_inc(kd_ready, 1)
                if h:
                    when_filled(dve, ("go", h - 1))
                dve.wait_ge(decays, h + 1)
                for c in range(TT):
                    key = ("st", h, c)
                    when_filled(dve, key)
                    src = flat(key)[:, 0:HV]
                    if c == 0:
                        empties(dve.tensor_copy(state[:, 0, :], src), key)
                    else:
                        when_emptied(dve, ("st", h, c - 1))
                        empties(dve.scalar_tensor_tensor(state[:, c, :], state[:, c - 1, :], dec[:, c - 1:c], src,
                                                         ALU.mult, ALU.add), key)
            for h in range(HG):
                r = inverse(f"g{h}", T)
                for e in range(2):
                    scale_by(oT[:, 2 * h + e, :], oT[:, 2 * h + e, :], V("gnorm", e), r, e == 1)
            dve.wait_ge(normed, NORM[f"g{HG - 1}"] + 1)
            for h in range(HG):
                when_emptied(dve, ("gg", h))
                o = oT[:, 2 * h:2 * h + 2, :]
                dve.tensor_tensor(o, o, gate_s[:, h % 2, :, :], ALU.mult).then_inc(gated, 1)
            for m in range(4):
                when_filled(dve, ("oa", m))
                when_emptied(dve, ("ta", m))
                empties(dve.tensor_tensor(mixT[:, 2 * m:2 * m + 2, :], gate_s[:, m % 2, :, :], pair(("oa", m)),
                                          ALU.mult), ("oa", m))
            when_emptied(dve, ("oa", 3))
            for m in range(4):
                when_filled(dve, ("ob", m))
                when_emptied(dve, ("tb", m))
                if m:
                    dve.wait_ge(mixed, m)
                empties(dve.tensor_tensor(mix_tmp, gate_s[:, m % 2, :, :], pair(("ob", m)), ALU.mult), ("ob", m))
                when_emptied(dve, ("ob", m))
                x = mixT[:, 2 * m:2 * m + 2, :]
                dve.tensor_tensor(x, x, mix_tmp, ALU.add).then_inc(mixed, 1)
            for m in range(4):
                when_filled(dve, ("w2", m))
                x = resid[:, 2 * m:2 * m + 2, 0:T]
                empties(dve.tensor_tensor(x, x, pair(("w2", m)), ALU.add), ("w2", m))
            when_emptied(dve, ("w2", 3))
            big_norm("ffn", "ffn", normed_x, resid)

            iota16 = C("iota", 0, TOPK)
            for t in range(TT):
                if t:
                    when_filled(dve, ("tr", t - 1))
                for half in range(2):
                    when_emptied(dve, ("ps", t, half))
                for src, vals, index, n in ((sc, topv, topi_u, 16), (cand, best, bpos_u, HP)):
                    if src is cand:
                        v4 = topv.rearrange("p (h a) k -> p h a k", a=2)
                        link(dve.tensor_tensor(cand.rearrange("p h (a b) -> p h a b", a=TOPK),
                                               v4[:, :, 0, :].unsqueeze(3).to_broadcast([P, HP, TOPK, TOPK]),
                                               v4[:, :, 1, :].unsqueeze(2).to_broadcast([P, HP, TOPK, TOPK]), ALU.add))
                    for part in (slice(0, 8), slice(8, 16)):
                        for f in range(n):
                            ins = dve.max(vals[:, f, part], src[:, f, :])
                        link(ins)
                        for f in range(n):
                            ins = dve.max_index(index[:, f, part], vals[:, f, part], src[:, f, :])
                        link(ins)
                        if part.start == 0:
                            for f in range(n):
                                ins = dve.match_replace(src[:, f, :], vals[:, f, part], src[:, f, :], -3.0e38)
                            link(ins)
                dve.tensor_tensor(ent[:, 2, :].rearrange("p (h k) -> p h k", h=HP), best,
                                  best[:, :, 0:1].to_broadcast([P, HP, TOPK]), ALU.subtract).then_inc(soft_diff, 1)
                pos = bpos_u.rearrange("p h k -> p (h k)")
                dve.tensor_scalar(bi_u, pos, 4, None, ALU.logical_shift_right)
                link(dve.tensor_scalar(bj_u, pos, 15, None, ALU.bitwise_and))
                dve.tensor_copy(bi, bi_u)
                dve.tensor_copy(bj, bj_u)
                link(dve.tensor_copy(topi, topi_u))
                i4 = topi.rearrange("p (h a) k -> p h a k", a=2)
                for a, b in ((0, bi), (1, bj)):
                    link(dve.tensor_tensor(onehot, b.unsqueeze(2).to_broadcast([P, ENTRIES, TOPK]),
                                           iota16.unsqueeze(1).to_broadcast([P, ENTRIES, TOPK]), ALU.is_equal))
                    link(dve.tensor_tensor(onehot2.rearrange("p (h k) n -> p h k n", h=HP),
                                           onehot.rearrange("p (h k) n -> p h k n", h=HP),
                                           i4[:, :, a, :].unsqueeze(2).to_broadcast([P, HP, TOPK, TOPK]), ALU.mult))
                    link(dve.tensor_reduce(ent[:, a, :], onehot2, AX_X, ALU.add))
                dve.wait_ge(soft_exp, t + 1)
                e3 = ent[:, 2, :].rearrange("p (h k) -> p h k", h=HP)
                link(dve.tensor_reduce(bsum, e3, AX_X, ALU.add))
                link(dve.reciprocal(bsum, bsum))
                dve.tensor_tensor(e3, e3, bsum.unsqueeze(2).to_broadcast([P, HP, TOPK]), ALU.mult).then_inc(entries, 1)
            when_emptied(dve, ("tr", TT - 1))

            def one_hots(step):
                for half in range(2):
                    at_least(dve, spread, 2 * step + half - 1)
                    for j in range(4):
                        q = 4 * half + j
                        t = 8 * step + q
                        dve.tensor_scalar(oneA[:, q, :], C("iota"), entT[:, 0, bass.ds(t, 1)], entT[:, 2, bass.ds(t, 1)],
                                          ALU.is_equal, ALU.mult)
                        ins = dve.tensor_scalar(oneB[:, q, :], C("iota"), entT[:, 1, bass.ds(t, 1)], None, ALU.is_equal)
                    ins.then_inc(hot, 1)

            one_hots(0)
            with dve.Fori(1, T // 8) as step:
                one_hots(step)

            def coefs(g, s, turn):
                dve.wait_ge(g_in[s], 16 * turn)
                for j in range(EG):
                    dve.wait_ge(gelu_done, EG * g + j + 1)
                    c = coef[s][:, j, :]
                    dve.tensor_tensor(c, c, gslot[s][:, j, :], ALU.mult).then_inc(coef_done, 1)

            def add(g):
                for m in range(KD):
                    dve.wait_ge(out_done, KD * g + m + 1)
                    x = resid[:, m, 0:T]
                    dve.tensor_tensor(x, x, ps[:, 4 + m % 4, :], ALU.add).then_inc(added, 1)

            def both(it, last=False):
                coefs(2 * it + 1, 1, it + 1)
                at_least(dve, added, 2 * KD * it)
                add(2 * it)
                if not last:
                    coefs(2 * it + 2, 0, it + 2)
                dve.wait_ge(added, 2 * KD * it + KD)
                add(2 * it + 1)

            coefs(0, 0, 1)
            both(0)
            with dve.Fori(1, GROUPS // 2 - 1) as it:
                both(it)
            both(GROUPS // 2 - 1, last=True)


def at_least(eng, s, value):
    if not isinstance(value, int) or value > 0:
        eng.wait_ge(s, value)


def tables():
    c = np.zeros((P, NCONST), np.float32)

    def put(name, m):
        at, n = CONST[name]
        c[:, at:at + n] = m

    r = np.arange(P)
    put("ident", np.eye(P))
    put("ones", 1.0)
    put("heads64", (r[:, None] // 64 == r[None, :] // 64))
    rot = np.zeros((P, P), np.float32)
    for m in range(P):
        low = m % ROPE < ROPE // 2
        rot[m + 32 if low else m - 32, m] = -1.0 if low else 1.0
    put("rot", rot)
    put("iota", r[None, :])
    col = np.arange(T)
    at = T - P + r[:, None]
    seen = col[None, :] // CHUNK <= at // CHUNK
    put("dist", np.where(seen, np.abs(at - col[None, :]), 1e30))
    j, i = r[:, None], r[None, :]
    levels = [j == i]
    for s in LEVELS:
        levels.append((j // (2 * s) == i // (2 * s)) & (j % (2 * s) < s) & (i % (2 * s) >= s))
    put("levels", np.concatenate(levels, 1))
    reset = np.ones(TM)
    reset[0::P] = 0.0
    put("reset", reset[None, :])
    half = ROPE // 2
    inv = (np.float32(10000.0) ** (-np.arange(half, dtype=np.float32) / np.float32(half))).astype(np.float32)
    pos = np.concatenate([np.arange(META, TM), np.arange(META)]).astype(np.float32)
    ang = (inv[r % half][:, None] * pos[None, :]).astype(np.float32)
    put("cos", np.cos(ang))
    put("sin", np.sin(ang))
    return c


def kernel(**inputs):
    import concourse.bacc as _bacc
    from concourse.bass_utils import run_bass_kernel_spmd as _run

    x = {n: np.asarray(a) for n, a in inputs.items()}
    f = np.float32

    def cols(a):
        return np.asarray(a).reshape(-1, P).T

    def feature_major(a):
        return np.ascontiguousarray(a.T.reshape(-1, P, a.shape[0]).transpose(1, 0, 2))

    vecs = np.zeros((P, NVEC), f)

    def put(name, m):
        at, n = VEC[name]
        vecs[:m.shape[0], at:at + n] = m

    put("pre", cols(x["pre_norm_gain"][0]))
    put("mix", cols(x["norm_mix_2"][0]))
    put("subln", cols(x["subln_gain"][0]))
    put("conv", x["conv_w"][0].reshape(3, 4, P).transpose(2, 0, 1).reshape(P, 12))
    put("post", cols(x["post_norm_gain"][0]))
    put("ple", cols(x["ple_norm_gain"][0]))
    put("qnorm", cols(x["mla_q_norm_2"][0]))
    put("kvnorm", cols(x["mla_kv_norm_2"][0]))
    put("qn", cols(x["qn_nope_2"][0]))
    put("kn", cols(x["kn_nope_2"][0]))
    put("qp", np.concatenate([x["qn_pe_2"][0], x["qn_pe_2"][0]])[:, None])
    put("kp", np.concatenate([x["kn_pe_2"][0], x["kn_pe_2"][0]])[:, None])
    put("ba", cols(x["gla_b_a_2"][0]))
    put("gnorm", cols(x["gla_norm_2"][0]))
    put("ffn", cols(x["norm_ffn_2"][0]))
    put("lam", np.stack([x["lambda_q1"][0], x["lambda_q2"][0], x["lambda_k1"][0], x["lambda_k2"][0]], 1))
    put("eps", np.full((P, 1), EPS, f))
    put("subeps", np.full((P, 1), SUBLN_EPS, f))

    w1, w2 = x["w_in"][0], x["w_in_2"][0]
    part = {}
    for n, g in enumerate(("q", "k", "v", "za", "b", "c", "u", "zc")):
        part[g] = w1[:, n * 512:(n + 1) * 512]
    at = 0
    two = {}
    for g, n in (("cq", 384), ("ckv", 256), ("kpe", 64), ("gq", 512), ("gk", 512), ("gv", 1024), ("ga", 16),
                 ("gg", 1024), ("ta", 1024), ("tb", 1024)):
        two[g] = w2[:, at:at + n]
        at += n
    part["cq"] = two["cq"]
    part["ckv"] = np.concatenate([two["ckv"], two["kpe"], two["kpe"]], 1)
    for g in ("gq", "gk", "ga"):
        part[g] = two[g]
    uq = x["mla_w_uq_2"][0].reshape(384, HM, 192)
    part["uqn"] = uq[:, :, 0:128].reshape(384, 1024)
    part["uqp"] = uq[:, :, 128:192].reshape(384, 512)
    ukv = x["mla_w_ukv_2"][0].reshape(256, HM, 256)
    part["ukv"] = np.concatenate([ukv[:, :, 0:128].reshape(256, 1024), ukv[:, :, 128:256].reshape(256, 1024)], 1)
    part["ple"] = x["w_ple_proj"][0]
    for g, m in (("wo", x["w_out"][0]), ("pg", x["w_ple_gate"][0]), ("gv", two["gv"]), ("gg", two["gg"]),
                 ("ta", two["ta"]), ("tb", two["tb"]), ("oa", x["w_o_mla_2"][0]), ("ob", x["w_o_gla_2"][0]),
                 ("w2", x["w_out_2"][0]), ("pq", x["peer_w_q_2"][0])):
        for n in range(m.shape[1] // 512):
            part[f"{g}{n}"] = m[:, n * 512:(n + 1) * 512]
    weights = np.concatenate([part[n].reshape(k, P, c).transpose(1, 0, 2).reshape(P, k * c) for n, k, c in WEIGHTS], 1)

    u = x["peer_u_2"][0].reshape(P, GROUPS, EG, KD, P)
    v = x["peer_v_2"][0].reshape(P, GROUPS, EG, D)
    arrays = {
        "xT": feature_major(x["x"][0]), "metaT": feature_major(x["meta_2"]), "pT": feature_major(x["p"][0, 0]),
        "consts": tables(), "vecs": vecs, "weights": np.ascontiguousarray(weights),
        "wa2": x["gla_w_a2_2"][0], "keysT": np.ascontiguousarray(x["peer_keys_2"][0].transpose(2, 0, 1)),
        "uT": np.ascontiguousarray(u.transpose(1, 4, 3, 2, 0)).reshape(GROUPS, P, KD * EG * P),
        "vT": np.ascontiguousarray(v.transpose(1, 0, 2, 3)).reshape(GROUPS, P, EG * D),
    }
    nc = _bacc.Bacc("TRN2", target_bir_lowering=False, num_devices=1)
    A, ins = {}, {}
    for name, a in arrays.items():
        ins[f"in_{name}_dram"] = np.ascontiguousarray(a)
        A[name] = nc.dram_tensor(f"in_{name}_dram", a.shape, F32, kind="ExternalInput").ap()
    A["gates"] = nc.dram_tensor("gate_table", (P, GROUPS, EG * T), F32, kind="Internal").ap()
    A["out"] = nc.dram_tensor("out_0_dram", (D, T), F32, kind="ExternalOutput").ap()
    build(nc, A)
    r = _run(nc, [ins], core_ids=[0])
    return np.ascontiguousarray(r.results[0]["out_0_dram"].T)[None]
```

```python
from contextlib import ExitStack

import numpy as np

import concourse.bass as bass
from concourse import mybir

F32 = mybir.dt.float32
BF16 = mybir.dt.bfloat16
U32 = mybir.dt.uint32
ALU = mybir.AluOpType
ACT = mybir.ActivationFunctionType
AX_X = mybir.AxisListType.X

P = 128
D = 1024
KD = D // P
T = 512
TT = T // P
META = 16
TM = T + META
CHUNK = 64
NEG = -1e30

HA = 4
DQK = 64
SCALE_A = DQK ** -0.5
SLOPES = [2.0 ** (-8.0 * (h + 1) / HA) for h in range(HA)]
LAMBDA_INIT = 0.8 - 0.6
HM = 8
ROPE = 64
SCALE_M = (128 + ROPE) ** -0.5
HG = 4
HK = 128
HV = 256
TAU = 16.0
LEVELS = [64, 32, 16, 8, 4, 2, 1]
HP = 8
NKEYS = 128
TOPK = 16
ENTRIES = HP * TOPK
NE = NKEYS * NKEYS
EG = 4
GROUPS = NKEYS // EG
HALF = 64

EPS = 1e-6
SUBLN_EPS = 1e-5

CONST = {}
_at = 0
for _name, _n in (("ident", P), ("ones", P), ("heads64", P), ("rot", P), ("iota", P), ("dist", T),
                  ("levels", 8 * P), ("reset", TM), ("cos", TM), ("sin", TM)):
    CONST[_name] = (_at, _n)
    _at += _n
NCONST = _at

VEC = {}
_at = 0
for _name, _n in (("pre", 8), ("mix", 8), ("subln", 1), ("conv", 12), ("post", 8), ("ple", 8), ("qnorm", 3),
                  ("kvnorm", 2), ("qn", 1), ("kn", 1), ("qp", 1), ("kp", 1), ("ba", 4), ("gnorm", 2),
                  ("ffn", 8), ("lam", 4), ("eps", 1), ("subeps", 1)):
    VEC[_name] = (_at, _n)
    _at += _n
NVEC = _at

WEIGHTS = [("q", 8, 512), ("k", 8, 512), ("v", 8, 512), ("c", 8, 512), ("u", 8, 512), ("zc", 8, 512), ("b", 8, 512),
           ("za", 8, 512), ("wo0", 8, 512), ("wo1", 8, 512), ("ple", 2, 1024), ("pg0", 8, 512), ("pg1", 8, 512),
           ("cq", 8, 384), ("ckv", 8, 384), ("uqn", 3, 1024), ("uqp", 3, 512), ("ukv", 2, 2048),
           ("gq", 8, 512), ("gk", 8, 512), ("ga", 8, 16), ("gv0", 8, 512), ("gv1", 8, 512),
           ("ta0", 8, 512), ("oa0", 8, 512), ("ta1", 8, 512), ("oa1", 8, 512), ("gg0", 8, 512), ("gg1", 8, 512),
           ("tb0", 8, 512), ("ob0", 8, 512), ("tb1", 8, 512), ("ob1", 8, 512), ("w20", 8, 512), ("w21", 8, 512),
           ("pq0", 8, 512), ("pq1", 8, 512), ("pq2", 8, 512), ("pq3", 8, 512)]
WSLOT = 4096
NW = 3
WN = {w[0]: n for n, w in enumerate(WEIGHTS)}
WAT = {}
_at = 0
for _name, _k, _n in WEIGHTS:
    WAT[_name] = _at
    _at += _k * _n
NWTOT = _at

UNITS_A = [(h, i) for h in range(HA) for i in range(TT)]
UNITS_M = [(h, i) for h in range(HM) for i in range(TT)]


PARTS = [f"qn{m}" for m in range(4)] + [f"qp{m}" for m in range(2)] + [f"kn{h}" for h in range(HM)]

SIDE_M = {4 * n + 2: key for n, key in enumerate([("gq", 0), ("gq", 1)] + [("gk", h) for h in range(HG)] + [("ga", 0)])}


def psum_jobs():
    jobs = [("lam",), ("ss", "n1")]
    for g in ("q", "k", "v"):
        jobs += [(g, 0), (g, 1)]
    side = [(g, m) for g in ("c", "u", "zc", "b", "za") for m in (0, 1)]
    jobs += [("S", 0), ("S", 1)]
    for u in range(len(UNITS_A)):
        jobs.append(("T", u))
        if u + 2 < len(UNITS_A):
            jobs.append(("S", u + 2))
        if side:
            jobs.append(side.pop(0))
        jobs.append(("O", u))
    jobs += [("ss", "sl0"), ("ss", "sl1")]
    jobs += [("wo", m) for m in range(4)] + [("ple", m) for m in range(4)] + [("ss", "post"), ("ss", "ple")]
    jobs += [("pg", m) for m in range(4)]
    jobs.append(("ss", "mix"))
    jobs += [("cq", 0), ("cq", 1), ("ckv", 0), ("ckv", 1), ("kpe", 0)]
    jobs += [("ss", "cq"), ("ss", "ckv"), ("ss", "kpe"), ("rot", "kpe")]
    for n, name in enumerate(PARTS):
        jobs.append(({"qn": "uqn", "qp": "uqp", "kn": "kn"}[name[0:2]], int(name[2:])))
        if n >= 1:
            jobs.append(("ss", PARTS[n - 1]))
        if n >= 3 and PARTS[n - 3][0:2] == "qp":
            jobs.append(("rot", int(PARTS[n - 3][2:])))
    jobs.append(("ss", PARTS[-1]))
    jobs += [("mv", t) for t in range(TT + 1)]
    jobs += [("MS", 0), ("MS", 1)]
    for u in range(len(UNITS_M)):
        jobs.append(("MT", u))
        if u + 2 < len(UNITS_M):
            jobs.append(("MS", u + 2))
        if u in SIDE_M:
            jobs.append(SIDE_M[u])
        jobs.append(("MO", u))
    jobs += [("gv", g, m) for g in (0, 1) for m in (0, 1, 2)]
    for h in range(HG):
        jobs += [("z", h)] + [("lev", h, n) for n in range(3)] + [("ta", h)]
        jobs += [("lev", h, n) for n in range(3, 6)] + [("oa", h)] + [("lev", h, n) for n in range(6, 8)] + [("kd", h)]
        jobs += [("st", h, c) for c in range(TT)] + [("go", h)]
    jobs += [("ss", f"g{h}") for h in range(HG)]
    jobs += [("gg", h) for h in range(HG)]
    for m in range(4):
        jobs += [("tb", m), ("ob", m)]
    jobs += [("w2", m) for m in range(4)]
    jobs.append(("ss", "ffn"))
    jobs += [("pq", m) for m in range(8)]
    for t in range(TT):
        jobs += [("ps", t, 0), ("ps", t, 1), ("tr", t)]
    return {key: n for n, key in enumerate(jobs)}


JOB = psum_jobs()
NPAIR = 4

LAST = {"q": ("q", 1), "k": ("k", 1), "v": ("v", 1), "c": ("c", 1), "u": ("u", 1), "zc": ("zc", 1), "b": ("b", 1),
        "za": ("za", 1), "wo0": ("wo", 1), "wo1": ("wo", 3), "ple": ("ple", 3), "pg0": ("pg", 1), "pg1": ("pg", 3),
        "cq": ("cq", 1), "ckv": ("kpe", 0), "uqn": ("uqn", 3), "uqp": ("uqp", 1), "ukv": ("mv", TT),
        "gq": ("gq", 1), "gk": ("gk", HG - 1), "ga": ("ga", 0), "gv0": ("gv", 0, 2), "gv1": ("gv", 1, 2),
        "gg0": ("gg", 1), "gg1": ("gg", 3), "ta0": ("ta", 1), "ta1": ("ta", 3), "tb0": ("tb", 1), "tb1": ("tb", 3),
        "oa0": ("oa", 1), "oa1": ("oa", 3), "ob0": ("ob", 1), "ob1": ("ob", 3), "w20": ("w2", 1), "w21": ("w2", 3),
        "pq0": ("pq", 1), "pq1": ("pq", 3), "pq2": ("pq", 5), "pq3": ("pq", 7)}

NORMS = ([("n1", D, True), ("sl0", 128, False), ("sl1", 128, False), ("post", D, True), ("ple", D, True),
          ("mix", D, True), ("cq", 384, True), ("ckv", 256, False), ("kpe", 64, False)]
         + [(f"qn{m}", 128, False) for m in range(4)] + [(f"qp{m}", 64, False) for m in range(2)]
         + [(f"kn{h}", 128, False) for h in range(HM)] + [(f"g{h}", 256, False) for h in range(HG)]
         + [("ffn", D, True)])
NORM = {n[0]: k for k, n in enumerate(NORMS)}


def build(nc, A):
    ctx = ExitStack()
    with ctx:
        def sb(name, shape, dt=F32):
            return ctx.enter_context(nc.sbuf_tensor(name, shape, dt))

        def sem(name):
            return ctx.enter_context(nc.semaphore(name))

        wring = sb("wring", [P, NW * WSLOT])
        cst = sb("cst", [P, NCONST])
        vec = sb("vec", [P, NVEC])
        resid = sb("resid", [P, KD, TM])
        normed_x = sb("normed_x", [P, KD, TM])
        sqbuf = sb("sqbuf", [P, KD * TM])
        rt = sb("rt", [P, 2, 1056])
        small = sb("small", [P, 320])
        AREA = 25600
        area = sb("area", [P, AREA])
        ps = ctx.enter_context(nc.psum_tensor("ps", [P, 8, 512], F32))

        def C(name, a=0, b=None):
            at, n = CONST[name]
            return cst[:, at + a:at + (n if b is None else b)]

        def V(name, i=0):
            at, _ = VEC[name]
            return vec[:, at + i:at + i + 1]

        def view(start, *dims):
            n = int(np.prod(dims))
            assert start + n <= AREA, (start, dims)
            flat = area[:, start:start + n]
            if len(dims) == 1:
                return flat
            if len(dims) == 2:
                return flat.rearrange("p (a b) -> p a b", a=dims[0])
            return flat.rearrange("p (a b c) -> p a b c", a=dims[0], b=dims[1])

        xs = resid[:, :, 0:T]
        hs = normed_x[:, :, 0:T]
        small_sq = [sqbuf[:, 0:1056], sqbuf[:, 1056:2112]]
        sq_hi = sqbuf[:, 2112:4224]

        qT = view(0, 4, T)
        kT = view(2048, 4, T)
        v_tok = view(4096, TT, 512)
        zaT = view(6144, 4, T)
        gT = view(8192, 4, T + 2)
        szT = view(10248, 4, T)
        mixin = view(12296, KD, T)
        probs = view(21512, 6, 512).rearrange("p (s m) k -> p s m k", s=3)
        weights_p = view(18440, 2, 512)
        pT_sb = view(19464, 2, 512)
        pin = view(20488, 2, T)
        cT = sqbuf[:, 2112:4160].rearrange("p (a b) -> p a b", a=4)
        mixedT = view(0, KD, T)
        eT = view(4096, KD, T)
        sgT = view(8192, KD, T)
        qn = view(0, HM, T)
        qp = view(4096, 4, T)
        kn = view(6144, HM, TM)
        mv = view(10368, TT, 1024)
        mvm = view(14464, 1024)
        ya = view(15488, HM, T)
        cq = view(15488, 3, T)
        ckv = view(17024, 2, TM)
        mpt = view(19584, 2, 640)
        mp = sq_hi[:, 0:3 * TM].rearrange("p (a b) -> p a b", a=3)
        kp = sq_hi[:, 3 * TM:4 * TM]
        rot_tmp = view(19584, 1056)
        gq = sqbuf[:, 0:HG * T].rearrange("p (a b) -> p a b", a=HG)
        gk = view(21376, HG, TM)
        gv = view(4160, TT, 1024)
        gvm = view(8256, 1024)
        oT = view(9280, KD, T)
        la = view(13376, TM)
        bc = view(13904, TM)
        dec = view(14432, 8)
        gaT = view(23488, TM)
        wl = [view(24528, T), sqbuf[:, 2112:2112 + T]]
        ql = [view(14448, T), sqbuf[:, 2640:2640 + T]]
        kl = [sqbuf[:, 3152:3152 + TM], view(24016, T)]
        attT = sqbuf[:, 3680:3680 + T]
        state = view(19584, TT, HV)
        kdt = view(20608, TT + 1, P)
        qb = view(14976, T)
        mixT = view(0, KD, T)
        mix_tmp = view(24016, 2, T)
        gate_a = rt[:, :, 0:1024].rearrange("p s (a b) -> p s a b", a=2)
        gate_s = sq_hi[:, 0:2048].rearrange("p (s a b) -> p s a b", s=2, a=2)
        pq = view(0, 16, T)
        sc = view(8192, 16, P)
        cand = view(12288, HP, 256)
        onehot = view(14592, ENTRIES, TOPK)
        onehot2 = view(16640, ENTRIES, TOPK)
        topv = view(18688, 16, TOPK)
        topi = view(18944, 16, TOPK)
        best = view(19200, HP, TOPK)
        ent = view(19328, 3, P)
        bsum = view(19712, HP)
        topi_u = view(19728, 16, TOPK).bitcast(U32)
        bpos_u = view(19984, HP, TOPK).bitcast(U32)
        bi_u = view(20112, ENTRIES).bitcast(U32)
        bj_u = view(20240, ENTRIES).bitcast(U32)
        bi = view(20368, ENTRIES)
        bj = view(20496, ENTRIES)
        entT = rt[:, :, :].rearrange("p a b -> p (a b)")[:, 0:3 * T].rearrange("p (a b) -> p a b", a=3)
        ones_at = normed_x[:, :, :].rearrange("p k t -> p (k t)")
        oneA = ones_at[:, 0:16 * P].rearrange("p (a b) -> p a b", a=16)
        oneB = ones_at[:, 16 * P:32 * P].rearrange("p (a b) -> p a b", a=16)
        stage = view(0, 2, 8192)

        def halves(ap, *dims):
            flat2 = ap.bitcast(BF16).rearrange("p (z n) -> p z n", z=2)
            return [flat2[:, z, :].rearrange("p (a b) -> p a b", a=dims[0]) for z in range(2)]

        h_hl = halves(sqbuf[:, 0:KD * T], KD)
        u_raw = wring[:, 0:WSLOT].rearrange("p (k n) -> p k n", k=KD)
        v_raw = wring[:, WSLOT:2 * WSLOT].rearrange("p (j d) -> p j d", j=EG)
        u_hl = [halves(wring[:, 2 * WSLOT:3 * WSLOT], KD), halves(view(0, 4096), KD)]
        v_hl = [halves(view(4096, 4096), EG), halves(view(8192, 4096), EG)]
        gslot = [view(12288, EG, T), view(14336, EG, T)]
        coef = view(16384, EG, T)
        c_hl = [halves(view(18432, EG * T), EG), halves(view(20480, EG * T), EG)]

        wa2_sb = C("dist")[0:16, :]
        keys_sb = sb("keys_sb", [P, 2, P])

        consts_in = sem("consts_in")
        x_in = sem("x_in")
        p_in = sem("p_in")
        keys_in = sem("keys_in")
        w_in = [sem(f"w_in{i}") for i in range(NW)]
        filled = [sem(f"filled{i}") for i in range(NPAIR)]
        emptied = [sem(f"emptied{i}") for i in range(NPAIR)]
        squared = sem("squared")
        normed = sem("normed")
        dve_step = sem("dve_step")
        act_step = sem("act_step")
        lam_ready = sem("lam_ready")
        stats_ready = sem("stats_ready")
        exp_done = sem("exp_done")
        probs_ready = sem("probs_ready")
        mixin_ready = sem("mixin_ready")
        x1_ready = sem("x1_ready")
        x2_ready = sem("x2_ready")
        roped = sem("roped")
        neg_max = sem("neg_max")
        mprobs = sem("mprobs")
        zbias = sem("zbias")
        log_decay = sem("log_decay")
        cumulated = sem("cumulated")
        level_diff = sem("level_diff")
        level_exp = sem("level_exp")
        level_qk = sem("level_qk")
        kd_diff = sem("kd_diff")
        kd_exp = sem("kd_exp")
        kd_ready = sem("kd_ready")
        decays = sem("decays")
        qb_ready = sem("qb_ready")
        mixed = sem("mixed")
        gated = sem("gated")
        soft_diff = sem("soft_diff")
        soft_exp = sem("soft_exp")
        entries = sem("entries")
        hot = sem("hot")
        spread = sem("spread")
        copied = sem("copied")
        stored = [sem(f"stored{i}") for i in range(2)]
        hot_n1 = sem("hot_n1")
        hot_n2 = sem("hot_n2")
        n2_copied = sem("n2_copied")
        h_rounded = sem("h_rounded")
        h_split = sem("h_split")
        u_in = sem("u_in")
        u_rounded = sem("u_rounded")
        u_split = sem("u_split")
        v_in = sem("v_in")
        v_rounded = sem("v_rounded")
        v_split = sem("v_split")
        coef_mult = sem("coef_mult")
        coef_rounded = sem("coef_rounded")
        g_in = [sem(f"g_in{i}") for i in range(2)]
        pre_done = sem("pre_done")
        gelu_done = sem("gelu_done")
        coef_done = sem("coef_done")
        out_done = sem("out_done")
        added = sem("added")
        out_stored = sem("out_stored")

        def pair(key):
            n = JOB[key] % NPAIR
            return ps[:, 2 * n:2 * n + 2, :]

        def flat(key):
            return pair(key).rearrange("p a b -> p (a b)")

        def when_filled(eng, key):
            eng.wait_ge(filled[JOB[key] % NPAIR], JOB[key] // NPAIR + 1)

        def when_emptied(eng, key):
            eng.wait_ge(emptied[JOB[key] % NPAIR], JOB[key] // NPAIR + 1)

        def fills(ins, key):
            ins.then_inc(filled[JOB[key] % NPAIR], 1)

        def empties(ins, key):
            ins.then_inc(emptied[JOB[key] % NPAIR], 1)

        def W(name):
            g = WN[name]
            _, k, n = WEIGHTS[g]
            at = (g % NW) * WSLOT
            return wring[:, at:at + k * n].rearrange("p (k n) -> p k n", k=k)

        def norm_sq(name):
            k = NORM[name]
            return sqbuf if NORMS[k][2] else small_sq[k % 2]

        block = ctx.enter_context(nc.Block())

        @block.sync
        def _(sp):
            sp.dma_start(cst[:, :], A["consts"]).then_inc(consts_in, 16)
            sp.dma_start(vec[:, :], A["vecs"]).then_inc(consts_in, 16)
            sp.dma_start(xs, A["xT"]).then_inc(x_in, 16)
            sp.dma_start(resid[:, :, T:TM], A["metaT"]).then_inc(x_in, 16)
            for g, (name, k, n) in enumerate(WEIGHTS):
                if g >= NW:
                    when_filled(sp, LAST[WEIGHTS[g - NW][0]])
                at = (g % NW) * WSLOT
                sp.dma_start(wring[:, at:at + k * n],
                             A["weights"][:, WAT[name]:WAT[name] + k * n]).then_inc(w_in[g % NW], 16)
                if g == NW:
                    sp.dma_start(pin, A["pT"]).then_inc(p_in, 16)
                    sp.dma_start(keys_sb[:, :, :], A["keysT"]).then_inc(keys_in, 16)
                if name == "pg1":
                    when_emptied(sp, ("S", len(UNITS_A) - 1))
                    sp.dma_start(wa2_sb, A["wa2"]).then_inc(keys_in, 16)
            when_filled(sp, ("pq", 7))

            def load_u(g):
                at_least(sp, u_split, g)
                sp.dma_start(wring[:, 0:WSLOT], A["uT"][bass.ds(g, 1), :, :].rearrange("g p n -> p (g n)")
                             ).then_inc(u_in, 16)

            def load_v(g):
                at_least(sp, v_split, g)
                sp.dma_start(wring[:, WSLOT:2 * WSLOT], A["vT"][bass.ds(g, 1), :, :].rearrange("g p n -> p (g n)")
                             ).then_inc(v_in, 16)

            def load_gates(g, s):
                at_least(sp, coef_mult, EG * g - EG)
                sp.dma_start(gslot[s], A["gates"][:, bass.ds(g, 1), :].rearrange("p g (j t) -> p (g j) t", j=EG)
                             ).then_inc(g_in[s], 16)

            load_u(0)
            load_v(0)
            for n in range(T // HALF):
                sp.wait_ge(copied, (n + 1) * (HALF // 4))
                sp.dma_start(A["gates"].rearrange("p g (j t) -> p (g j) t", j=EG)[:, :, n * HALF:(n + 1) * HALF],
                             stage[:, n % 2, :].rearrange("p (j t) -> p j t", t=HALF)).then_inc(stored[n % 2], 16)
                if n == 0:
                    load_u(1)
            for i in range(2):
                sp.wait_ge(stored[i], 8 * (T // HALF))
            load_gates(0, 0)
            load_gates(1, 1)

            def ahead(g, s, last=0):
                if last < 2:
                    load_u(g + 2)
                if last < 3:
                    load_v(g + 1)
                if last < 2:
                    load_gates(g + 2, s)

            with sp.Fori(0, GROUPS // 2 - 1) as it:
                ahead(2 * it, 0)
                ahead(2 * it + 1, 1)
            ahead(GROUPS - 2, 0, last=2)
            for k in range(KD):
                sp.wait_ge(added, KD * (GROUPS - 1) + k + 1)
                sp.dma_start(A["out"][k * P:(k + 1) * P, :], resid[:, k, 0:T]).then_inc(out_stored, 16)
            sp.wait_ge(out_stored, 16 * KD)

        @block.tensor
        def _(pe):
            def claim(key):
                if JOB[key] >= NPAIR:
                    n = JOB[key] - NPAIR
                    pe.wait_ge(emptied[n % NPAIR], n // NPAIR + 1)

            def arrived(name):
                g = WN[name]
                pe.wait_ge(w_in[g % NW], 16 * (g // NW + 1))

            def project(key, name, tiles, src, k_tiles, width=T, col0=0):
                claim(key)
                arrived(name)
                out = flat(key)
                w = W(name)
                for a, m in enumerate(tiles):
                    for k in range(k_tiles):
                        mm = pe.matmul(out[:, a * 512:a * 512 + T], w[:, k, col0 + m * P:col0 + (m + 1) * P],
                                       src[:, k, 0:T], start=(k == 0), stop=(k == k_tiles - 1))
                    if width == TM:
                        for k in range(k_tiles):
                            mm = pe.matmul(out[:, T:TM], w[:, k, col0 + m * P:col0 + (m + 1) * P],
                                           src[:, k, T:TM], start=(k == 0), stop=(k == k_tiles - 1))
                fills(mm, key)

            def tokens(key, name, tiles, src, k_tiles, col0, width):
                claim(key)
                arrived(name)
                out = flat(key)
                w = W(name)
                at = 0
                for t in tiles:
                    n = P if t < TT else META
                    for c in range(0, width, 512):
                        for k in range(k_tiles):
                            mm = pe.matmul(out[0:n, at:at + 512], src[:, k, t * P:t * P + n],
                                           w[:, k, col0 + c:col0 + c + 512], start=(k == 0), stop=(k == k_tiles - 1))
                        at += 512
                fills(mm, key)

            def sums(name, ones, groups, width=T):
                key = ("ss", name)
                claim(key)
                pe.wait_ge(squared, NORM[name] + 1)
                sq = norm_sq(name)
                out = flat(key)
                for a, starts in enumerate(groups):
                    for n, c in enumerate(starts):
                        mm = pe.matmul(out[:, a * 512:a * 512 + T], ones, sq[:, c:c + T],
                                       start=(n == 0), stop=(n == len(starts) - 1))
                    if width == TM:
                        for n, c in enumerate(starts):
                            mm = pe.matmul(out[:, T:TM], ones, sq[:, c + T:c + TM],
                                           start=(n == 0), stop=(n == len(starts) - 1))
                fills(mm, key)

            ident, ones, heads64 = C("ident"), C("ones"), C("heads64")

            pe.wait_ge(consts_in, 32)
            pe.wait_ge(lam_ready, 1)
            claim(("lam",))
            fills(pe.matmul(flat(("lam",))[:, 0:2], ones, small[:, 0:2], start=True, stop=True), ("lam",))
            sums("n1", ones, [[k * T for k in range(KD)]])
            pe.wait_ge(normed, NORM["n1"] + 1)
            for g in ("q", "k"):
                for m in (0, 1):
                    project((g, m), g, (2 * m, 2 * m + 1), hs, KD)
            for m in (0, 1):
                tokens(("v", m), "v", (2 * m, 2 * m + 1), hs, KD, 0, 512)

            def scores_a(u):
                h, i = UNITS_A[u]
                key = ("S", u)
                claim(key)
                if u == 0:
                    when_emptied(pe, ("k", 1))
                for m in range(2):
                    mm = pe.matmul(pair(key)[:, m, 0:(i + 1) * P], qT[64 * m:64 * m + 64, h, i * P:(i + 1) * P],
                                   kT[64 * m:64 * m + 64, h, 0:(i + 1) * P], start=True, stop=True)
                fills(mm, key)

            side = [(g, m) for g in ("c", "u", "zc", "b", "za") for m in (0, 1)]
            scores_a(0)
            scores_a(1)
            for u, (h, i) in enumerate(UNITS_A):
                claim(("T", u))
                pe.wait_ge(probs_ready, u + 1)
                for b in range(i + 1):
                    mm = pe.transpose(flat(("T", u))[:, b * P:(b + 1) * P], weights_p[:, u % 2, b * P:(b + 1) * P], ident)
                fills(mm, ("T", u))
                if u + 2 < len(UNITS_A):
                    scores_a(u + 2)
                if side:
                    g, m = side.pop(0)
                    project((g, m), g, (2 * m, 2 * m + 1), hs, KD)
                claim(("O", u))
                when_emptied(pe, ("T", u))
                for b in range(i + 1):
                    mm = pe.matmul(flat(("O", u))[:, 0:P], v_tok[:, b, h * P:(h + 1) * P],
                                   pT_sb[:, u % 2, b * P:(b + 1) * P], start=(b == 0), stop=(b == i))
                fills(mm, ("O", u))
            for n in range(2):
                sums(f"sl{n}", ones, [[0], [T]])
            pe.wait_ge(mixin_ready, 2)
            for m in range(4):
                project(("wo", m), f"wo{m // 2}", (2 * (m % 2), 2 * (m % 2) + 1), mixin, KD)
            pe.wait_ge(p_in, 16)
            for m in range(4):
                project(("ple", m), "ple", (2 * m, 2 * m + 1), pin, 2)
            sums("post", ones, [[k * T for k in range(KD)]])
            sums("ple", ones, [[k * T for k in range(KD)]])
            pe.wait_ge(x1_ready, 1)
            for m in range(4):
                project(("pg", m), f"pg{m // 2}", (2 * (m % 2), 2 * (m % 2) + 1), xs, KD)

            sums("mix", ones, [[k * TM for k in range(KD)]], TM)
            pe.wait_ge(normed, NORM["mix"] + 1)
            project(("cq", 0), "cq", (0, 1), hs, KD)
            project(("cq", 1), "cq", (2,), hs, KD)
            project(("ckv", 0), "ckv", (0,), normed_x, KD, TM)
            project(("ckv", 1), "ckv", (1,), normed_x, KD, TM)
            project(("kpe", 0), "ckv", (2,), normed_x, KD, TM)
            sums("cq", ones, [[0, T, 2 * T]])
            sums("ckv", ones, [[0, TM]], TM)
            sums("kpe", heads64, [[0]], TM)
            claim(("rot", "kpe"))
            pe.wait_ge(normed, NORM["kpe"] + 1)
            pe.matmul(flat(("rot", "kpe"))[:, 0:T], C("rot"), kp[:, 0:T], start=True, stop=True)
            fills(pe.matmul(flat(("rot", "kpe"))[:, T:TM], C("rot"), kp[:, T:TM], start=True, stop=True), ("rot", "kpe"))
            def project_part(name):
                kind, m = name[0:2], int(name[2:])
                if kind == "qn":
                    if m == 0:
                        pe.wait_ge(normed, NORM["cq"] + 1)
                    project(("uqn", m), "uqn", (2 * m, 2 * m + 1), cq, 3)
                elif kind == "qp":
                    project(("uqp", m), "uqp", (2 * m, 2 * m + 1), cq, 3)
                else:
                    if m == 0:
                        pe.wait_ge(normed, NORM["ckv"] + 1)
                    project(("kn", m), "ukv", (m,), ckv, 2, TM)

            def sum_part(name):
                kind = name[0:2]
                if kind == "qn":
                    sums(name, ones, [[0], [T]])
                elif kind == "qp":
                    sums(name, heads64, [[0], [T]])
                else:
                    sums(name, ones, [[0]], TM)

            for n, name in enumerate(PARTS):
                project_part(name)
                if n >= 1:
                    sum_part(PARTS[n - 1])
                if n >= 3 and PARTS[n - 3][0:2] == "qp":
                    m = int(PARTS[n - 3][2:])
                    claim(("rot", m))
                    pe.wait_ge(normed, NORM[f"qp{m}"] + 1)
                    for a in range(2):
                        mm = pe.matmul(pair(("rot", m))[:, a, :], C("rot"), qp[:, 2 * m + a, :], start=True, stop=True)
                    fills(mm, ("rot", m))
            sum_part(PARTS[-1])
            for t in range(TT + 1):
                tokens(("mv", t), "ukv", (t,), ckv, 2, 1024, 1024)

            def scores_m(u):
                h, i = UNITS_M[u]
                key = ("MS", u)
                claim(key)
                if u == 0:
                    pe.wait_ge(normed, NORM["kn7"] + 1)
                    pe.wait_ge(roped, 3)
                nk = (i + 1) * P
                r = 64 * (h % 2)
                out = flat(key)
                for at, a, n in ((0, 0, nk), (nk, T, META)):
                    pe.matmul(out[:, at:at + n], qn[:, h, i * P:(i + 1) * P], kn[:, h, a:a + n], start=True, stop=False)
                    mm = pe.matmul(out[:, at:at + n], qp[r:r + 64, h // 2, i * P:(i + 1) * P], kp[r:r + 64, a:a + n],
                                   start=False, stop=True)
                fills(mm, key)

            def side_m(g, m):
                if g == "gq":
                    project((g, m), "gq", (2 * m, 2 * m + 1), hs, KD)
                elif g == "gk":
                    project((g, m), "gk", (m,), normed_x, KD, TM)
                else:
                    claim(("ga", 0))
                    arrived("ga")
                    for a, n in ((0, T), (T, META)):
                        for k in range(KD):
                            mm = pe.matmul(flat(("ga", 0))[0:16, a:a + n], W("ga")[:, k, :], normed_x[:, k, a:a + n],
                                           start=(k == 0), stop=(k == KD - 1))
                    fills(mm, ("ga", 0))

            scores_m(0)
            scores_m(1)
            for u, (h, i) in enumerate(UNITS_M):
                nk = (i + 1) * P
                claim(("MT", u))
                pe.wait_ge(mprobs, u + 1)
                for b in range(i + 1):
                    pe.transpose(flat(("MT", u))[:, b * P:(b + 1) * P], mp[:, u % 3, b * P:(b + 1) * P], ident)
                fills(pe.transpose(flat(("MT", u))[0:META, 512:640], mp[:, u % 3, nk:nk + META], ident), ("MT", u))
                if u + 2 < len(UNITS_M):
                    scores_m(u + 2)
                if u in SIDE_M:
                    side_m(*SIDE_M[u])
                claim(("MO", u))
                when_emptied(pe, ("MT", u))
                for b in range(i + 1):
                    pe.matmul(flat(("MO", u))[:, 0:P], mv[:, b, h * P:(h + 1) * P], mpt[:, u % 2, b * P:(b + 1) * P],
                              start=(b == 0), stop=False)
                fills(pe.matmul(flat(("MO", u))[:, 0:P], mvm[0:META, h * P:(h + 1) * P], mpt[0:META, u % 2, 512:640],
                                start=False, stop=True), ("MO", u))

            for g in (0, 1):
                for m in (0, 1):
                    tokens(("gv", g, m), f"gv{g}", (2 * m, 2 * m + 1), normed_x, KD, 0, 512)
                tokens(("gv", g, 2), f"gv{g}", (TT,), normed_x, KD, 0, 512)
            pe.wait_ge(keys_in, 32)
            when_emptied(pe, ("gv", 1, 2))
            for h in range(HG):
                claim(("z", h))
                if h == 0:
                    when_emptied(pe, ("ga", 0))
                for a, n in ((0, T), (T, META)):
                    mm = pe.matmul(flat(("z", h))[:, a:a + n], wa2_sb[:, h * P:(h + 1) * P], gaT[0:16, a:a + n],
                                   start=True, stop=True)
                fills(mm, ("z", h))
                for n in range(8):
                    key = ("lev", h, n)
                    claim(key)
                    if n:
                        pe.wait_ge(level_qk, 7 * h + n)
                    for c in range(TT):
                        lhs = gk[:, h, c * P:(c + 1) * P] if n == 0 else kl[n % 2][:, c * P:(c + 1) * P]
                        rhs = gq[:, h, c * P:(c + 1) * P] if n == 0 else ql[n % 2][:, c * P:(c + 1) * P]
                        mm = pe.matmul(flat(key)[:, c * P:(c + 1) * P], lhs, rhs, start=True, stop=True)
                    fills(mm, key)
                    if n in (2, 5):
                        g = "ta" if n == 2 else "oa"
                        project((g, h), f"{g}{h // 2}", (2 * (h % 2), 2 * (h % 2) + 1), hs if n == 2 else ya, KD)
                claim(("kd", h))
                pe.wait_ge(kd_ready, h + 1)
                for c in range(TT):
                    pe.transpose(flat(("kd", h))[:, c * P:(c + 1) * P], kl[0][:, c * P:(c + 1) * P], ident)
                fills(pe.transpose(flat(("kd", h))[0:META, 512:640], kl[0][:, T:TM], ident), ("kd", h))
                when_emptied(pe, ("kd", h))
                for c in range(TT):
                    key = ("st", h, c)
                    claim(key)
                    if c == 0:
                        mm = pe.matmul(flat(key)[:, 0:HV], kdt[0:META, TT, :], gvm[0:META, h * HV:(h + 1) * HV],
                                       start=True, stop=True)
                    else:
                        mm = pe.matmul(flat(key)[:, 0:HV], kdt[:, c - 1, :], gv[:, c - 1, h * HV:(h + 1) * HV],
                                       start=True, stop=True)
                    fills(mm, key)
                key = ("go", h)
                claim(key)
                when_emptied(pe, ("lev", h, 7))
                pe.wait_ge(qb_ready, h + 1)
                when_emptied(pe, ("st", h, TT - 1))
                for e in range(2):
                    for c in range(TT):
                        pe.matmul(pair(key)[:, e, c * P:(c + 1) * P], gv[:, c, h * HV + e * P:h * HV + (e + 1) * P],
                                  attT[:, c * P:(c + 1) * P], start=True, stop=False)
                        mm = pe.matmul(pair(key)[:, e, c * P:(c + 1) * P], state[:, c, e * P:(e + 1) * P],
                                       qb[:, c * P:(c + 1) * P], start=False, stop=True)
                fills(mm, key)
            for h in range(HG):
                sums(f"g{h}", ones, [[0, T]])
            for h in range(HG):
                project(("gg", h), f"gg{h // 2}", (2 * (h % 2), 2 * (h % 2) + 1), hs, KD)
            for m in range(4):
                tiles = (2 * (m % 2), 2 * (m % 2) + 1)
                project(("tb", m), f"tb{m // 2}", tiles, hs, KD)
                pe.wait_ge(gated, HG)
                project(("ob", m), f"ob{m // 2}", tiles, oT, KD)
            pe.wait_ge(mixed, 4)
            for m in range(4):
                project(("w2", m), f"w2{m // 2}", (2 * (m % 2), 2 * (m % 2) + 1), mixT, KD)

            sums("ffn", ones, [[k * T for k in range(KD)]])
            pe.wait_ge(normed, NORM["ffn"] + 1)
            for m in range(8):
                project(("pq", m), f"pq{m // 2}", (2 * (m % 2), 2 * (m % 2) + 1), hs, KD)
            when_emptied(pe, ("pq", 7))
            when_emptied(pe, ("pq", 6))
            for t in range(TT):
                for half in range(2):
                    key = ("ps", t, half)
                    claim(key)
                    for j in range(8):
                        f = 8 * half + j
                        mm = pe.matmul(flat(key)[:, j * P:(j + 1) * P], pq[:, f, t * P:(t + 1) * P],
                                       keys_sb[:, f % 2, :], start=True, stop=True)
                    fills(mm, key)
                key = ("tr", t)
                claim(key)
                pe.wait_ge(entries, t + 1)
                for j in range(3):
                    mm = pe.transpose(flat(key)[:, j * P:(j + 1) * P], ent[:, j, :], ident)
                fills(mm, key)

            for key in (("ps", TT - 1, 0), ("ps", TT - 1, 1), ("tr", TT - 1), ("tr", TT - 2)):
                when_emptied(pe, key)

            def spread_tokens(step):
                for q in range(4):
                    pe.wait_ge(hot, 4 * step + q + 1)
                    pe.wait_ge(hot_n2, 4 * step + q + 1)
                    at_least(pe, copied, 4 * step + q - 3)
                    for j in range(4):
                        mm = pe.matmul(ps[:, q, j * P:(j + 1) * P], oneA[:, 4 * q + j, :],
                                       oneB[:, 4 * q + j, :], start=True, stop=True)
                    mm.then_inc(spread, 1)

            spread_tokens(0)
            with pe.Fori(1, T // 16) as step:
                spread_tokens(step)
            pe.wait_ge(copied, T // 4)

            def pre(g, s):
                pe.wait_ge(u_split, g + 1)
                (u_hi, u_lo), (h_hi, h_lo) = u_hl[s], h_hl
                for j in range(EG):
                    at_least(pe, gelu_done, EG * g - EG + j + 1)
                    n = slice(j * P, (j + 1) * P)
                    for k in range(KD):
                        pe.matmul(ps[:, j, :], u_hi[:, k, n], h_hi[:, k, :], start=(k == 0), stop=False)
                        pe.matmul(ps[:, j, :], u_hi[:, k, n], h_lo[:, k, :], start=False, stop=False)
                        mm = pe.matmul(ps[:, j, :], u_lo[:, k, n], h_hi[:, k, :], start=False, stop=(k == KD - 1))
                    mm.then_inc(pre_done, 1)

            def combine(g, s):
                pe.wait_ge(v_split, g + 1)
                pe.wait_ge(coef_done, EG * g + EG)
                (v_hi, v_lo), (c_hi, c_lo) = v_hl[s], c_hl[s]
                for m in range(KD):
                    at_least(pe, added, KD * g + m - 3)
                    d = slice(m * P, (m + 1) * P)
                    out = ps[:, 4 + m % 4, :]
                    for j in range(EG):
                        pe.matmul(out, v_hi[:, j, d], c_hi[:, j, :], start=(j == 0), stop=False)
                        pe.matmul(out, v_hi[:, j, d], c_lo[:, j, :], start=False, stop=False)
                        mm = pe.matmul(out, v_lo[:, j, d], c_hi[:, j, :], start=False, stop=(j == EG - 1))
                    mm.then_inc(out_done, 1)

            def two_groups(it, last=False):
                pre(2 * it + 1, 1)
                combine(2 * it, 0)
                if not last:
                    pre(2 * it + 2, 0)
                combine(2 * it + 1, 1)

            pe.wait_ge(h_split, 1)
            pre(0, 0)
            two_groups(0)
            with pe.Fori(1, GROUPS // 2 - 1) as it:
                two_groups(it)
            two_groups(GROUPS // 2 - 1, last=True)

        @block.scalar
        def _(act):
            steps = [0]

            def link(ins):
                steps[0] += 1
                ins.then_inc(act_step, 1)
                act.wait_ge(act_step, steps[0])

            def copy_out(key, dst, src, func=ACT.Copy, scale=1.0):
                when_filled(act, key)
                empties(act.activation(dst, src, func, scale=scale), key)

            def square(name, dst, src):
                k = NORM[name]
                back = 1 if (NORMS[k][2] or NORMS[k - 1][2]) else 2
                if k >= back:
                    when_filled(act, ("ss", NORMS[k - back][0]))
                act.activation(dst, src, ACT.Square).then_inc(squared, 1)

            def root(name, width, eps="eps"):
                k = NORM[name]
                if k >= 2:
                    act.wait_ge(normed, k - 1)
                when_filled(act, ("ss", name))
                empties(act.activation(rt[:, k % 2, 0:width], flat(("ss", name))[:, 0:width], ACT.Sqrt,
                                       bias=V(eps), scale=1.0 / NORMS[k][1]), ("ss", name))

            sq_x = sqbuf[:, 0:KD * T].rearrange("p (k t) -> p k t", k=KD)

            act.wait_ge(x_in, 32)
            act.wait_ge(consts_in, 32)
            square("n1", sq_x, xs)
            copy_out(("lam",), small[:, 2:4], flat(("lam",))[:, 0:2], ACT.Exp)
            root("n1", T)
            for m in range(2):
                copy_out(("q", m), qT[:, 2 * m:2 * m + 2, :], pair(("q", m)))
            for m in range(2):
                copy_out(("k", m), kT[:, 2 * m:2 * m + 2, :], pair(("k", m)))
            for m in range(2):
                copy_out(("v", m), v_tok[:, 2 * m:2 * m + 2, :], pair(("v", m)))

            def exps_a(u):
                h, i = UNITS_A[u]
                nk = (i + 1) * P
                st = small[:, 16 + 16 * (u % 3):32 + 16 * (u % 3)]
                act.wait_ge(stats_ready, u + 1)
                for m in range(2):
                    e = act.activation(probs[:, u % 3, m, 0:nk], probs[:, u % 3, m, 0:nk], ACT.Exp,
                                       bias=st[:, 2 + m:3 + m], scale=SCALE_A, accum_out=st[:, 4 + m:5 + m])
                e.then_inc(exp_done, 1)

            side = [(g, m) for g in ("c", "u", "zc", "b", "za") for m in (0, 1)]
            exps_a(0)
            exps_a(1)
            for u, (h, i) in enumerate(UNITS_A):
                nk = (i + 1) * P
                if u >= 2:
                    when_filled(act, ("O", u - 2))
                copy_out(("T", u), pT_sb[:, u % 2, 0:nk], flat(("T", u))[:, 0:nk])
                if side:
                    g, m = side.pop(0)
                    if g == "c":
                        copy_out((g, m), cT[:, 2 * m:2 * m + 2, :], pair((g, m)))
                    if g == "zc":
                        copy_out((g, m), szT[:, 2 * m:2 * m + 2, :], pair((g, m)), ACT.Silu)
                    if g == "za":
                        copy_out((g, m), zaT[:, 2 * m:2 * m + 2, :], pair((g, m)), ACT.Silu)
                copy_out(("O", u), mixin[:, h, i * P:(i + 1) * P], flat(("O", u))[:, 0:P])
                if u + 2 < len(UNITS_A):
                    exps_a(u + 2)
            when_emptied(act, ("O", len(UNITS_A) - 1))
            for n in range(2):
                square(f"sl{n}", small_sq[NORM[f"sl{n}"] % 2][:, 0:1024].rearrange("p (a b) -> p a b", a=2),
                       mixin[:, 2 * n:2 * n + 2, :])
            for n in range(2):
                root(f"sl{n}", 1024, "subeps")
            for m in range(4):
                copy_out(("wo", m), mixedT[:, 2 * m:2 * m + 2, :], pair(("wo", m)))
            when_emptied(act, ("wo", 3))
            square("post", sq_x, mixedT)
            for m in range(4):
                copy_out(("ple", m), eT[:, 2 * m:2 * m + 2, :], pair(("ple", m)))
            root("post", T)
            when_emptied(act, ("ple", 3))
            square("ple", sq_x, eT)
            root("ple", T)
            for m in range(4):
                copy_out(("pg", m), sgT[:, 2 * m:2 * m + 2, :], pair(("pg", m)), ACT.Sigmoid)

            act.wait_ge(x2_ready, 1)
            square("mix", sqbuf[:, :].rearrange("p (k t) -> p k t", k=KD), resid[:, :, :])
            root("mix", TM)
            copy_out(("cq", 0), cq[:, 0:2, :], pair(("cq", 0)))
            copy_out(("cq", 1), cq[:, 2, :], flat(("cq", 1))[:, 0:T])
            when_emptied(act, ("cq", 1))
            square("cq", sqbuf[:, 0:3 * T].rearrange("p (k t) -> p k t", k=3), cq)
            for k in range(2):
                copy_out(("ckv", k), ckv[:, k, :], flat(("ckv", k))[:, 0:TM])
            copy_out(("kpe", 0), kp, flat(("kpe", 0))[:, 0:TM])
            root("cq", T)
            when_emptied(act, ("kpe", 0))
            square("ckv", norm_sq("ckv")[:, 0:2 * TM].rearrange("p (k t) -> p k t", k=2), ckv)
            square("kpe", norm_sq("kpe")[:, 0:TM], kp)
            root("ckv", TM)
            root("kpe", TM)

            def raw_part(name):
                kind, m = name[0:2], int(name[2:])
                sq = norm_sq(name)
                if kind == "kn":
                    key = ("kn", m)
                    copy_out(key, kn[:, m, :], flat(key)[:, 0:TM])
                    when_emptied(act, key)
                    square(name, sq[:, 0:TM], kn[:, m, :])
                else:
                    key, dst = (("uqn", m), qn) if kind == "qn" else (("uqp", m), qp)
                    copy_out(key, dst[:, 2 * m:2 * m + 2, :], pair(key))
                    when_emptied(act, key)
                    square(name, sq[:, 0:1024].rearrange("p (a b) -> p a b", a=2), dst[:, 2 * m:2 * m + 2, :])

            for n, name in enumerate(PARTS):
                raw_part(name)
                if n >= 1:
                    root(PARTS[n - 1], TM if PARTS[n - 1][0:2] == "kn" else 1024)
            root(PARTS[-1], TM)
            for t in range(TT + 1):
                if t < TT:
                    copy_out(("mv", t), mv[:, t, :], flat(("mv", t)))
                else:
                    copy_out(("mv", t), mvm[0:META, :], flat(("mv", t))[0:META, :])

            def exps_m(u):
                h, i = UNITS_M[u]
                n = (i + 1) * P + META
                st = small[:, 64 + 8 * (u % 3):72 + 8 * (u % 3)]
                act.wait_ge(neg_max, u + 1)
                if u >= 3:
                    when_filled(act, ("MT", u - 3))
                empties(act.activation(mp[:, u % 3, 0:n], flat(("MS", u))[:, 0:n], ACT.Exp, bias=st[:, 1:2],
                                       scale=SCALE_M, accum_out=st[:, 2:3]), ("MS", u))

            exps_m(0)
            exps_m(1)
            for u, (h, i) in enumerate(UNITS_M):
                nk = (i + 1) * P
                key = ("MT", u)
                when_filled(act, key)
                if u >= 2:
                    when_filled(act, ("MO", u - 2))
                act.activation(mpt[0:META, u % 2, 512:640], flat(key)[0:META, 512:640], ACT.Copy)
                empties(act.activation(mpt[:, u % 2, 0:nk], flat(key)[:, 0:nk], ACT.Copy), key)
                if u in SIDE_M:
                    g, m = key = SIDE_M[u]
                    if g == "gq":
                        copy_out(key, gq[:, 2 * m:2 * m + 2, :], pair(key), scale=HK ** -0.5)
                    elif g == "gk":
                        copy_out(key, gk[:, m, :], flat(key)[:, 0:TM])
                    else:
                        copy_out(key, gaT[0:16, :], flat(key)[0:16, 0:TM])
                copy_out(("MO", u), ya[:, h, i * P:(i + 1) * P], flat(("MO", u))[:, 0:P])
                if u + 2 < len(UNITS_M):
                    exps_m(u + 2)

            for g in (0, 1):
                for m in (0, 1):
                    copy_out(("gv", g, m), gv[:, 2 * m:2 * m + 2, 512 * g:512 * g + 512], pair(("gv", g, m)))
                copy_out(("gv", g, 2), gvm[0:META, 512 * g:512 * g + 512], flat(("gv", g, 2))[0:META, 0:512])
            for h in range(HG):
                key = ("z", h)
                when_filled(act, key)
                if h:
                    act.wait_ge(kd_ready, h)
                act.activation(la, flat(key)[:, 0:TM], ACT.Identity, bias=V("ba", h))
                empties(act.activation(bc, flat(key)[:, 0:TM], ACT.Abs, bias=V("ba", h)), key)
                when_emptied(act, key)
                link(act.activation(bc, bc, ACT.Exp, scale=-1.0))
                act.activation(bc, bc, ACT.Ln, bias=C("ones", 0, 1)).then_inc(zbias, 1)
                act.wait_ge(cumulated, h + 1)
                if h:
                    when_filled(act, ("go", h - 1))
                act.activation(qb, bc[:, 0:T], ACT.Exp, scale=1 / TAU)
                act.activation(dec[:, 0:TT], bc[:, 0:T].rearrange("p (c t) -> p c t", t=P)[:, :, P - 1], ACT.Exp,
                               scale=1 / TAU).then_inc(decays, 1)
                for n, s in enumerate(LEVELS):
                    act.wait_ge(level_diff, 7 * h + n + 1)
                    w = wl[(n + 1) % 2].rearrange("p (b x s) -> p b x s", x=2, s=s)
                    act.activation(w[:, :, 0, :], w[:, :, 0, :], ACT.Exp, scale=-1 / TAU)
                    act.activation(w[:, :, 1, :], w[:, :, 1, :], ACT.Exp, scale=1 / TAU).then_inc(level_exp, 1)
                    if n == 3:
                        when_filled(act, ("ta", h))
                        if h >= 2:
                            when_emptied(act, ("oa", h - 2))
                        empties(act.activation(gate_a[:, h % 2, :, :], pair(("ta", h)), ACT.Sigmoid), ("ta", h))
                act.wait_ge(kd_diff, h + 1)
                act.activation(kl[0], kl[0], ACT.Exp, scale=1 / TAU).then_inc(kd_exp, 1)
                key = ("kd", h)
                when_filled(act, key)
                if h:
                    when_filled(act, ("st", h - 1, TT - 1))
                act.activation(kdt[0:META, TT, :], flat(key)[0:META, 512:640], ACT.Copy)
                empties(act.activation(kdt[:, 0:TT, :].rearrange("p a b -> p (a b)"), flat(key)[:, 0:T], ACT.Copy), key)
                copy_out(("go", h), oT[:, 2 * h:2 * h + 2, :], pair(("go", h)))
            when_emptied(act, ("go", HG - 1))
            for h in range(HG):
                square(f"g{h}", norm_sq(f"g{h}")[:, 0:1024].rearrange("p (a b) -> p a b", a=2),
                       oT[:, 2 * h:2 * h + 2, :])
                if h >= 1:
                    root(f"g{h - 1}", T)
            root(f"g{HG - 1}", T)

            def gate(key, func, k, before):
                when_filled(act, key)
                if before is not None:
                    before()
                empties(act.activation(gate_s[:, k % 2, :, :], pair(key), func), key)

            for h in range(HG):
                gate(("gg", h), ACT.Silu, h, (lambda: act.wait_ge(gated, h - 1)) if h >= 2 else None)
            for m in range(4):
                gate(("tb", m), ACT.Sigmoid, m,
                     (lambda: act.wait_ge(gated, HG)) if m < 2 else (lambda: when_emptied(act, ("ob", m - 2))))

            when_emptied(act, ("w2", 3))
            square("ffn", sq_x, xs)
            root("ffn", T)
            act.wait_ge(normed, NORM["ffn"] + 1)
            act.activation(h_hl[0], hs, ACT.Copy).then_inc(h_rounded, 1)
            for m in range(8):
                copy_out(("pq", m), pq[:, 2 * m:2 * m + 2, :], pair(("pq", m)))
            for t in range(TT):
                if t:
                    act.wait_ge(entries, t)
                for half in range(2):
                    key = ("ps", t, half)
                    copy_out(key, sc[:, 8 * half:8 * half + 8, :].rearrange("p a b -> p (a b)"), flat(key))
                act.wait_ge(soft_diff, t + 1)
                act.activation(ent[:, 2, :], ent[:, 2, :], ACT.Exp).then_inc(soft_exp, 1)
                copy_out(("tr", t), entT[:, :, t * P:(t + 1) * P],
                         flat(("tr", t))[:, 0:3 * P].rearrange("p (a b) -> p a b", a=3))

            def copy_tokens(n, i):
                dst = stage[:, n % 2, :].rearrange("p (j t) -> p t j", t=HALF)
                for q in range(4):
                    act.wait_ge(spread, 4 * (4 * n + i) + q + 1)
                    act.activation(dst[:, bass.ds(16 * i + 4 * q, 4), :],
                                   ps[:, q, :].rearrange("p (t j) -> p t j", t=4), ACT.Copy).then_inc(copied, 1)

            def round_u(g, s):
                act.wait_ge(u_in, 16 * g + 16)
                at_least(act, pre_done, EG * g - EG)
                act.activation(u_hl[s][0], u_raw, ACT.Copy).then_inc(u_rounded, 1)

            def round_v(g, s):
                act.wait_ge(v_in, 16 * g + 16)
                at_least(act, out_done, KD * g - KD)
                act.activation(v_hl[s][0], v_raw, ACT.Copy).then_inc(v_rounded, 1)

            round_u(0, 0)
            for n in range(T // HALF):
                if n >= 2:
                    act.wait_ge(stored[n % 2], 16 * (n // 2))
                with act.Fori(0, HALF // 16) as i:
                    copy_tokens(n, i)
            for i in range(2):
                act.wait_ge(stored[i], 8 * (T // HALF))

            def gelus(g, s):
                def gelu(j):
                    act.wait_ge(pre_done, EG * g + j + 1)
                    at_least(act, coef_done, EG * g - EG + j + 1)
                    act.activation(coef[:, j, :], ps[:, j, :], ACT.Gelu).then_inc(gelu_done, 1)

                def round_coef(j):
                    act.wait_ge(coef_mult, EG * g + j + 1)
                    act.activation(c_hl[s][0][:, j, :], coef[:, j, :], ACT.Copy).then_inc(coef_rounded, 1)

                gelu(0)
                at_least(act, out_done, KD * g - KD)
                for j in range(1, EG):
                    gelu(j)
                    round_coef(j - 1)
                round_coef(EG - 1)

            def period(g, s, last=0):
                if last < 2:
                    round_u(g + 2, s)
                if last < 3:
                    round_v(g + 1, 1 - s)
                    gelus(g + 1, 1 - s)

            round_u(1, 1)
            round_v(0, 0)
            gelus(0, 0)
            period(0, 0)
            period(1, 1)
            with act.Fori(1, GROUPS // 2 - 1) as it:
                period(2 * it, 0)
                period(2 * it + 1, 1)
            period(GROUPS - 2, 0, last=2)

        @block.vector
        def _(dve):
            steps = [0]

            def link(ins):
                steps[0] += 1
                ins.then_inc(dve_step, 1)
                dve.wait_ge(dve_step, steps[0])

            def inverse(name, width):
                when_emptied(dve, ("ss", name))
                r = rt[:, NORM[name] % 2, 0:width]
                link(dve.reciprocal(r, r))
                return r

            def scale_by(dst, src, gain, r, last=None):
                ins = dve.scalar_tensor_tensor(dst, src, gain, r, ALU.mult, ALU.mult)
                if last:
                    ins.then_inc(normed, 1)

            def big_norm(name, gain, dst, src, width=T):
                r = inverse(name, width)
                for k in range(KD):
                    scale_by(dst[:, k, 0:width], src[:, k, 0:width], V(gain, k), r, k == KD - 1)
                dve.wait_ge(normed, NORM[name] + 1)

            dve.wait_ge(consts_in, 32)
            dve.tensor_tensor(small[:, 0:2], vec[:, VEC["lam"][0]:VEC["lam"][0] + 2],
                              vec[:, VEC["lam"][0] + 2:VEC["lam"][0] + 4], ALU.mult).then_inc(lam_ready, 1)
            dve.memset(gT[:, :, 0:2], 0.0)
            when_emptied(dve, ("lam",))
            link(dve.scalar_tensor_tensor(small[:, 4:5], small[:, 3:4], -LAMBDA_INIT, small[:, 2:3],
                                          ALU.add, ALU.subtract))
            dve.wait_ge(x_in, 32)
            big_norm("n1", "pre", normed_x, resid)

            def stats_a(u):
                h, i = UNITS_A[u]
                nk = (i + 1) * P
                st = small[:, 16 + 16 * (u % 3):32 + 16 * (u % 3)]
                key = ("S", u)
                when_filled(dve, key)
                for m in range(2):
                    ins = dve.scalar_tensor_tensor(probs[:, u % 3, m, 0:nk], C("dist", T - nk, T), -SLOPES[h] / SCALE_A,
                                                   pair(key)[:, m, 0:nk], ALU.mult, ALU.add)
                empties(ins, key)
                when_emptied(dve, key)
                link(dve.tensor_reduce(st[:, 0:2], probs[:, u % 3, :, 0:nk], AX_X, ALU.max))
                dve.tensor_scalar(st[:, 2:4], st[:, 0:2], -SCALE_A, None, ALU.mult).then_inc(stats_ready, 1)

            def combine_a(u):
                h, i = UNITS_A[u]
                nk = (i + 1) * P
                st = small[:, 16 + 16 * (u % 3):32 + 16 * (u % 3)]
                dve.wait_ge(exp_done, u + 1)
                if u >= 2:
                    when_filled(dve, ("T", u - 2))
                link(dve.reciprocal(st[:, 6:8], st[:, 4:6]))
                link(dve.tensor_scalar(weights_p[:, u % 2, 0:nk], probs[:, u % 3, 1, 0:nk], st[:, 7:8], small[:, 4:5],
                                       ALU.mult, ALU.mult))
                dve.scalar_tensor_tensor(weights_p[:, u % 2, 0:nk], probs[:, u % 3, 0, 0:nk], st[:, 6:7],
                                         weights_p[:, u % 2, 0:nk], ALU.mult, ALU.add).then_inc(probs_ready, 1)

            def conv_part(m):
                for a in (2 * m, 2 * m + 1):
                    dst = mixin[:, 4 + a, :]
                    link(dve.tensor_scalar(dst, gT[:, a, 0:T], V("conv", a), None, ALU.mult))
                    link(dve.scalar_tensor_tensor(dst, gT[:, a, 1:T + 1], V("conv", 4 + a), dst, ALU.mult, ALU.add))
                    link(dve.scalar_tensor_tensor(dst, gT[:, a, 2:T + 2], V("conv", 8 + a), dst, ALU.mult, ALU.add))

            side = [(g, m) for g in ("c", "u", "zc", "b", "za") for m in (0, 1)]
            stats_a(0)
            stats_a(1)
            for u in range(len(UNITS_A)):
                combine_a(u)
                if u + 2 < len(UNITS_A):
                    stats_a(u + 2)
                if side:
                    g, m = side.pop(0)
                    if g == "u":
                        when_filled(dve, (g, m))
                        when_emptied(dve, ("c", m))
                        empties(dve.tensor_tensor(gT[:, 2 * m:2 * m + 2, 2:T + 2], cT[:, 2 * m:2 * m + 2, :],
                                                  pair((g, m)), ALU.mult), (g, m))
                    if g == "zc":
                        when_emptied(dve, ("u", m))
                        conv_part(m)
                    if g == "b":
                        when_filled(dve, (g, m))
                        when_emptied(dve, ("zc", m))
                        sz = szT[:, 2 * m:2 * m + 2, :]
                        empties(dve.tensor_tensor(sz, sz, pair((g, m)), ALU.mult), (g, m))
                        when_emptied(dve, (g, m))
                        mx = mixin[:, 4 + 2 * m:6 + 2 * m, :]
                        dve.tensor_tensor(mx, mx, sz, ALU.mult)
            for n in range(2):
                r = inverse(f"sl{n}", 1024).rearrange("p (a b) -> p a b", a=2)
                mx = mixin[:, 2 * n:2 * n + 2, :]
                scale_by(mx, mx, V("subln"), r, True)
                dve.wait_ge(normed, NORM[f"sl{n}"] + 1)
                when_emptied(dve, ("za", n))
                dve.scalar_tensor_tensor(mx, mx, 1.0 - LAMBDA_INIT, zaT[:, 2 * n:2 * n + 2, :],
                                         ALU.mult, ALU.mult).then_inc(mixin_ready, 1)
            big_norm("post", "post", mixedT, mixedT)
            dve.tensor_tensor(xs, xs, mixedT, ALU.add).then_inc(x1_ready, 1)
            big_norm("ple", "ple", eT, eT)
            dve.wait_ge(x1_ready, 1)
            for m in range(4):
                when_emptied(dve, ("pg", m))
                sg = sgT[:, 2 * m:2 * m + 2, :]
                link(dve.tensor_tensor(sg, sg, eT[:, 2 * m:2 * m + 2, :], ALU.mult))
                when_filled(dve, ("pg", 3))
                x = resid[:, 2 * m:2 * m + 2, 0:T]
                ins = dve.tensor_tensor(x, x, sg, ALU.add)
            ins.then_inc(x2_ready, 1)

            dve.wait_ge(x2_ready, 1)
            big_norm("mix", "mix", normed_x, resid, TM)
            r = inverse("cq", T)
            for k in range(3):
                scale_by(cq[:, k, :], cq[:, k, :], V("qnorm", k), r, k == 2)
            r = inverse("ckv", TM)
            for k in range(2):
                scale_by(ckv[:, k, :], ckv[:, k, :], V("kvnorm", k), r, k == 1)
            scale_by(kp, kp, V("kp"), inverse("kpe", TM), True)

            def rope(key, dst, turned, cos, sin, tmp):
                when_filled(dve, key)
                empties(dve.tensor_tensor(tmp, turned, sin, ALU.mult), key)
                link(dve.tensor_tensor(dst, dst, cos, ALU.mult))
                when_emptied(dve, key)
                dve.tensor_tensor(dst, dst, tmp, ALU.add).then_inc(roped, 1)

            rope(("rot", "kpe"), kp, flat(("rot", "kpe"))[:, 0:TM], C("cos"), C("sin"), rot_tmp[:, 0:TM])
            for n, name in enumerate(PARTS):
                kind, m = name[0:2], int(name[2:])
                if kind == "kn":
                    scale_by(kn[:, m, :], kn[:, m, :], V("kn"), inverse(name, TM), True)
                else:
                    dst = (qn if kind == "qn" else qp)[:, 2 * m:2 * m + 2, :]
                    scale_by(dst, dst, V(kind), inverse(name, 1024).rearrange("p (a b) -> p a b", a=2), True)
                if n >= 2 and PARTS[n - 2][0:2] == "qp":
                    b = int(PARTS[n - 2][2:])
                    rope(("rot", b), qp[:, 2 * b:2 * b + 2, :], pair(("rot", b)),
                         C("cos", 0, T).unsqueeze(1).to_broadcast([P, 2, T]),
                         C("sin", 0, T).unsqueeze(1).to_broadcast([P, 2, T]),
                         rot_tmp[:, 0:1024].rearrange("p (a b) -> p a b", a=2))

            def stats_m(u):
                h, i = UNITS_M[u]
                nk = (i + 1) * P
                st = small[:, 64 + 8 * (u % 3):72 + 8 * (u % 3)]
                key = ("MS", u)
                when_filled(dve, key)
                link(dve.memset(flat(key)[0:CHUNK, nk - CHUNK:nk], NEG))
                link(dve.tensor_reduce(st[:, 0:1], flat(key)[:, 0:nk + META], AX_X, ALU.max))
                dve.tensor_scalar(st[:, 1:2], st[:, 0:1], -SCALE_M, None, ALU.mult).then_inc(neg_max, 1)

            stats_m(0)
            stats_m(1)
            for u, (h, i) in enumerate(UNITS_M):
                n = (i + 1) * P + META
                st = small[:, 64 + 8 * (u % 3):72 + 8 * (u % 3)]
                when_emptied(dve, ("MS", u))
                link(dve.reciprocal(st[:, 3:4], st[:, 2:3]))
                dve.tensor_scalar(mp[:, u % 3, 0:n], mp[:, u % 3, 0:n], st[:, 3:4], None, ALU.mult).then_inc(mprobs, 1)
                if u + 2 < len(UNITS_M):
                    stats_m(u + 2)

            bx = bc[:, 0:T]

            def level_difference(h, n):
                s = LEVELS[n - 1]
                b = bx.rearrange("p (b x) -> p b x", x=2 * s)
                mid = b[:, :, s - 1:s].to_broadcast([P, T // (2 * s), 2 * s])
                dve.tensor_tensor(wl[n % 2].rearrange("p (b x) -> p b x", x=2 * s), b, mid,
                                  ALU.subtract).then_inc(level_diff, 1)

            att = attT.rearrange("p (c t) -> p c t", c=TT)

            def mask(n):
                return C("levels", n * P, (n + 1) * P).unsqueeze(1).to_broadcast([P, TT, P])

            def choose(h, n):
                key = ("lev", h, n)
                when_filled(dve, key)
                src = flat(key)[:, 0:T].rearrange("p (c t) -> p c t", c=TT)
                if n == 0:
                    if h:
                        when_filled(dve, ("go", h - 1))
                    empties(dve.tensor_tensor(att, src, mask(0), ALU.mult), key)
                else:
                    when_emptied(dve, ("lev", h, n - 1))
                    empties(dve.copy_predicated(att, mask(n).bitcast(U32), src), key)

            when_emptied(dve, ("gk", HG - 1))
            for h in range(HG):
                dve.wait_ge(zbias, h + 1)
                link(dve.scalar_tensor_tensor(la, la, 0.0, bc, ALU.min, ALU.subtract))
                dve.tensor_tensor_scan(bc, C("reset"), la, 0.0, ALU.mult, ALU.add).then_inc(cumulated, 1)
                dve.wait_ge(cumulated, h + 1)
                if h:
                    dve.wait_ge(level_qk, 7 * h)
                level_difference(h, 1)
                level_difference(h, 2)
                choose(h, 0)
                dve.wait_ge(decays, h + 1)
                dve.tensor_tensor(qb, qb, gq[:, h, :], ALU.mult).then_inc(qb_ready, 1)
                for n in range(1, 8):
                    dve.wait_ge(level_exp, 7 * h + n)
                    if n > 2:
                        when_filled(dve, ("lev", h, n - 2))
                    elif h:
                        when_filled(dve, ("kd", h - 1))
                    dve.tensor_tensor(ql[n % 2], gq[:, h, :], wl[n % 2], ALU.mult)
                    dve.tensor_tensor(kl[n % 2][:, 0:T], gk[:, h, 0:T], wl[n % 2], ALU.mult).then_inc(level_qk, 1)
                    dve.wait_ge(level_qk, 7 * h + n)
                    if n < 6:
                        level_difference(h, n + 2)
                    if n > 1:
                        choose(h, n - 1)
                when_filled(dve, ("oa", h))
                when_emptied(dve, ("ta", h))
                empties(dve.tensor_tensor(mixT[:, 2 * h:2 * h + 2, :], gate_a[:, h % 2, :, :], pair(("oa", h)),
                                          ALU.mult), ("oa", h))
                when_filled(dve, ("lev", h, 6))
                b4 = bx.rearrange("p (c t) -> p c t", c=TT)
                dve.tensor_tensor(kl[0][:, 0:T].rearrange("p (c t) -> p c t", c=TT),
                                  b4[:, :, P - 1:P].to_broadcast([P, TT, P]), b4, ALU.subtract)
                dve.tensor_tensor(kl[0][:, T:TM], bc[:, TM - 1:TM].to_broadcast([P, META]), bc[:, T:TM],
                                  ALU.subtract).then_inc(kd_diff, 1)
                choose(h, 7)
                dve.wait_ge(kd_exp, h + 1)
                dve.tensor_tensor(kl[0], kl[0], gk[:, h, :], ALU.mult).then_inc(kd_ready, 1)
                if h:
                    when_filled(dve, ("go", h - 1))
                dve.wait_ge(decays, h + 1)
                for c in range(TT):
                    key = ("st", h, c)
                    when_filled(dve, key)
                    src = flat(key)[:, 0:HV]
                    if c == 0:
                        empties(dve.tensor_copy(state[:, 0, :], src), key)
                    else:
                        when_emptied(dve, ("st", h, c - 1))
                        empties(dve.scalar_tensor_tensor(state[:, c, :], state[:, c - 1, :], dec[:, c - 1:c], src,
                                                         ALU.mult, ALU.add), key)
            for h in range(HG):
                r = inverse(f"g{h}", T)
                for e in range(2):
                    scale_by(oT[:, 2 * h + e, :], oT[:, 2 * h + e, :], V("gnorm", e), r, e == 1)
            dve.wait_ge(normed, NORM[f"g{HG - 1}"] + 1)
            for h in range(HG):
                when_emptied(dve, ("gg", h))
                o = oT[:, 2 * h:2 * h + 2, :]
                dve.tensor_tensor(o, o, gate_s[:, h % 2, :, :], ALU.mult).then_inc(gated, 1)
            for m in range(4):
                when_filled(dve, ("ob", m))
                when_emptied(dve, ("tb", m))
                if m:
                    dve.wait_ge(mixed, m)
                empties(dve.tensor_tensor(mix_tmp, gate_s[:, m % 2, :, :], pair(("ob", m)), ALU.mult), ("ob", m))
                when_emptied(dve, ("ob", m))
                x = mixT[:, 2 * m:2 * m + 2, :]
                dve.tensor_tensor(x, x, mix_tmp, ALU.add).then_inc(mixed, 1)
            for m in range(4):
                when_filled(dve, ("w2", m))
                x = resid[:, 2 * m:2 * m + 2, 0:T]
                empties(dve.tensor_tensor(x, x, pair(("w2", m)), ALU.add), ("w2", m))
            when_emptied(dve, ("w2", 3))
            big_norm("ffn", "ffn", normed_x, resid)
            dve.wait_ge(h_rounded, 1)
            dve.tensor_tensor(h_hl[1], hs, h_hl[0], ALU.subtract).then_inc(h_split, 1)

            iota16 = C("iota", 0, TOPK)
            for t in range(TT):
                if t:
                    when_filled(dve, ("tr", t - 1))
                for half in range(2):
                    when_emptied(dve, ("ps", t, half))
                for src, vals, index, n in ((sc, topv, topi_u, 16), (cand, best, bpos_u, HP)):
                    if src is cand:
                        v4 = topv.rearrange("p (h a) k -> p h a k", a=2)
                        link(dve.tensor_tensor(cand.rearrange("p h (a b) -> p h a b", a=TOPK),
                                               v4[:, :, 0, :].unsqueeze(3).to_broadcast([P, HP, TOPK, TOPK]),
                                               v4[:, :, 1, :].unsqueeze(2).to_broadcast([P, HP, TOPK, TOPK]), ALU.add))
                    for part in (slice(0, 8), slice(8, 16)):
                        for f in range(n):
                            ins = dve.max(vals[:, f, part], src[:, f, :])
                        link(ins)
                        for f in range(n):
                            ins = dve.max_index(index[:, f, part], vals[:, f, part], src[:, f, :])
                        link(ins)
                        if part.start == 0:
                            for f in range(n):
                                ins = dve.match_replace(src[:, f, :], vals[:, f, part], src[:, f, :], -3.0e38)
                            link(ins)
                dve.tensor_tensor(ent[:, 2, :].rearrange("p (h k) -> p h k", h=HP), best,
                                  best[:, :, 0:1].to_broadcast([P, HP, TOPK]), ALU.subtract).then_inc(soft_diff, 1)
                pos = bpos_u.rearrange("p h k -> p (h k)")
                dve.tensor_scalar(bi_u, pos, 4, None, ALU.logical_shift_right)
                link(dve.tensor_scalar(bj_u, pos, 15, None, ALU.bitwise_and))
                dve.tensor_copy(bi, bi_u)
                dve.tensor_copy(bj, bj_u)
                link(dve.tensor_copy(topi, topi_u))
                i4 = topi.rearrange("p (h a) k -> p h a k", a=2)
                for a, b in ((0, bi), (1, bj)):
                    link(dve.tensor_tensor(onehot, b.unsqueeze(2).to_broadcast([P, ENTRIES, TOPK]),
                                           iota16.unsqueeze(1).to_broadcast([P, ENTRIES, TOPK]), ALU.is_equal))
                    link(dve.tensor_tensor(onehot2.rearrange("p (h k) n -> p h k n", h=HP),
                                           onehot.rearrange("p (h k) n -> p h k n", h=HP),
                                           i4[:, :, a, :].unsqueeze(2).to_broadcast([P, HP, TOPK, TOPK]), ALU.mult))
                    link(dve.tensor_reduce(ent[:, a, :], onehot2, AX_X, ALU.add))
                dve.wait_ge(soft_exp, t + 1)
                e3 = ent[:, 2, :].rearrange("p (h k) -> p h k", h=HP)
                link(dve.tensor_reduce(bsum, e3, AX_X, ALU.add))
                link(dve.reciprocal(bsum, bsum))
                dve.tensor_tensor(e3, e3, bsum.unsqueeze(2).to_broadcast([P, HP, TOPK]), ALU.mult).then_inc(entries, 1)
            when_emptied(dve, ("tr", TT - 1))

            def one_hots(step):
                for q in range(4):
                    at_least(dve, spread, 4 * step + q - 3)
                    for one, key, done in ((oneA, 0, hot_n1), (oneB, 1, hot_n2)):
                        dve.tensor_tensor(one[:, 4 * q:4 * q + 4, :],
                                          C("iota").unsqueeze(1).to_broadcast([P, 4, P]),
                                          entT[:, key, bass.ds(16 * step + 4 * q, 4)].unsqueeze(2)
                                          .to_broadcast([P, 4, P]), ALU.is_equal).then_inc(done, 1)

            def split_u(g, s):
                dve.wait_ge(u_rounded, g + 1)
                dve.tensor_tensor(u_hl[s][1], u_raw, u_hl[s][0], ALU.subtract).then_inc(u_split, 1)

            def split_v(g, s):
                dve.wait_ge(v_rounded, g + 1)
                dve.tensor_tensor(v_hl[s][1], v_raw, v_hl[s][0], ALU.subtract).then_inc(v_split, 1)

            split_u(0, 0)
            one_hots(0)
            with dve.Fori(1, T // 16) as step:
                one_hots(step)

            def coefs(g, s, turn):
                dve.wait_ge(g_in[s], 16 * turn)

                def multiply(j):
                    dve.wait_ge(gelu_done, EG * g + j + 1)
                    c = coef[:, j, :]
                    dve.tensor_tensor(c, c, gslot[s][:, j, :], ALU.mult).then_inc(coef_mult, 1)

                def split(j):
                    dve.wait_ge(coef_rounded, EG * g + j + 1)
                    dve.tensor_tensor(c_hl[s][1][:, j, :], coef[:, j, :], c_hl[s][0][:, j, :],
                                      ALU.subtract).then_inc(coef_done, 1)

                multiply(0)
                for j in range(1, EG):
                    multiply(j)
                    split(j - 1)
                split(EG - 1)

            def add(g):
                at_least(dve, added, KD * g)
                for m in range(KD):
                    dve.wait_ge(out_done, KD * g + m + 1)
                    x = resid[:, m, 0:T]
                    dve.tensor_tensor(x, x, ps[:, 4 + m % 4, :], ALU.add).then_inc(added, 1)

            def period(g, s, turn, last=0):
                if last < 2:
                    split_u(g + 2, s)
                if last < 3:
                    split_v(g + 1, 1 - s)
                    coefs(g + 1, 1 - s, turn)
                add(g)

            split_u(1, 1)
            split_v(0, 0)
            coefs(0, 0, 1)
            period(0, 0, 1)
            period(1, 1, 2)
            with dve.Fori(1, GROUPS // 2 - 1) as it:
                period(2 * it, 0, it + 1)
                period(2 * it + 1, 1, it + 2)
            period(GROUPS - 2, 0, GROUPS // 2, last=2)
            period(GROUPS - 1, 1, 0, last=3)

        @block.gpsimd
        def _(pool):
            def weigh(step):
                for q in range(4):
                    pool.wait_ge(hot_n1, 4 * step + q + 1)
                    one = oneA[:, 4 * q:4 * q + 4, :]
                    nc.gpsimd.tensor_tensor(one, one, entT[:, 2, bass.ds(16 * step + 4 * q, 4)].unsqueeze(2)
                                            .to_broadcast([P, 4, P]), ALU.mult).then_inc(hot, 1)

            when_emptied(pool, ("tr", TT - 1))
            weigh(0)
            with pool.Fori(1, T // 16) as step:
                weigh(step)


def at_least(eng, s, value):
    if not isinstance(value, int) or value > 0:
        eng.wait_ge(s, value)


def tables():
    c = np.zeros((P, NCONST), np.float32)

    def put(name, m):
        at, n = CONST[name]
        c[:, at:at + n] = m

    r = np.arange(P)
    put("ident", np.eye(P))
    put("ones", 1.0)
    put("heads64", (r[:, None] // 64 == r[None, :] // 64))
    rot = np.zeros((P, P), np.float32)
    for m in range(P):
        low = m % ROPE < ROPE // 2
        rot[m + 32 if low else m - 32, m] = -1.0 if low else 1.0
    put("rot", rot)
    put("iota", r[None, :])
    col = np.arange(T)
    at = T - P + r[:, None]
    seen = col[None, :] // CHUNK <= at // CHUNK
    put("dist", np.where(seen, np.abs(at - col[None, :]), 1e30))
    j, i = r[:, None], r[None, :]
    levels = [j == i]
    for s in LEVELS:
        levels.append((j // (2 * s) == i // (2 * s)) & (j % (2 * s) < s) & (i % (2 * s) >= s))
    put("levels", np.concatenate(levels, 1))
    reset = np.ones(TM)
    reset[0::P] = 0.0
    put("reset", reset[None, :])
    half = ROPE // 2
    inv = (np.float32(10000.0) ** (-np.arange(half, dtype=np.float32) / np.float32(half))).astype(np.float32)
    pos = np.concatenate([np.arange(META, TM), np.arange(META)]).astype(np.float32)
    ang = (inv[r % half][:, None] * pos[None, :]).astype(np.float32)
    put("cos", np.cos(ang))
    put("sin", np.sin(ang))
    return c


def kernel(**inputs):
    import concourse.bacc as _bacc
    from concourse.bass_utils import run_bass_kernel_spmd as _run

    x = {n: np.asarray(a) for n, a in inputs.items()}
    f = np.float32

    def cols(a):
        return np.asarray(a).reshape(-1, P).T

    def feature_major(a):
        return np.ascontiguousarray(a.T.reshape(-1, P, a.shape[0]).transpose(1, 0, 2))

    vecs = np.zeros((P, NVEC), f)

    def put(name, m):
        at, n = VEC[name]
        vecs[:m.shape[0], at:at + n] = m

    put("pre", cols(x["pre_norm_gain"][0]))
    put("mix", cols(x["norm_mix_2"][0]))
    put("subln", cols(x["subln_gain"][0]))
    put("conv", x["conv_w"][0].reshape(3, 4, P).transpose(2, 0, 1).reshape(P, 12))
    put("post", cols(x["post_norm_gain"][0]))
    put("ple", cols(x["ple_norm_gain"][0]))
    put("qnorm", cols(x["mla_q_norm_2"][0]))
    put("kvnorm", cols(x["mla_kv_norm_2"][0]))
    put("qn", cols(x["qn_nope_2"][0]))
    put("kn", cols(x["kn_nope_2"][0]))
    put("qp", np.concatenate([x["qn_pe_2"][0], x["qn_pe_2"][0]])[:, None])
    put("kp", np.concatenate([x["kn_pe_2"][0], x["kn_pe_2"][0]])[:, None])
    put("ba", cols(x["gla_b_a_2"][0]))
    put("gnorm", cols(x["gla_norm_2"][0]))
    put("ffn", cols(x["norm_ffn_2"][0]))
    put("lam", np.stack([x["lambda_q1"][0], x["lambda_q2"][0], x["lambda_k1"][0], x["lambda_k2"][0]], 1))
    put("eps", np.full((P, 1), EPS, f))
    put("subeps", np.full((P, 1), SUBLN_EPS, f))

    w1, w2 = x["w_in"][0], x["w_in_2"][0]
    part = {}
    for n, g in enumerate(("q", "k", "v", "za", "b", "c", "u", "zc")):
        part[g] = w1[:, n * 512:(n + 1) * 512]
    at = 0
    two = {}
    for g, n in (("cq", 384), ("ckv", 256), ("kpe", 64), ("gq", 512), ("gk", 512), ("gv", 1024), ("ga", 16),
                 ("gg", 1024), ("ta", 1024), ("tb", 1024)):
        two[g] = w2[:, at:at + n]
        at += n
    part["cq"] = two["cq"]
    part["ckv"] = np.concatenate([two["ckv"], two["kpe"], two["kpe"]], 1)
    for g in ("gq", "gk", "ga"):
        part[g] = two[g]
    uq = x["mla_w_uq_2"][0].reshape(384, HM, 192)
    part["uqn"] = uq[:, :, 0:128].reshape(384, 1024)
    part["uqp"] = uq[:, :, 128:192].reshape(384, 512)
    ukv = x["mla_w_ukv_2"][0].reshape(256, HM, 256)
    part["ukv"] = np.concatenate([ukv[:, :, 0:128].reshape(256, 1024), ukv[:, :, 128:256].reshape(256, 1024)], 1)
    part["ple"] = x["w_ple_proj"][0]
    for g, m in (("wo", x["w_out"][0]), ("pg", x["w_ple_gate"][0]), ("gv", two["gv"]), ("gg", two["gg"]),
                 ("ta", two["ta"]), ("tb", two["tb"]), ("oa", x["w_o_mla_2"][0]), ("ob", x["w_o_gla_2"][0]),
                 ("w2", x["w_out_2"][0]), ("pq", x["peer_w_q_2"][0])):
        for n in range(m.shape[1] // 512):
            part[f"{g}{n}"] = m[:, n * 512:(n + 1) * 512]
    weights = np.concatenate([part[n].reshape(k, P, c).transpose(1, 0, 2).reshape(P, k * c) for n, k, c in WEIGHTS], 1)

    u = x["peer_u_2"][0].reshape(P, GROUPS, EG, KD, P)
    v = x["peer_v_2"][0].reshape(P, GROUPS, EG, D)
    arrays = {
        "xT": feature_major(x["x"][0]), "metaT": feature_major(x["meta_2"]), "pT": feature_major(x["p"][0, 0]),
        "consts": tables(), "vecs": vecs, "weights": np.ascontiguousarray(weights),
        "wa2": x["gla_w_a2_2"][0], "keysT": np.ascontiguousarray(x["peer_keys_2"][0].transpose(2, 0, 1)),
        "uT": np.ascontiguousarray(u.transpose(1, 4, 3, 2, 0)).reshape(GROUPS, P, KD * EG * P),
        "vT": np.ascontiguousarray(v.transpose(1, 0, 2, 3)).reshape(GROUPS, P, EG * D),
    }
    nc = _bacc.Bacc("TRN2", target_bir_lowering=False, num_devices=1,
                    dynamic_dma_scratch_size=256)
    A, ins = {}, {}
    for name, a in arrays.items():
        ins[f"in_{name}_dram"] = np.ascontiguousarray(a)
        A[name] = nc.dram_tensor(f"in_{name}_dram", a.shape, F32, kind="ExternalInput").ap()
    A["gates"] = nc.dram_tensor("gate_table", (P, GROUPS, EG * T), F32, kind="Internal").ap()
    A["out"] = nc.dram_tensor("out_0_dram", (D, T), F32, kind="ExternalOutput").ap()
    build(nc, A)
    r = _run(nc, [ins], core_ids=[0])
    return np.ascontiguousarray(r.results[0]["out_0_dram"].T)[None]
```

```python
from contextlib import ExitStack

import numpy as np

import concourse.bass as bass
from concourse import mybir

F32 = mybir.dt.float32
BF16 = mybir.dt.bfloat16
F32R = mybir.dt.float32r
U32 = mybir.dt.uint32
ALU = mybir.AluOpType
ACT = mybir.ActivationFunctionType
AX_X = mybir.AxisListType.X

P = 128
D = 1024
KD = D // P
T = 512
TT = T // P
META = 16
TM = T + META
CHUNK = 64
NEG = -1e30

HA = 4
DQK = 64
SCALE_A = DQK ** -0.5
SLOPES = [2.0 ** (-8.0 * (h + 1) / HA) for h in range(HA)]
LAMBDA_INIT = 0.8 - 0.6
HM = 8
ROPE = 64
SCALE_M = (128 + ROPE) ** -0.5
HG = 4
HK = 128
HV = 256
TAU = 16.0
LEVELS = [64, 32, 16, 8, 4, 2, 1]
HP = 8
NKEYS = 128
TOPK = 16
EG = 4
GROUPS = NKEYS // EG
HALF = 64
PIECES = T // HALF
EARLY = 4
CA, CB = 4 * TOPK, 12 * 4
NCAND = CA + CB

EPS = 1e-6
SUBLN_EPS = 1e-5

CONST = {}
_at = 0
for _name, _n in (("ident", P), ("ones", P), ("heads64", P), ("rot", P), ("iota", P), ("dist", T),
                  ("levels", 8 * P), ("reset", TM), ("cos", TM), ("sin", TM)):
    CONST[_name] = (_at, _n)
    _at += _n
NCONST = _at

VEC = {}
_at = 0
for _name, _n in (("pre", 8), ("mix", 8), ("subln", 1), ("conv", 12), ("post", 8), ("ple", 8), ("qnorm", 3),
                  ("kvnorm", 2), ("qn", 1), ("kn", 1), ("qp", 1), ("kp", 1), ("ba", 4), ("gnorm", 2),
                  ("ffn", 8), ("lam", 4), ("eps", 1), ("subeps", 1)):
    VEC[_name] = (_at, _n)
    _at += _n
NVEC = _at

WEIGHTS = ([(f"{g}{m}", 8, 256, True) for g in ("q", "k", "v", "c", "u", "zc", "b", "za") for m in (0, 1)]
           + [(f"wo{m}", 8, 256, True) for m in range(4)] + [("ple", 2, 1024, False)]
           + [(f"pg{m}", 8, 256, True) for m in range(4)]
           + [("cq0", 8, 256, True), ("cq1", 8, 128, True), ("ckv0", 8, 128, True), ("ckv1", 8, 128, True),
              ("kpe0", 8, 128, True), ("uqn0", 3, 512, False), ("uqn1", 3, 512, False), ("uqp", 3, 512, False),
              ("ukv0", 2, 1024, False), ("ukv1", 2, 1024, False), ("gq0", 8, 256, True), ("gq1", 8, 256, True)]
           + [(f"gk{h}", 8, 128, True) for h in range(HG)] + [("ga0", 8, 16, True)]
           + [(f"gv{g}", 8, 256, True) for g in range(4)]
           + [(f"{g}{m}", 8, 256, g == "ta") for m in range(4) for g in ("ta", "oa")]
           + [(f"gg{m}", 8, 256, True) for m in range(4)]
           + [(f"{g}{m}", 8, 256, True) for m in range(4) for g in ("tb", "ob")]
           + [(f"w2{m}", 8, 256, True) for m in range(4)] + [(f"pq{m}", 8, 256, True) for m in range(HP)])
WSLOT = 2048
NW = 4
NU = 2
WN = {w[0]: n for n, w in enumerate(WEIGHTS)}
WAT = {}
_at = 0
for _name, _k, _n, _ in WEIGHTS:
    WAT[_name] = _at
    _at += _k * _n
SPLIT = [w[0] for w in WEIGHTS if w[3]]

UNITS_A = [(h, i) for h in range(HA) for i in range(TT)]
UNITS_M = [(h, i) for h in range(HM) for i in range(TT)]


PARTS = [f"qn{m}" for m in range(4)] + [f"qp{m}" for m in range(2)] + [f"kn{h}" for h in range(HM)]

SIDE_M = {4 * n + 2: key for n, key in enumerate([("gq", 0), ("gq", 1)] + [("gk", h) for h in range(HG)] + [("ga", 0)])}


def psum_jobs():
    jobs = [("lam",), ("ss", "n1")]
    for g in ("q", "k", "v"):
        jobs += [(g, 0), (g, 1)]
    side = [(g, m) for g in ("c", "u", "zc", "b", "za") for m in (0, 1)]
    jobs += [("S", 0), ("S", 1)]
    for u in range(len(UNITS_A)):
        jobs.append(("T", u))
        if u + 2 < len(UNITS_A):
            jobs.append(("S", u + 2))
        if side:
            jobs.append(side.pop(0))
        if u:
            jobs.append(("O", u - 1))
    jobs.append(("O", len(UNITS_A) - 1))
    jobs += [("ss", "sl0"), ("ss", "sl1")]
    jobs += [("wo", m) for m in range(4)] + [("ple", 0), ("ss", "post")] + [("ple", m) for m in (1, 2, 3)]
    jobs.append(("ss", "ple"))
    jobs += [("pg", m) for m in range(4)]
    jobs.append(("ss", "mix"))
    jobs += [("cq", 0), ("cq", 1), ("ckv", 0), ("ckv", 1), ("kpe", 0)]
    jobs += [("ss", "cq"), ("ss", "ckv"), ("ss", "kpe"), ("rot", "kpe")]
    for n, name in enumerate(PARTS):
        jobs.append(({"qn": "uqn", "qp": "uqp", "kn": "kn"}[name[0:2]], int(name[2:])))
        if n >= 1:
            jobs.append(("ss", PARTS[n - 1]))
        if n >= 3 and PARTS[n - 3][0:2] == "qp":
            jobs.append(("rot", int(PARTS[n - 3][2:])))
    jobs.append(("ss", PARTS[-1]))
    jobs += [("mv", t) for t in range(TT + 1)]
    jobs += [("MS", 0), ("MS", 1)]
    for u in range(len(UNITS_M)):
        jobs.append(("MT", u))
        if u + 2 < len(UNITS_M):
            jobs.append(("MS", u + 2))
        if u in SIDE_M:
            jobs.append(SIDE_M[u])
        if u:
            jobs.append(("MO", u - 1))
    jobs.append(("MO", len(UNITS_M) - 1))
    jobs.append(("z", 0))
    jobs += [("gv", g, m) for g in range(4) for m in (0, 1)]
    for h in range(HG):
        jobs += [("lev", h, 0), ("ta", h)] + [("lev", h, n) for n in (1, 2, 3)]
        if h + 1 < HG:
            jobs.append(("z", h + 1))
        jobs += [("lev", h, 4), ("lev", h, 5), ("oa", h), ("lev", h, 6), ("lev", h, 7), ("kd", h)]
        jobs += [("st", h, c) for c in range(TT)] + [("go", h)]
    jobs.append(("gg", 0))
    jobs += [("ss", f"g{h}") for h in range(HG)]
    jobs += [("gg", h) for h in range(1, HG)]
    for m in range(4):
        jobs += [("tb", m), ("ob", m)]
    jobs += [("w2", m) for m in range(4)]
    jobs.append(("ss", "ffn"))
    jobs += [("pq", 0)]
    for h in range(HP):
        if h + 1 < HP:
            jobs.append(("pq", h + 1))
        jobs.append(("ps", h))
    jobs += [("pre", g, half) for g in range(EARLY) for half in (0, 1)]
    jobs += [("tr", t) for t in range(TT)]
    return {key: n for n, key in enumerate(jobs)}


JOB = psum_jobs()
NPAIR = 4



def last_job(name):
    special = {"ple": ("ple", 3), "uqn0": ("uqn", 1), "uqn1": ("uqn", 3), "uqp": ("uqp", 1), "ukv0": ("kn", HM - 1),
               "ukv1": ("mv", TT)}
    if name in special:
        return special[name]
    return (name[:-1], int(name[-1]), 1) if name[:-1] == "gv" else (name[:-1], int(name[-1]))


NORMS = ([("n1", D, True), ("sl0", 128, False), ("sl1", 128, False), ("post", D, True), ("ple", D, True),
          ("mix", D, True), ("cq", 384, True), ("ckv", 256, False), ("kpe", 64, False)]
         + [(f"qn{m}", 128, False) for m in range(4)] + [(f"qp{m}", 64, False) for m in range(2)]
         + [(f"kn{h}", 128, False) for h in range(HM)] + [(f"g{h}", 256, False) for h in range(HG)]
         + [("ffn", D, True)])
NORM = {n[0]: k for k, n in enumerate(NORMS)}



def squared_count(name):
    return sum(n[1] != D for n in NORMS[:NORM[name] + 1])


BIG = [n[0] for n in NORMS if n[1] == D]


def build(nc, A):
    ctx = ExitStack()
    with ctx:
        def sb(name, shape, dt=F32):
            return ctx.enter_context(nc.sbuf_tensor(name, shape, dt))

        def sem(name):
            return ctx.enter_context(nc.semaphore(name))

        def both(name, shape):
            with nc.sbuf_tensor(name, shape, F32) as wide:
                pass
            return wide, sb(name + "_parts", shape, F32R)

        wring, wparts = both("wring", [P, (NW + NU) * WSLOT])
        cst = sb("cst", [P, NCONST])
        vec = sb("vec", [P, NVEC])
        resid, h_upper = both("resid", [P, KD, TM])
        normed_x, h_lower = both("normed_x", [P, KD, TM])
        sqbuf = sb("sqbuf", [P, KD * TM])
        rt = sb("rt", [P, 2, 1056])
        small = sb("small", [P, 320])
        AREA = 25600
        area, area_parts = both("area", [P, AREA])
        ps = ctx.enter_context(nc.psum_tensor("ps", [P, 8, 512], F32))

        def C(name, a=0, b=None):
            at, n = CONST[name]
            return cst[:, at + a:at + (n if b is None else b)]

        def V(name, i=0):
            at, _ = VEC[name]
            return vec[:, at + i:at + i + 1]

        def view(start, *dims):
            n = int(np.prod(dims))
            assert start + n <= AREA, (start, dims)
            flat = area[:, start:start + n]
            if len(dims) == 1:
                return flat
            if len(dims) == 2:
                return flat.rearrange("p (a b) -> p a b", a=dims[0])
            return flat.rearrange("p (a b c) -> p a b c", a=dims[0], b=dims[1])

        def blocks(start, width=T):
            return area_parts[:, start:start + KD * width].rearrange("p (k t) -> p k t", k=KD)

        xs = resid[:, :, 0:T]
        hs = normed_x[:, :, 0:T]
        small_sq = [sqbuf[:, 0:1056], sqbuf[:, 1056:2112]]
        sq_hi = sqbuf[:, 2112:4224]

        qT = view(0, 4, T)
        kT = view(2048, 4, T)
        v_tok = view(4096, TT, 512)
        zaT = view(6144, 4, T)
        gT = view(8192, 4, T + 2)
        szT = view(10248, 4, T)
        mixin = view(12296, KD, T)
        MIXIN_PARTS = (h_lower[:, :, 0:T], blocks(12296))
        X1_PARTS = (h_lower[:, :, 0:T], blocks(12296))
        O_PARTS = (blocks(16384), blocks(9280))
        MIX_PARTS = (blocks(20480), blocks(0))
        Q_PARTS = (blocks(16384), blocks(20480))
        probs = view(21512, 6, 512).rearrange("p (s m) k -> p s m k", s=3)
        weights_p = view(18440, 2, 512)
        pT_sb = view(19464, 2, 512)
        pin = view(20488, 2, T)
        cT = sqbuf[:, 2112:4160].rearrange("p (a b) -> p a b", a=4)
        mixedT = view(0, KD, T)
        eT = view(4096, KD, T)
        sgT = view(8192, KD, T)
        qn = view(0, HM, T)
        qp = view(4096, 4, T)
        kn = view(6144, HM, TM)
        mv = view(10368, TT, 1024)
        mvm = view(14464, 1024)
        ya = view(15488, HM, T)
        cq = view(15488, 3, T)
        ckv = view(17024, 2, TM)
        mpt = view(19584, 2, 640)
        mp = sq_hi[:, 0:3 * TM].rearrange("p (a b) -> p a b", a=3)
        kp = sq_hi[:, 3 * TM:4 * TM]
        rot_tmp = view(19584, 1056)
        gq = sqbuf[:, 0:HG * T].rearrange("p (a b) -> p a b", a=HG)
        gk = view(21376, HG, TM)
        gv = view(4160, TT, 1024)
        gvm = view(8256, 1024)
        oT = view(9280, KD, T)
        la = view(13376, TM)
        bc = [view(13904, TM), view(25040, TM)]
        dec = view(14432, 8)
        gaT = view(23488, TM)
        wl = [view(24528, T), sqbuf[:, 2112:2112 + T]]
        ql = [view(14448, T), sqbuf[:, 2640:2640 + T]]
        kl = [sqbuf[:, 3152:3152 + TM], view(24016, T)]
        attT = sqbuf[:, 3680:3680 + T]
        state = view(19584, TT, HV)
        kdt = view(20608, TT + 1, P)
        qb = view(14976, T)
        mixT = view(0, KD, T)
        mix_tmp = view(24576, 2, T)
        gate_a = rt[:, :, 0:1024].rearrange("p s (a b) -> p s a b", a=2)
        gate_s = sq_hi[:, 0:2048].rearrange("p (s a b) -> p s a b", s=2, a=2)
        pq = view(0, 4, T)
        sc = view(2048, HP, 2 * TT, P)
        at = 10240
        cand = view(at, TT, NCAND)
        hot_places = [view(at + 448, TT * TOPK, TOPK), view(at + 1472, TT * TOPK, TOPK)]
        topv = view(at + 2496, 2 * TT, TOPK)
        topi = view(at + 2624, 2 * TT, TOPK)
        topi_u = view(at + 2752, 2 * TT, TOPK).bitcast(U32)
        best = view(at + 2880, TT, TOPK)
        bpos_u = view(at + 2944, TT, TOPK).bitcast(U32)
        parts_u = view(at + 3008, 4, TT * TOPK).bitcast(U32)
        parts_f = view(at + 3264, 4, TT * TOPK)
        low_rows = view(at + 3520, TT * TOPK)
        turn_ij = view(at + 3584, 2, TT * TOPK)
        ent = view(at + 3712, TT, 3, P)
        bsum = view(at + 5248, TT, HP)
        entT = rt[:, :, :].rearrange("p a b -> p (a b)")[:, 0:3 * T].rearrange("p (a b) -> p a b", a=3)
        ones_at = normed_x[:, :, :].rearrange("p k t -> p (k t)")
        oneA = ones_at[:, 0:16 * P].rearrange("p (a b) -> p a b", a=16)
        oneB = ones_at[:, 16 * P:32 * P].rearrange("p (a b) -> p a b", a=16)
        stage = view(0, 2, 8192)
        early = view(16384, EARLY, EG, T)

        def halves(ap, *dims):
            flat2 = ap.bitcast(BF16).rearrange("p (z n) -> p z n", z=2)
            return [flat2[:, z, :].rearrange("p (a b) -> p a b", a=dims[0]) for z in range(2)]

        h_hl = halves(sqbuf[:, 0:KD * T], KD)
        u_raw = wring[:, 4096:8192].rearrange("p (k n) -> p k n", k=KD)
        v_raw = wring[:, 0:4096].rearrange("p (j d) -> p j d", j=EG)
        early_u_hl = [halves(wring[:, 8192:12288], KD), halves(wring[:, 0:4096], KD)]
        u_hl = [early_u_hl[0], halves(view(12288, 4096), KD)]
        v_hl = [halves(view(4096, 4096), EG), halves(view(8192, 4096), EG)]
        gslot = [view(0, PIECES, EG, HALF), view(2048, PIECES, EG, HALF)]
        coef = early[:, 0]
        c_hl = [halves(ones_at[:, 2048 * i:2048 * i + 2048], EG) for i in range(2)]

        wa2_sb = C("dist")[0:16, :]
        keys_sb = sb("keys_sb", [P, 2, P])

        consts_in = sem("consts_in")
        first_consts = sem("first_consts")
        x_first = [sem(f"x_first{m}") for m in range(4)]
        x_in = sem("x_in")
        p_in = sem("p_in")
        keys_in = sem("keys_in")
        w_in = [sem(f"w_in{i}") for i in range(NW)]
        filled = [sem(f"filled{i}") for i in range(NPAIR)]
        emptied = [sem(f"emptied{i}") for i in range(NPAIR)]
        weights_split = sem("weights_split")
        part_rounded = sem("part_rounded")
        norm_part = sem("norm_part")
        h_rounded_k = sem("h_rounded_k")
        h_ready = sem("h_ready")
        pair_made = sem("pair_made")
        pair_rounded = sem("pair_rounded")
        pair_split = sem("pair_split")
        x2_stored = sem("x2_stored")
        x2_in = sem("x2_in")
        squared = sem("squared")
        squares = sem("squares")
        rooted = sem("rooted")
        normed = sem("normed")
        dve_step = sem("dve_step")
        act_step = sem("act_step")
        lam_ready = sem("lam_ready")
        stats_ready = sem("stats_ready")
        exp_done = sem("exp_done")
        probs_ready = sem("probs_ready")
        x2_ready = sem("x2_ready")
        roped = sem("roped")
        neg_max = sem("neg_max")
        mprobs = sem("mprobs")
        zbias = sem("zbias")
        cumulated = sem("cumulated")
        level_diff = sem("level_diff")
        level_exp = sem("level_exp")
        level_qk = sem("level_qk")
        kd_diff = sem("kd_diff")
        kd_exp = sem("kd_exp")
        kd_ready = sem("kd_ready")
        decays = sem("decays")
        qb_ready = sem("qb_ready")
        soft_diff = sem("soft_diff")
        soft_exp = sem("soft_exp")
        entries = sem("entries")
        hot = sem("hot")
        spread = sem("spread")
        copied = sem("copied")
        stored = [sem(f"stored{i}") for i in range(2)]
        half_stored = sem("half_stored")
        places_hot = sem("places_hot")
        places_weighed = sem("places_weighed")
        hot_n1 = sem("hot_n1")
        hot_n2 = sem("hot_n2")
        h_rounded = sem("h_rounded")
        h_split = sem("h_split")
        chosen = sem("chosen")
        first_stored = [sem(f"first_stored{i}") for i in range(2)]
        u_in = sem("u_in")
        u_rounded = sem("u_rounded")
        u_split = sem("u_split")
        v_in = sem("v_in")
        v_rounded = sem("v_rounded")
        v_split = sem("v_split")
        coef_mult = sem("coef_mult")
        coef_rounded = sem("coef_rounded")
        g_in = [sem(f"g_in{i}") for i in range(2)]
        pre_done = sem("pre_done")
        gelu_done = sem("gelu_done")
        coef_done = sem("coef_done")
        out_done = sem("out_done")
        added = sem("added")
        out_stored = sem("out_stored")

        def pair(key):
            n = JOB[key] % NPAIR
            return ps[:, 2 * n:2 * n + 2, :]

        def flat(key):
            return pair(key).rearrange("p a b -> p (a b)")

        def when_filled(eng, key):
            eng.wait_ge(filled[JOB[key] % NPAIR], JOB[key] // NPAIR + 1)

        def when_emptied(eng, key):
            eng.wait_ge(emptied[JOB[key] % NPAIR], JOB[key] // NPAIR + 1)

        def fills(ins, key):
            ins.then_inc(filled[JOB[key] % NPAIR], 1)

        def empties(ins, key):
            ins.then_inc(emptied[JOB[key] % NPAIR], 1)

        def slot(ring, index, name):
            _, k, n, _ = WEIGHTS[WN[name]]
            return ring[:, index * WSLOT:index * WSLOT + k * n].rearrange("p (k n) -> p k n", k=k)

        def W(name):
            return slot(wring, WN[name] % NW, name)

        def W_parts(name):
            return slot(wparts, NW + SPLIT.index(name) % NU, name), slot(wparts, WN[name] % NW, name)

        def part_job(name):
            return {"qn": "uqn", "qp": "uqp", "kn": "kn"}[name[0:2]], int(name[2:])

        def norm_sq(name):
            k = NORM[name]
            return sqbuf if NORMS[k][2] else small_sq[k % 2]

        block = ctx.enter_context(nc.Block())

        @block.sync
        def _(sp):
            for m in range(4):
                sp.dma_start(resid[:, 2 * m:2 * m + 2, 0:T], A["xT"][:, 2 * m:2 * m + 2, :]).then_inc(x_first[m], 16)
                if m == 1:
                    sp.dma_start(vec[:, :], A["vecs"]).then_inc(first_consts, 16)
                    sp.dma_start(cst[:, 0:2 * P], A["consts"][:, 0:2 * P]).then_inc(first_consts, 16)
            for g, (name, k, n, _) in enumerate(WEIGHTS):
                before = WEIGHTS[g - NW][0] if g >= NW else None
                if before == "pg3":
                    for m in range(4):
                        sp.wait_ge(x2_ready, m + 1)
                        sp.dma_start(A["x2"][:, 2 * m:2 * m + 2, :], resid[:, 2 * m:2 * m + 2, 0:T]
                                     ).then_inc(x2_stored, 16)
                if before:
                    when_filled(sp, last_job(before))
                at = (g % NW) * WSLOT
                sp.dma_start(wring[:, at:at + k * n],
                             A["weights"][:, WAT[name]:WAT[name] + k * n]).then_inc(w_in[g % NW], 16)
                if g == 1:
                    sp.dma_start(resid[:, :, T:TM], A["metaT"]).then_inc(consts_in, 16)
                if g == NW - 1:
                    sp.dma_start(cst[:, 2 * P:NCONST], A["consts"][:, 2 * P:NCONST]).then_inc(consts_in, 16)
                if g == 2 * NW:
                    sp.dma_start(pin, A["pT"]).then_inc(p_in, 16)
                    sp.dma_start(keys_sb[:, :, :], A["keysT"]).then_inc(keys_in, 16)
                if before == "za1":
                    sp.dma_start(xs, A["xT"]).then_inc(x_in, 16)
                if before == "tb3":
                    sp.wait_ge(x2_stored, 64)
                    sp.dma_start(xs, A["x2"]).then_inc(x2_in, 16)
                if name == "pg3":
                    when_emptied(sp, ("S", len(UNITS_A) - 1))
                    sp.dma_start(wa2_sb, A["wa2"]).then_inc(keys_in, 16)

            def load_u(g):
                at_least(sp, u_split, g)
                sp.dma_start(wring[:, 4096:8192], A["uT"][bass.ds(g, 1), :, :].rearrange("g p n -> p (g n)")
                             ).then_inc(u_in, 16)

            def load_v(g):
                at_least(sp, v_split, g)
                sp.dma_start(wring[:, 0:4096], A["vT"][bass.ds(g, 1), :, :].rearrange("g p n -> p (g n)")
                             ).then_inc(v_in, 16)

            def load_gates(g, s):
                at_least(sp, coef_mult, EG * g - EG)
                sp.dma_start(gslot[s].rearrange("p n j t -> p n (j t)"),
                             A["gates"][:, :, bass.ds(g, 1), :].rearrange("p n g x -> p (n g) x")).then_inc(g_in[s], 16)

            for name, _, _, _ in WEIGHTS[-NW:]:
                if WN[name] % NW >= 2:
                    when_filled(sp, last_job(name))
            for g in range(EARLY + 1):
                load_u(g)
            when_filled(sp, ("pre", EARLY - 1, 1))
            load_v(0)
            load_u(EARLY + 1)
            for n in range(PIECES):
                sp.wait_ge(copied, (n + 1) * (HALF // 4))
                piece = stage[:, n % 2, :].rearrange("p (g x) -> p g x", g=GROUPS)
                sp.dma_start(A["gates"][:, n, 0:2, :], piece[:, 0:2, :]).then_inc(first_stored[n % 2], 16)
                if n < PIECES - 1:
                    sp.dma_start(A["gates"][:, n, 2:GROUPS, :], piece[:, 2:GROUPS, :]).then_inc(stored[n % 2], 16)
            for i in range(2):
                sp.wait_ge(first_stored[i], 8 * PIECES)
            sp.wait_ge(stored[0], 8 * PIECES)
            load_gates(0, 0)
            half = GROUPS // 2
            sp.dma_start(A["gates"][:, PIECES - 1, 2:half, :], piece[:, 2:half, :]).then_inc(half_stored, 16)
            load_gates(1, 1)
            load_v(1)
            sp.dma_start(A["gates"][:, PIECES - 1, half:GROUPS, :], piece[:, half:GROUPS, :]).then_inc(stored[1], 16)
            sp.wait_ge(half_stored, 16)
            sp.wait_ge(stored[1], 8 * PIECES)

            def ahead(g, s, last=0):
                if last < 2:
                    load_u(g + 2)
                if last < 3:
                    load_v(g + 1)
                if last < 2:
                    load_gates(g + 2, s)

            load_gates(2, 0)
            for g in range(1, EARLY):
                load_v(g + 1)
                load_gates(g + 2, g % 2)
            with sp.Fori(EARLY // 2, GROUPS // 2 - 1) as it:
                ahead(2 * it, 0)
                ahead(2 * it + 1, 1)
            ahead(GROUPS - 2, 0, last=2)
            for k in range(KD):
                sp.wait_ge(added, KD * (GROUPS - 1) + k + 1)
                sp.dma_start(A["out"][k * P:(k + 1) * P, :], resid[:, k, 0:T]).then_inc(out_stored, 16)
            sp.wait_ge(out_stored, 16 * KD)

        @block.tensor
        def _(pe):
            def claim(key):
                if JOB[key] >= NPAIR:
                    n = JOB[key] - NPAIR
                    pe.wait_ge(emptied[n % NPAIR], n // NPAIR + 1)

            def arrived(name):
                g = WN[name]
                pe.wait_ge(w_in[g % NW], 16 * (g // NW + 1))

            def project(key, name, tiles, src, k_tiles, width=T):
                claim(key)
                arrived(name)
                out = flat(key)
                w = W(name)
                for a, m in enumerate(tiles):
                    for at, n in ((0, T), (T, META)) if width == TM else ((0, T),):
                        for k in range(k_tiles):
                            mm = pe.matmul(out[:, a * 512 + at:a * 512 + at + n], w[:, k, m * P:(m + 1) * P],
                                           src[:, k, at:at + n], start=(k == 0), stop=(k == k_tiles - 1))
                fills(mm, key)

            def split_arrived(name):
                pe.wait_ge(weights_split, SPLIT.index(name) + 1)
                return W_parts(name)

            def three(out, a_parts, b_parts, first, last):
                (a_up, a_low), (b_up, b_low) = a_parts, b_parts
                pe.matmul(out, a_up, b_up, start=first, stop=False)
                pe.matmul(out, a_up, b_low, start=False, stop=False)
                return pe.matmul(out, a_low, b_up, start=False, stop=last)

            def h_parts(k, a, n):
                return h_upper[:, k, a:a + n], h_lower[:, k, a:a + n]

            def project_h(key, width=T, rows=P, ready=None):
                name = f"{key[0]}{key[1]}"
                claim(key)
                up, low = split_arrived(name)
                out = flat(key)
                tiles = max(1, WEIGHTS[WN[name]][2] // P)
                for m in range(tiles):
                    for at, n in ((0, T), (T, META)) if width == TM else ((0, T),):
                        for k in range(KD):
                            if ready is not None and m == 0 and at == 0:
                                pe.wait_ge(h_ready, ready + k + 1)
                            d = slice(m * P, m * P + rows)
                            mm = three(out[0:rows, m * 512 + at:m * 512 + at + n], (up[:, k, d], low[:, k, d]),
                                       h_parts(k, at, n), k == 0, k == KD - 1)
                fills(mm, key)

            def project_parts(key, parts, turn, order=range(KD)):
                claim(key)
                up, low = split_arrived(f"{key[0]}{key[1]}")
                for m in range(2):
                    d = slice(m * P, (m + 1) * P)
                    for n, k in enumerate(order):
                        if key[1] == 0 and m == 0 and n % 2 == 0:
                            pe.wait_ge(pair_split, 4 * turn + n // 2 + 1)
                        mm = three(pair(key)[:, m, :], (up[:, k, d], low[:, k, d]),
                                   (parts[0][:, k, :], parts[1][:, k, :]), n == 0, n == KD - 1)
                fills(mm, key)

            def tokens_h(key, tiles):
                name = f"{key[0]}{key[1]}"
                claim(key)
                up, low = split_arrived(name)
                for a, t in enumerate(tiles):
                    n = P if t < TT else META
                    for k in range(KD):
                        mm = three(flat(key)[0:n, a * 256:a * 256 + 256], h_parts(k, t * P, n),
                                   (up[:, k, :], low[:, k, :]), k == 0, k == KD - 1)
                fills(mm, key)

            def tokens(key, name, tiles, src, k_tiles, col0, width):
                claim(key)
                arrived(name)
                out = flat(key)
                w = W(name)
                at = 0
                for t in tiles:
                    n = P if t < TT else META
                    for c in range(0, width, 512):
                        for k in range(k_tiles):
                            mm = pe.matmul(out[0:n, at:at + 512], src[:, k, t * P:t * P + n],
                                           w[:, k, col0 + c:col0 + c + 512], start=(k == 0), stop=(k == k_tiles - 1))
                        at += 512
                fills(mm, key)

            def sums(name, ones, groups, width=T):
                key = ("ss", name)
                claim(key)
                pe.wait_ge(squared, squared_count(name))
                sq = norm_sq(name)
                out = flat(key)
                for a, starts in enumerate(groups):
                    for n, c in enumerate(starts):
                        mm = pe.matmul(out[:, a * 512:a * 512 + T], ones, sq[:, c:c + T],
                                       start=(n == 0), stop=(n == len(starts) - 1))
                    if width == TM:
                        for n, c in enumerate(starts):
                            mm = pe.matmul(out[:, T:TM], ones, sq[:, c + T:c + TM],
                                           start=(n == 0), stop=(n == len(starts) - 1))
                fills(mm, key)

            def big_sums(name, width=T):
                key = ("ss", name)
                claim(key)
                sq = norm_sq(name)[:, 0:KD * width].rearrange("p (k t) -> p k t", k=KD)
                for m in range(4):
                    pe.wait_ge(squares, 4 * BIG.index(name) + m + 1)
                    for k in (2 * m, 2 * m + 1):
                        for at, n in ((0, T), (T, META)) if width == TM else ((0, T),):
                            mm = pe.matmul(flat(key)[:, at:at + n], ones, sq[:, k, at:at + n],
                                           start=(k == 0), stop=(k == KD - 1))
                fills(mm, key)

            ident, ones, heads64 = C("ident"), C("ones"), C("heads64")

            pe.wait_ge(first_consts, 32)
            pe.wait_ge(lam_ready, 1)
            claim(("lam",))
            fills(pe.matmul(flat(("lam",))[:, 0:2], ones, small[:, 0:2], start=True, stop=True), ("lam",))
            big_sums("n1")
            for g in ("q", "k"):
                for m in (0, 1):
                    project_h((g, m), ready=0 if (g, m) == ("q", 0) else None)
            for m in (0, 1):
                tokens_h(("v", m), range(TT))

            def scores_a(u):
                h, i = UNITS_A[u]
                key = ("S", u)
                claim(key)
                if u == 0:
                    when_emptied(pe, ("k", 1))
                for m in range(2):
                    mm = pe.matmul(pair(key)[:, m, 0:(i + 1) * P], qT[64 * m:64 * m + 64, h, i * P:(i + 1) * P],
                                   kT[64 * m:64 * m + 64, h, 0:(i + 1) * P], start=True, stop=True)
                fills(mm, key)

            def outputs_a(u):
                h, i = UNITS_A[u]
                claim(("O", u))
                when_emptied(pe, ("T", u))
                for b in range(i + 1):
                    mm = pe.matmul(flat(("O", u))[:, 0:P], v_tok[:, b, h * P:(h + 1) * P],
                                   pT_sb[:, u % 2, b * P:(b + 1) * P], start=(b == 0), stop=(b == i))
                fills(mm, ("O", u))

            side = [(g, m) for g in ("c", "u", "zc", "b", "za") for m in (0, 1)]
            scores_a(0)
            scores_a(1)
            for u, (h, i) in enumerate(UNITS_A):
                claim(("T", u))
                pe.wait_ge(probs_ready, u + 1)
                for b in range(i + 1):
                    mm = pe.transpose(flat(("T", u))[:, b * P:(b + 1) * P], weights_p[:, u % 2, b * P:(b + 1) * P], ident)
                fills(mm, ("T", u))
                if u + 2 < len(UNITS_A):
                    scores_a(u + 2)
                if side:
                    g, m = side.pop(0)
                    project_h((g, m))
                if u:
                    outputs_a(u - 1)
            outputs_a(len(UNITS_A) - 1)
            for n in range(2):
                sums(f"sl{n}", ones, [[0], [T]])
            for m in range(4):
                project_parts(("wo", m), MIXIN_PARTS, 0, (4, 5, 6, 7, 0, 1, 2, 3))
            pe.wait_ge(p_in, 16)
            for m in range(4):
                project(("ple", m), "ple", (2 * m, 2 * m + 1), pin, 2)
                if m == 0:
                    big_sums("post")
            big_sums("ple")
            for m in range(4):
                project_parts(("pg", m), X1_PARTS, 1)

            big_sums("mix", TM)
            project_h(("cq", 0), ready=KD)
            project_h(("cq", 1))
            project_h(("ckv", 0), TM)
            project_h(("ckv", 1), TM)
            project_h(("kpe", 0), TM)
            sums("cq", ones, [[0, T, 2 * T]])
            sums("ckv", ones, [[0, TM]], TM)
            sums("kpe", heads64, [[0]], TM)
            claim(("rot", "kpe"))
            pe.wait_ge(normed, NORM["kpe"] + 1)
            pe.matmul(flat(("rot", "kpe"))[:, 0:T], C("rot"), kp[:, 0:T], start=True, stop=True)
            fills(pe.matmul(flat(("rot", "kpe"))[:, T:TM], C("rot"), kp[:, T:TM], start=True, stop=True), ("rot", "kpe"))
            def project_part(name):
                kind, m = name[0:2], int(name[2:])
                if kind == "qn":
                    if m == 0:
                        pe.wait_ge(normed, NORM["cq"] + 1)
                    project(("uqn", m), f"uqn{m // 2}", (2 * (m % 2), 2 * (m % 2) + 1), cq, 3)
                elif kind == "qp":
                    project(("uqp", m), "uqp", (2 * m, 2 * m + 1), cq, 3)
                else:
                    if m == 0:
                        pe.wait_ge(normed, NORM["ckv"] + 1)
                    project(("kn", m), "ukv0", (m,), ckv, 2, TM)

            def sum_part(name):
                kind = name[0:2]
                if kind == "qn":
                    sums(name, ones, [[0], [T]])
                elif kind == "qp":
                    sums(name, heads64, [[0], [T]])
                else:
                    sums(name, ones, [[0]], TM)

            for n, name in enumerate(PARTS):
                project_part(name)
                if n >= 1:
                    sum_part(PARTS[n - 1])
                if n >= 3 and PARTS[n - 3][0:2] == "qp":
                    m = int(PARTS[n - 3][2:])
                    claim(("rot", m))
                    pe.wait_ge(normed, NORM[f"qp{m}"] + 1)
                    for a in range(2):
                        mm = pe.matmul(pair(("rot", m))[:, a, :], C("rot"), qp[:, 2 * m + a, :], start=True, stop=True)
                    fills(mm, ("rot", m))
            sum_part(PARTS[-1])
            for t in range(TT + 1):
                tokens(("mv", t), "ukv1", (t,), ckv, 2, 0, 1024)

            def scores_m(u):
                h, i = UNITS_M[u]
                key = ("MS", u)
                claim(key)
                if u == 0:
                    pe.wait_ge(normed, NORM["kn7"] + 1)
                    pe.wait_ge(roped, 3)
                nk = (i + 1) * P
                r = 64 * (h % 2)
                out = flat(key)
                for at, a, n in ((0, 0, nk), (nk, T, META)):
                    pe.matmul(out[:, at:at + n], qn[:, h, i * P:(i + 1) * P], kn[:, h, a:a + n], start=True, stop=False)
                    mm = pe.matmul(out[:, at:at + n], qp[r:r + 64, h // 2, i * P:(i + 1) * P], kp[r:r + 64, a:a + n],
                                   start=False, stop=True)
                fills(mm, key)

            def side_m(g, m):
                if g == "gq":
                    project_h((g, m))
                elif g == "gk":
                    project_h((g, m), TM)
                else:
                    project_h((g, m), TM, rows=16)

            def outputs_m(u):
                h, i = UNITS_M[u]
                claim(("MO", u))
                when_emptied(pe, ("MT", u))
                for b in range(i + 1):
                    pe.matmul(flat(("MO", u))[:, 0:P], mv[:, b, h * P:(h + 1) * P], mpt[:, u % 2, b * P:(b + 1) * P],
                              start=(b == 0), stop=False)
                fills(pe.matmul(flat(("MO", u))[:, 0:P], mvm[0:META, h * P:(h + 1) * P], mpt[0:META, u % 2, 512:640],
                                start=False, stop=True), ("MO", u))

            scores_m(0)
            scores_m(1)
            for u, (h, i) in enumerate(UNITS_M):
                nk = (i + 1) * P
                claim(("MT", u))
                pe.wait_ge(mprobs, u + 1)
                for b in range(i + 1):
                    pe.transpose(flat(("MT", u))[:, b * P:(b + 1) * P], mp[:, u % 3, b * P:(b + 1) * P], ident)
                fills(pe.transpose(flat(("MT", u))[0:META, 512:640], mp[:, u % 3, nk:nk + META], ident), ("MT", u))
                if u + 2 < len(UNITS_M):
                    scores_m(u + 2)
                if u in SIDE_M:
                    side_m(*SIDE_M[u])
                if u:
                    outputs_m(u - 1)
            outputs_m(len(UNITS_M) - 1)

            pe.wait_ge(keys_in, 32)

            def decay_input(h):
                claim(("z", h))
                for a, n in ((0, T), (T, META)):
                    mm = pe.matmul(flat(("z", h))[:, a:a + n], wa2_sb[:, h * P:(h + 1) * P], gaT[0:16, a:a + n],
                                   start=True, stop=True)
                fills(mm, ("z", h))

            def level(h, n):
                key = ("lev", h, n)
                claim(key)
                if n:
                    pe.wait_ge(level_qk, 7 * h + n)
                for c in range(TT):
                    lhs = gk[:, h, c * P:(c + 1) * P] if n == 0 else kl[n % 2][:, c * P:(c + 1) * P]
                    rhs = gq[:, h, c * P:(c + 1) * P] if n == 0 else ql[n % 2][:, c * P:(c + 1) * P]
                    mm = pe.matmul(flat(key)[:, c * P:(c + 1) * P], lhs, rhs, start=True, stop=True)
                fills(mm, key)

            def gate_quarter(h, q):
                key = ("ta", h)
                m = q // 2
                if q == 0:
                    claim(key)
                up, low = split_arrived(f"ta{h}") if q == 0 else W_parts(f"ta{h}")
                d = slice(m * P, (m + 1) * P)
                for k in range(4 * (q % 2), 4 * (q % 2) + 4):
                    mm = three(pair(key)[:, m, :], (up[:, k, d], low[:, k, d]), h_parts(k, 0, T), k == 0, k == KD - 1)
                if q == 3:
                    fills(mm, key)

            def output_quarter(h, q):
                key = ("oa", h)
                m = q // 2
                if q == 0:
                    claim(key)
                    arrived(f"oa{h}")
                for k in range(4 * (q % 2), 4 * (q % 2) + 4):
                    mm = pe.matmul(pair(key)[:, m, :], W(f"oa{h}")[:, k, m * P:(m + 1) * P], ya[:, k, :],
                                   start=(k == 0), stop=(k == KD - 1))
                if q == 3:
                    fills(mm, key)

            when_emptied(pe, ("ga", 0))
            decay_input(0)
            for g in range(4):
                tokens_h(("gv", g, 0), range(TT))
                tokens_h(("gv", g, 1), (TT,))
            when_emptied(pe, ("gv", 3, 1))
            for h in range(HG):
                level(h, 0)
                gate_quarter(h, 0)
                level(h, 1)
                gate_quarter(h, 1)
                level(h, 2)
                gate_quarter(h, 2)
                gate_quarter(h, 3)
                level(h, 3)
                if h + 1 < HG:
                    decay_input(h + 1)
                level(h, 4)
                level(h, 5)
                output_quarter(h, 0)
                level(h, 6)
                output_quarter(h, 1)
                level(h, 7)
                output_quarter(h, 2)
                claim(("kd", h))
                pe.wait_ge(kd_ready, h + 1)
                for c in range(TT):
                    pe.transpose(flat(("kd", h))[:, c * P:(c + 1) * P], kl[0][:, c * P:(c + 1) * P], ident)
                fills(pe.transpose(flat(("kd", h))[0:META, 512:640], kl[0][:, T:TM], ident), ("kd", h))
                output_quarter(h, 3)
                when_emptied(pe, ("kd", h))
                for c in range(TT):
                    key = ("st", h, c)
                    claim(key)
                    if c == 0:
                        mm = pe.matmul(flat(key)[:, 0:HV], kdt[0:META, TT, :], gvm[0:META, h * HV:(h + 1) * HV],
                                       start=True, stop=True)
                    else:
                        mm = pe.matmul(flat(key)[:, 0:HV], kdt[:, c - 1, :], gv[:, c - 1, h * HV:(h + 1) * HV],
                                       start=True, stop=True)
                    fills(mm, key)
                key = ("go", h)
                claim(key)
                when_emptied(pe, ("lev", h, 7))
                pe.wait_ge(qb_ready, h + 1)
                when_emptied(pe, ("st", h, TT - 1))
                for e in range(2):
                    for c in range(TT):
                        pe.matmul(pair(key)[:, e, c * P:(c + 1) * P], gv[:, c, h * HV + e * P:h * HV + (e + 1) * P],
                                  attT[:, c * P:(c + 1) * P], start=True, stop=False)
                        mm = pe.matmul(pair(key)[:, e, c * P:(c + 1) * P], state[:, c, e * P:(e + 1) * P],
                                       qb[:, c * P:(c + 1) * P], start=False, stop=True)
                fills(mm, key)
            project_h(("gg", 0))
            for h in range(HG):
                sums(f"g{h}", ones, [[0, T]])
            for h in range(1, HG):
                project_h(("gg", h))
            for m in range(4):
                project_h(("tb", m))
                project_parts(("ob", m), O_PARTS, 2)
            for m in range(4):
                project_parts(("w2", m), MIX_PARTS, 3)

            big_sums("ffn")

            def query(h):
                project_parts(("pq", h), Q_PARTS, 4)

            query(0)
            for h in range(HP):
                if h + 1 < HP:
                    query(h + 1)
                key = ("ps", h)
                claim(key)
                when_emptied(pe, ("pq", h))
                for t in range(TT):
                    for a in range(2):
                        n = 2 * t + a
                        mm = pe.matmul(flat(key)[:, n * P:(n + 1) * P], pq[:, 2 * (h % 2) + a, t * P:(t + 1) * P],
                                       keys_sb[:, a, :], start=True, stop=True)
                fills(mm, key)

            def hidden(out, u_parts, j):
                (u_hi, u_lo), (h_hi, h_lo) = u_parts, h_hl
                n = slice(j * P, (j + 1) * P)
                for k in range(KD):
                    pe.matmul(out, u_hi[:, k, n], h_hi[:, k, :], start=(k == 0), stop=False)
                    pe.matmul(out, u_hi[:, k, n], h_lo[:, k, :], start=False, stop=False)
                    mm = pe.matmul(out, u_lo[:, k, n], h_hi[:, k, :], start=False, stop=(k == KD - 1))
                return mm

            pe.wait_ge(h_split, 1)
            for g in range(EARLY):
                for half in range(2):
                    key = ("pre", g, half)
                    claim(key)
                    pe.wait_ge(u_split, g + 1)
                    for a in range(2):
                        mm = hidden(pair(key)[:, a, :], early_u_hl[g % 2], 2 * half + a)
                    fills(mm, key)
            pe.wait_ge(entries, 1)
            for t in range(TT):
                key = ("tr", t)
                claim(key)
                for j in range(3):
                    mm = pe.transpose(flat(key)[:, j * P:(j + 1) * P], ent[:, t, j, :], ident)
                fills(mm, key)

            for t in range(TT):
                when_emptied(pe, ("tr", t))

            def spread_tokens(step):
                for q in range(4):
                    pe.wait_ge(hot, 4 * step + q + 1)
                    pe.wait_ge(hot_n2, 4 * step + q + 1)
                    at_least(pe, copied, 4 * step + q - 3)
                    for j in range(4):
                        mm = pe.matmul(ps[:, q, j * P:(j + 1) * P], oneA[:, 4 * q + j, :],
                                       oneB[:, 4 * q + j, :], start=True, stop=True)
                    mm.then_inc(spread, 1)

            spread_tokens(0)
            with pe.Fori(1, T // 16) as step:
                spread_tokens(step)
            pe.wait_ge(copied, T // 4)

            def pre(g, s):
                pe.wait_ge(u_split, g + 1)
                for j in range(EG):
                    at_least(pe, gelu_done, EG * (g - EARLY) - EG + j + 1)
                    hidden(ps[:, j, :], u_hl[s], j).then_inc(pre_done, 1)

            def combine(g, s):
                pe.wait_ge(v_split, g + 1)
                pe.wait_ge(coef_done, EG * g + EG)
                (v_hi, v_lo), (c_hi, c_lo) = v_hl[s], c_hl[s]
                for m in range(KD):
                    at_least(pe, added, KD * g + m - 3)
                    d = slice(m * P, (m + 1) * P)
                    out = ps[:, 4 + m % 4, :]
                    for j in range(EG):
                        pe.matmul(out, v_hi[:, j, d], c_hi[:, j, :], start=(j == 0), stop=False)
                        pe.matmul(out, v_hi[:, j, d], c_lo[:, j, :], start=False, stop=False)
                        mm = pe.matmul(out, v_lo[:, j, d], c_hi[:, j, :], start=False, stop=(j == EG - 1))
                    mm.then_inc(out_done, 1)

            def two_groups(it, last=False):
                pre(2 * it + 1, 1)
                combine(2 * it, 0)
                if not last:
                    pre(2 * it + 2, 0)
                combine(2 * it + 1, 1)

            for g in range(EARLY - 1):
                combine(g, g % 2)
            pre(EARLY, 0)
            combine(EARLY - 1, 1)
            with pe.Fori(EARLY // 2, GROUPS // 2 - 1) as it:
                two_groups(it)
            two_groups(GROUPS // 2 - 1, last=True)

        @block.scalar
        def _(act):
            steps = [0]

            def link(ins):
                steps[0] += 1
                ins.then_inc(act_step, 1)
                act.wait_ge(act_step, steps[0])

            def copy_out(key, dst, src, func=ACT.Copy, scale=1.0):
                when_filled(act, key)
                empties(act.activation(dst, src, func, scale=scale), key)

            def square(name, dst, src):
                k = NORM[name]
                back = 1 if (NORMS[k][2] or NORMS[k - 1][2]) else 2
                if k >= back:
                    when_filled(act, ("ss", NORMS[k - back][0]))
                act.activation(dst, src, ACT.Square).then_inc(squared, 1)

            def root(name, width, eps="eps"):
                k = NORM[name]
                if k >= 2:
                    act.wait_ge(normed, k - 1)
                when_filled(act, ("ss", name))
                r = rt[:, k % 2, 0:width]
                empties(act.activation(r, flat(("ss", name))[:, 0:width], ACT.Ln, bias=V(eps),
                                       scale=1.0 / NORMS[k][1]), ("ss", name))
                when_emptied(act, ("ss", name))
                act.activation(r, r, ACT.Exp, scale=-0.5).then_inc(rooted, 1)

            def square_two(name, m, src, width=T):
                k = NORM[name]
                if m == 0 and k:
                    when_filled(act, ("ss", NORMS[k - 1][0]))
                dst = sqbuf[:, 0:KD * width].rearrange("p (k t) -> p k t", k=KD)[:, 2 * m:2 * m + 2, :]
                act.activation(dst, src, ACT.Square).then_inc(squares, 1)

            for m in range(4):
                act.wait_ge(x_first[m], 16)
                square_two("n1", m, xs[:, 2 * m:2 * m + 2, :])
            act.wait_ge(first_consts, 32)
            copy_out(("lam",), small[:, 2:4], flat(("lam",))[:, 0:2], ACT.Exp)
            root("n1", T)

            def round_h(turn, name, width):
                for k in range(KD):
                    if k < KD - 1:
                        act.wait_ge(norm_part, (KD - 1) * turn + k + 1)
                    else:
                        act.wait_ge(normed, NORM[name] + 1)
                    act.activation(h_upper[:, k, 0:width], normed_x[:, k, 0:width], ACT.Copy).then_inc(h_rounded_k, 1)

            round_h(0, "n1", T)
            for m in range(2):
                copy_out(("q", m), qT[:, 2 * m:2 * m + 2, :], pair(("q", m)))
            for m in range(2):
                copy_out(("k", m), kT[:, 2 * m:2 * m + 2, :], pair(("k", m)))
            for m in range(2):
                copy_out(("v", m), v_tok[:, :, 256 * m:256 * m + 256],
                         flat(("v", m)).rearrange("p (t n) -> p t n", t=TT))

            def exps_a(u):
                h, i = UNITS_A[u]
                nk = (i + 1) * P
                st = small[:, 16 + 16 * (u % 3):32 + 16 * (u % 3)]
                act.wait_ge(stats_ready, u + 1)
                for m in range(2):
                    e = act.activation(probs[:, u % 3, m, 0:nk], probs[:, u % 3, m, 0:nk], ACT.Exp,
                                       bias=st[:, 2 + m:3 + m], scale=SCALE_A, accum_out=st[:, 4 + m:5 + m])
                e.then_inc(exp_done, 1)

            def round_pair(n, parts, k, src):
                act.wait_ge(pair_made, n + 1)
                act.activation(parts[0][:, k:k + 2, :], src[:, k:k + 2, :], ACT.Copy).then_inc(pair_rounded, 1)

            def copy_a(u):
                h, i = UNITS_A[u]
                copy_out(("O", u), mixin[:, h, i * P:(i + 1) * P], flat(("O", u))[:, 0:P])

            side = [(g, m) for g in ("c", "u", "zc", "b", "za") for m in (0, 1)]
            exps_a(0)
            exps_a(1)
            for u, (h, i) in enumerate(UNITS_A):
                nk = (i + 1) * P
                if u >= 2:
                    when_filled(act, ("O", u - 2))
                copy_out(("T", u), pT_sb[:, u % 2, 0:nk], flat(("T", u))[:, 0:nk])
                if side:
                    g, m = side.pop(0)
                    if g == "c":
                        copy_out((g, m), cT[:, 2 * m:2 * m + 2, :], pair((g, m)))
                    if g == "zc":
                        copy_out((g, m), szT[:, 2 * m:2 * m + 2, :], pair((g, m)), ACT.Silu)
                    if g == "za":
                        copy_out((g, m), zaT[:, 2 * m:2 * m + 2, :], pair((g, m)), ACT.Silu)
                if u:
                    copy_a(u - 1)
                if u + 2 < len(UNITS_A):
                    exps_a(u + 2)
            copy_a(len(UNITS_A) - 1)
            when_emptied(act, ("O", len(UNITS_A) - 1))
            for n in range(2):
                square(f"sl{n}", small_sq[NORM[f"sl{n}"] % 2][:, 0:1024].rearrange("p (a b) -> p a b", a=2),
                       mixin[:, 2 * n:2 * n + 2, :])
            when_filled(act, ("za", 1))
            round_pair(0, MIXIN_PARTS, 4, mixin)
            round_pair(1, MIXIN_PARTS, 6, mixin)
            for n in range(2):
                root(f"sl{n}", 1024, "subeps")
            round_pair(2, MIXIN_PARTS, 0, mixin)
            round_pair(3, MIXIN_PARTS, 2, mixin)
            for m in range(4):
                when_filled(act, ("wo", m))
                square_two("post", m, pair(("wo", m)))
                copy_out(("wo", m), mixedT[:, 2 * m:2 * m + 2, :], pair(("wo", m)))
            root("post", T)
            for m in range(4):
                when_filled(act, ("ple", m))
                square_two("ple", m, pair(("ple", m)))
                copy_out(("ple", m), eT[:, 2 * m:2 * m + 2, :], pair(("ple", m)))
            for m in range(4):
                round_pair(4 + m, X1_PARTS, 2 * m, xs)
            root("ple", T)
            for m in range(4):
                copy_out(("pg", m), sgT[:, 2 * m:2 * m + 2, :], pair(("pg", m)), ACT.Sigmoid)

            for m in range(4):
                act.wait_ge(x2_ready, m + 1)
                square_two("mix", m, resid[:, 2 * m:2 * m + 2, :], TM)
            root("mix", TM)
            act.wait_ge(x2_stored, 64)
            round_h(1, "mix", TM)
            when_filled(act, ("ss", "mix"))
            when_filled(act, ("cq", 0))
            act.activation(sqbuf[:, 0:2 * T].rearrange("p (a b) -> p a b", a=2), pair(("cq", 0)), ACT.Square)
            copy_out(("cq", 0), cq[:, 0:2, :], pair(("cq", 0)))
            when_filled(act, ("cq", 1))
            square("cq", sqbuf[:, 2 * T:3 * T], flat(("cq", 1))[:, 0:T])
            copy_out(("cq", 1), cq[:, 2, :], flat(("cq", 1))[:, 0:T])
            for k in range(2):
                copy_out(("ckv", k), ckv[:, k, :], flat(("ckv", k))[:, 0:TM])
            copy_out(("kpe", 0), kp, flat(("kpe", 0))[:, 0:TM])
            root("cq", T)
            when_emptied(act, ("kpe", 0))
            square("ckv", norm_sq("ckv")[:, 0:2 * TM].rearrange("p (k t) -> p k t", k=2), ckv)
            square("kpe", norm_sq("kpe")[:, 0:TM], kp)
            root("ckv", TM)
            root("kpe", TM)

            def square_part(name):
                key = part_job(name)
                sq = norm_sq(name)
                when_filled(act, key)
                if name[0:2] == "kn":
                    square(name, sq[:, 0:TM], flat(key)[:, 0:TM])
                else:
                    square(name, sq[:, 0:1024].rearrange("p (a b) -> p a b", a=2), pair(key))

            for n, name in enumerate(PARTS):
                square_part(name)
                if n >= 1:
                    root(PARTS[n - 1], TM if PARTS[n - 1][0:2] == "kn" else 1024)
            root(PARTS[-1], TM)
            for t in range(TT + 1):
                if t < TT:
                    copy_out(("mv", t), mv[:, t, :], flat(("mv", t)))
                else:
                    copy_out(("mv", t), mvm[0:META, :], flat(("mv", t))[0:META, :])

            def exps_m(u):
                h, i = UNITS_M[u]
                n = (i + 1) * P + META
                st = small[:, 64 + 8 * (u % 3):72 + 8 * (u % 3)]
                act.wait_ge(neg_max, u + 1)
                if u >= 3:
                    when_filled(act, ("MT", u - 3))
                empties(act.activation(mp[:, u % 3, 0:n], flat(("MS", u))[:, 0:n], ACT.Exp, bias=st[:, 1:2],
                                       scale=SCALE_M, accum_out=st[:, 2:3]), ("MS", u))

            def copy_m(u):
                h, i = UNITS_M[u]
                copy_out(("MO", u), ya[:, h, i * P:(i + 1) * P], flat(("MO", u))[:, 0:P])

            exps_m(0)
            exps_m(1)
            for u, (h, i) in enumerate(UNITS_M):
                nk = (i + 1) * P
                key = ("MT", u)
                when_filled(act, key)
                if u >= 2:
                    when_filled(act, ("MO", u - 2))
                act.activation(mpt[0:META, u % 2, 512:640], flat(key)[0:META, 512:640], ACT.Copy)
                empties(act.activation(mpt[:, u % 2, 0:nk], flat(key)[:, 0:nk], ACT.Copy), key)
                if u in SIDE_M:
                    g, m = key = SIDE_M[u]
                    if g == "gq":
                        copy_out(key, gq[:, 2 * m:2 * m + 2, :], pair(key), scale=HK ** -0.5)
                    elif g == "gk":
                        copy_out(key, gk[:, m, :], flat(key)[:, 0:TM])
                    else:
                        copy_out(key, gaT[0:16, :], flat(key)[0:16, 0:TM])
                if u:
                    copy_m(u - 1)
                if u + 2 < len(UNITS_M):
                    exps_m(u + 2)
            copy_m(len(UNITS_M) - 1)


            def decay_terms(h):
                key = ("z", h)
                b = bc[h % 2]
                when_filled(act, key)
                if h:
                    act.wait_ge(cumulated, h)
                if h >= 2:
                    act.wait_ge(kd_ready, h - 1)
                act.activation(la, flat(key)[:, 0:TM], ACT.Identity, bias=V("ba", h))
                empties(act.activation(b, flat(key)[:, 0:TM], ACT.Abs, bias=V("ba", h)), key)
                when_emptied(act, key)
                link(act.activation(b, b, ACT.Exp, scale=-1.0))
                act.activation(b, b, ACT.Ln, bias=C("ones", 0, 1)).then_inc(zbias, 1)

            decay_terms(0)
            for g in range(4):
                cols = slice(256 * g, 256 * g + 256)
                copy_out(("gv", g, 0), gv[:, :, cols], flat(("gv", g, 0)).rearrange("p (t n) -> p t n", t=TT))
                copy_out(("gv", g, 1), gvm[0:META, cols], flat(("gv", g, 1))[0:META, 0:256])
            for h in range(HG):
                b = bc[h % 2]
                act.wait_ge(cumulated, h + 1)
                if h:
                    when_filled(act, ("go", h - 1))
                act.activation(qb, b[:, 0:T], ACT.Exp, scale=1 / TAU)
                act.activation(dec[:, 0:TT], b[:, 0:T].rearrange("p (c t) -> p c t", t=P)[:, :, P - 1], ACT.Exp,
                               scale=1 / TAU).then_inc(decays, 1)
                for n, s in enumerate(LEVELS):
                    act.wait_ge(level_diff, 7 * h + n + 1)
                    w = wl[(n + 1) % 2].rearrange("p (b x s) -> p b x s", x=2, s=s)
                    act.activation(w[:, :, 0, :], w[:, :, 0, :], ACT.Exp, scale=-1 / TAU)
                    act.activation(w[:, :, 1, :], w[:, :, 1, :], ACT.Exp, scale=1 / TAU).then_inc(level_exp, 1)
                    if n == 5 and h + 1 < HG:
                        decay_terms(h + 1)
                    if n == 3:
                        when_filled(act, ("ta", h))
                        if h >= 2:
                            when_emptied(act, ("oa", h - 2))
                        empties(act.activation(gate_a[:, h % 2, :, :], pair(("ta", h)), ACT.Sigmoid), ("ta", h))
                act.wait_ge(kd_diff, h + 1)
                act.activation(kl[0], kl[0], ACT.Exp, scale=1 / TAU).then_inc(kd_exp, 1)
                key = ("kd", h)
                when_filled(act, key)
                if h:
                    when_filled(act, ("st", h - 1, TT - 1))
                act.activation(kdt[0:META, TT, :], flat(key)[0:META, 512:640], ACT.Copy)
                empties(act.activation(kdt[:, 0:TT, :].rearrange("p a b -> p (a b)"), flat(key)[:, 0:T], ACT.Copy), key)
                copy_out(("go", h), oT[:, 2 * h:2 * h + 2, :], pair(("go", h)))
            when_emptied(act, ("go", HG - 1))
            def square_head(h):
                square(f"g{h}", norm_sq(f"g{h}")[:, 0:1024].rearrange("p (a b) -> p a b", a=2),
                       oT[:, 2 * h:2 * h + 2, :])

            square_head(0)
            square_head(1)
            def silu(h):
                if h >= 2:
                    act.wait_ge(pair_made, 8 + h - 1)
                copy_out(("gg", h), gate_s[:, h % 2, :, :], pair(("gg", h)), ACT.Silu)

            def sigmoid(m):
                if m < 2:
                    act.wait_ge(pair_made, 8 + HG)
                else:
                    when_emptied(act, ("ob", m - 2))
                copy_out(("tb", m), gate_s[:, m % 2, :, :], pair(("tb", m)), ACT.Sigmoid)

            silu(0)
            for h in range(HG):
                root(f"g{h}", T)
                if h + 2 < HG:
                    square_head(h + 2)
            for h in range(HG):
                if h + 1 < HG:
                    silu(h + 1)
                round_pair(8 + h, O_PARTS, 2 * h, oT)
            sigmoid(0)
            for m in range(4):
                if m + 1 < 4:
                    sigmoid(m + 1)
                round_pair(12 + m, MIX_PARTS, 2 * m, mixT)

            for m in range(4):
                when_emptied(act, ("w2", m))
                square_two("ffn", m, xs[:, 2 * m:2 * m + 2, :])
            root("ffn", T)
            for m in range(4):
                round_pair(16 + m, Q_PARTS, 2 * m, hs)
            act.activation(h_hl[0], hs, ACT.Copy).then_inc(h_rounded, 1)

            def query(h):
                if h >= 2:
                    when_filled(act, ("ps", h - 2))
                copy_out(("pq", h), pq[:, 2 * (h % 2):2 * (h % 2) + 2, :], pair(("pq", h)))

            def round_early(g):
                act.wait_ge(u_in, 16 * g + 16)
                when_filled(act, ("pre", g - 2, 1) if g >= 2 else ("pq", HP - 1))
                act.activation(early_u_hl[g % 2][0], u_raw, ACT.Copy).then_inc(u_rounded, 1)

            query(0)
            for h in range(HP):
                if h + 1 < HP:
                    query(h + 1)
                copy_out(("ps", h), sc[:, h].rearrange("p a b -> p (a b)"), flat(("ps", h)))
                if h == HP - 2:
                    round_early(0)
            round_early(1)
            for g in range(EARLY):
                for half in range(2):
                    copy_out(("pre", g, half), early[:, g, 2 * half:2 * half + 2, :], pair(("pre", g, half)), ACT.Gelu)
                if g + 2 <= EARLY:
                    round_early(g + 2)
            act.wait_ge(soft_diff, 1)
            act.activation(ent[:, :, 2, :], ent[:, :, 2, :], ACT.Exp).then_inc(soft_exp, 1)
            for t in range(TT):
                copy_out(("tr", t), entT[:, :, t * P:(t + 1) * P],
                         flat(("tr", t))[:, 0:3 * P].rearrange("p (a b) -> p a b", a=3))

            def copy_tokens(n, i):
                dst = stage[:, n % 2, :].rearrange("p (j t) -> p t j", t=HALF)
                for q in range(4):
                    act.wait_ge(spread, 4 * (4 * n + i) + q + 1)
                    act.activation(dst[:, bass.ds(16 * i + 4 * q, 4), :],
                                   ps[:, q, :].rearrange("p (t j) -> p t j", t=4), ACT.Copy).then_inc(copied, 1)

            def round_u(g, s):
                act.wait_ge(u_in, 16 * g + 16)
                at_least(act, pre_done, EG * (g - EARLY) - EG)
                act.activation(u_hl[s][0], u_raw, ACT.Copy).then_inc(u_rounded, 1)

            def round_v(g, s):
                act.wait_ge(v_in, 16 * g + 16)
                at_least(act, out_done, KD * g - KD)
                act.activation(v_hl[s][0], v_raw, ACT.Copy).then_inc(v_rounded, 1)

            for n in range(PIECES):
                if n >= 2:
                    act.wait_ge(first_stored[n % 2], 16 * (n // 2))
                    act.wait_ge(stored[n % 2], 16 * (n // 2))
                with act.Fori(0, HALF // 16) as i:
                    copy_tokens(n, i)
            act.wait_ge(first_stored[0], 8 * PIECES)
            act.wait_ge(stored[0], 8 * PIECES)

            def round_coef(g, s, j, src):
                act.wait_ge(coef_mult, EG * g + j + 1)
                act.activation(c_hl[s][0][:, j, :], src[:, j, :], ACT.Copy).then_inc(coef_rounded, 1)

            def round_early_coefs(g, s):
                at_least(act, out_done, KD * g - KD)
                for j in range(EG):
                    round_coef(g, s, j, early[:, g])

            def gelus(g, s):
                def gelu(j):
                    act.wait_ge(pre_done, EG * (g - EARLY) + j + 1)
                    act.wait_ge(coef_done, EG * g - EG + j + 1)
                    act.activation(coef[:, j, :], ps[:, j, :], ACT.Gelu).then_inc(gelu_done, 1)

                gelu(0)
                act.wait_ge(out_done, KD * g - KD)
                for j in range(1, EG):
                    gelu(j)
                    round_coef(g, s, j - 1, coef)
                round_coef(g, s, EG - 1, coef)

            def period(g, s, last=0):
                if last < 2:
                    round_u(g + 2, s)
                if last < 3:
                    round_v(g + 1, 1 - s)
                    gelus(g + 1, 1 - s)

            round_v(0, 0)
            round_early_coefs(0, 0)
            act.wait_ge(first_stored[1], 8 * PIECES)
            act.wait_ge(half_stored, 16)
            for g in range(1, EARLY):
                round_v(g, g % 2)
                round_early_coefs(g, g % 2)
            act.wait_ge(stored[1], 8 * PIECES)
            period(EARLY - 1, 1)
            with act.Fori(EARLY // 2, GROUPS // 2 - 1) as it:
                period(2 * it, 0)
                period(2 * it + 1, 1)
            period(GROUPS - 2, 0, last=2)

        @block.vector
        def _(dve):
            steps = [0]

            def link(ins):
                steps[0] += 1
                ins.then_inc(dve_step, 1)
                dve.wait_ge(dve_step, steps[0])

            def inverse(name, width):
                dve.wait_ge(rooted, NORM[name] + 1)
                return rt[:, NORM[name] % 2, 0:width]

            def scale_by(dst, src, gain, r, last=None):
                ins = dve.scalar_tensor_tensor(dst, src, gain, r, ALU.mult, ALU.mult)
                if last:
                    ins.then_inc(normed, 1)

            def big_norm(name, gain, dst, src, width=T):
                r = inverse(name, width)
                for k in range(KD):
                    scale_by(dst[:, k, 0:width], src[:, k, 0:width], V(gain, k), r, k == KD - 1)
                dve.wait_ge(normed, NORM[name] + 1)

            dve.wait_ge(first_consts, 32)
            dve.tensor_tensor(small[:, 0:2], vec[:, VEC["lam"][0]:VEC["lam"][0] + 2],
                              vec[:, VEC["lam"][0] + 2:VEC["lam"][0] + 4], ALU.mult).then_inc(lam_ready, 1)
            dve.memset(gT[:, :, 0:2], 0.0)
            when_emptied(dve, ("lam",))
            link(dve.scalar_tensor_tensor(small[:, 4:5], small[:, 3:4], -LAMBDA_INIT, small[:, 2:3],
                                          ALU.add, ALU.subtract))
            for m in range(4):
                dve.wait_ge(x_first[m], 16)

            def split_norm(turn, name, gain, width):
                r = inverse(name, width)

                def lower(k):
                    dve.wait_ge(h_rounded_k, KD * turn + k + 1)
                    dve.tensor_tensor(h_lower[:, k, 0:width], normed_x[:, k, 0:width], h_upper[:, k, 0:width],
                                      ALU.subtract).then_inc(h_ready, 1)

                for k in range(KD):
                    ins = dve.scalar_tensor_tensor(normed_x[:, k, 0:width], resid[:, k, 0:width], V(gain, k), r,
                                                   ALU.mult, ALU.mult)
                    ins.then_inc(norm_part if k < KD - 1 else normed, 1)
                    if k:
                        lower(k - 1)
                lower(KD - 1)

            split_norm(0, "n1", "pre", T)

            def stats_a(u):
                h, i = UNITS_A[u]
                nk = (i + 1) * P
                st = small[:, 16 + 16 * (u % 3):32 + 16 * (u % 3)]
                key = ("S", u)
                when_filled(dve, key)
                for m in range(2):
                    ins = dve.scalar_tensor_tensor(probs[:, u % 3, m, 0:nk], C("dist", T - nk, T), -SLOPES[h] / SCALE_A,
                                                   pair(key)[:, m, 0:nk], ALU.mult, ALU.add)
                empties(ins, key)
                when_emptied(dve, key)
                link(dve.tensor_reduce(st[:, 0:2], probs[:, u % 3, :, 0:nk], AX_X, ALU.max))
                dve.tensor_scalar(st[:, 2:4], st[:, 0:2], -SCALE_A, None, ALU.mult).then_inc(stats_ready, 1)

            def combine_a(u):
                h, i = UNITS_A[u]
                nk = (i + 1) * P
                st = small[:, 16 + 16 * (u % 3):32 + 16 * (u % 3)]
                dve.wait_ge(exp_done, u + 1)
                if u >= 2:
                    when_filled(dve, ("T", u - 2))
                link(dve.reciprocal(st[:, 6:8], st[:, 4:6]))
                link(dve.tensor_scalar(weights_p[:, u % 2, 0:nk], probs[:, u % 3, 1, 0:nk], st[:, 7:8], small[:, 4:5],
                                       ALU.mult, ALU.mult))
                dve.scalar_tensor_tensor(weights_p[:, u % 2, 0:nk], probs[:, u % 3, 0, 0:nk], st[:, 6:7],
                                         weights_p[:, u % 2, 0:nk], ALU.mult, ALU.add).then_inc(probs_ready, 1)

            def split_pair(n, parts, k, src):
                dve.wait_ge(pair_rounded, n + 1)
                dve.tensor_tensor(parts[1][:, k:k + 2, :], src[:, k:k + 2, :], parts[0][:, k:k + 2, :],
                                  ALU.subtract).then_inc(pair_split, 1)

            def conv_part(m):
                for a in (2 * m, 2 * m + 1):
                    dst = mixin[:, 4 + a, :]
                    link(dve.tensor_scalar(dst, gT[:, a, 0:T], V("conv", a), None, ALU.mult))
                    link(dve.scalar_tensor_tensor(dst, gT[:, a, 1:T + 1], V("conv", 4 + a), dst, ALU.mult, ALU.add))
                    link(dve.scalar_tensor_tensor(dst, gT[:, a, 2:T + 2], V("conv", 8 + a), dst, ALU.mult, ALU.add))

            side = [(g, m) for g in ("c", "u", "zc", "b", "za") for m in (0, 1)]
            dve.wait_ge(consts_in, 32)
            stats_a(0)
            stats_a(1)
            combine_a(0)
            for u in range(len(UNITS_A)):
                if u + 1 < len(UNITS_A):
                    combine_a(u + 1)
                if u + 2 < len(UNITS_A):
                    stats_a(u + 2)
                if side:
                    g, m = side.pop(0)
                    if g == "u":
                        when_filled(dve, (g, m))
                        when_emptied(dve, ("c", m))
                        empties(dve.tensor_tensor(gT[:, 2 * m:2 * m + 2, 2:T + 2], cT[:, 2 * m:2 * m + 2, :],
                                                  pair((g, m)), ALU.mult), (g, m))
                    if g == "zc":
                        when_emptied(dve, ("u", m))
                        conv_part(m)
                    if g == "b":
                        when_filled(dve, (g, m))
                        when_emptied(dve, ("zc", m))
                        sz = szT[:, 2 * m:2 * m + 2, :]
                        empties(dve.tensor_tensor(sz, sz, pair((g, m)), ALU.mult), (g, m))
                        when_emptied(dve, (g, m))
                        mx = mixin[:, 4 + 2 * m:6 + 2 * m, :]
                        dve.tensor_tensor(mx, mx, sz, ALU.mult).then_inc(pair_made, 1)
            for n in range(2):
                split_pair(n, MIXIN_PARTS, 4 + 2 * n, mixin)
            for n in range(2):
                r = inverse(f"sl{n}", 1024).rearrange("p (a b) -> p a b", a=2)
                mx = mixin[:, 2 * n:2 * n + 2, :]
                scale_by(mx, mx, V("subln"), r, True)
                dve.wait_ge(normed, NORM[f"sl{n}"] + 1)
                when_emptied(dve, ("za", n))
                dve.scalar_tensor_tensor(mx, mx, 1.0 - LAMBDA_INIT, zaT[:, 2 * n:2 * n + 2, :],
                                         ALU.mult, ALU.mult).then_inc(pair_made, 1)
            for n in range(2):
                split_pair(2 + n, MIXIN_PARTS, 2 * n, mixin)
            big_norm("post", "post", mixedT, mixedT)
            dve.wait_ge(x_in, 16)
            for m in range(4):
                x = xs[:, 2 * m:2 * m + 2, :]
                dve.tensor_tensor(x, x, mixedT[:, 2 * m:2 * m + 2, :], ALU.add).then_inc(pair_made, 1)
                if m:
                    split_pair(3 + m, X1_PARTS, 2 * m - 2, xs)
            split_pair(7, X1_PARTS, 6, xs)
            big_norm("ple", "ple", eT, eT)
            dve.wait_ge(pair_made, 8)
            for m in range(4):
                when_emptied(dve, ("pg", m))
                sg = sgT[:, 2 * m:2 * m + 2, :]
                link(dve.tensor_tensor(sg, sg, eT[:, 2 * m:2 * m + 2, :], ALU.mult))
                when_filled(dve, ("pg", 3))
                x = resid[:, 2 * m:2 * m + 2, 0:T]
                dve.tensor_tensor(x, x, sg, ALU.add).then_inc(x2_ready, 1)

            dve.wait_ge(x2_ready, 4)
            split_norm(1, "mix", "mix", TM)
            r = inverse("cq", T)
            for k in range(3):
                scale_by(cq[:, k, :], cq[:, k, :], V("qnorm", k), r, k == 2)
            r = inverse("ckv", TM)
            for k in range(2):
                scale_by(ckv[:, k, :], ckv[:, k, :], V("kvnorm", k), r, k == 1)
            scale_by(kp, kp, V("kp"), inverse("kpe", TM), True)

            def rope(n, key, dst, turned, cos, sin, tmp):
                if n:
                    dve.wait_ge(roped, n)
                when_filled(dve, key)
                empties(dve.tensor_tensor(tmp, turned, sin, ALU.mult), key)
                link(dve.tensor_tensor(dst, dst, cos, ALU.mult))
                when_emptied(dve, key)
                dve.tensor_tensor(dst, dst, tmp, ALU.add).then_inc(roped, 1)

            rope(0, ("rot", "kpe"), kp, flat(("rot", "kpe"))[:, 0:TM], C("cos"), C("sin"), rot_tmp[:, 0:TM])

            def part(name):
                kind, m = name[0:2], int(name[2:])
                key = part_job(name)
                r = rt[:, NORM[name] % 2, :]
                if kind == "kn":
                    return kn[:, m, :], flat(key)[:, 0:TM], r[:, 0:TM]
                return ((qn if kind == "qn" else qp)[:, 2 * m:2 * m + 2, :], pair(key),
                        r[:, 0:1024].rearrange("p (a b) -> p a b", a=2))

            def copy_part(name):
                dst, src, _ = part(name)
                dve.wait_ge(squared, squared_count(name))
                empties(dve.tensor_copy(dst, src), part_job(name))

            copy_part(PARTS[0])
            for n, name in enumerate(PARTS):
                if n + 1 < len(PARTS):
                    copy_part(PARTS[n + 1])
                dst, _, r = part(name)
                inverse(name, TM)
                when_emptied(dve, part_job(name))
                scale_by(dst, dst, V(name[0:2]), r, True)
                if n >= 2 and PARTS[n - 2][0:2] == "qp":
                    b = int(PARTS[n - 2][2:])
                    rope(b + 1, ("rot", b), qp[:, 2 * b:2 * b + 2, :], pair(("rot", b)),
                         C("cos", 0, T).unsqueeze(1).to_broadcast([P, 2, T]),
                         C("sin", 0, T).unsqueeze(1).to_broadcast([P, 2, T]),
                         rot_tmp[:, 0:1024].rearrange("p (a b) -> p a b", a=2))

            def stats_m(u):
                h, i = UNITS_M[u]
                nk = (i + 1) * P
                st = small[:, 64 + 8 * (u % 3):72 + 8 * (u % 3)]
                key = ("MS", u)
                when_filled(dve, key)
                link(dve.memset(flat(key)[0:CHUNK, nk - CHUNK:nk], NEG))
                link(dve.tensor_reduce(st[:, 0:1], flat(key)[:, 0:nk + META], AX_X, ALU.max))
                dve.tensor_scalar(st[:, 1:2], st[:, 0:1], -SCALE_M, None, ALU.mult).then_inc(neg_max, 1)

            stats_m(0)
            stats_m(1)

            def probs_m(u):
                n = (UNITS_M[u][1] + 1) * P + META
                st = small[:, 64 + 8 * (u % 3):72 + 8 * (u % 3)]
                when_emptied(dve, ("MS", u))
                link(dve.reciprocal(st[:, 3:4], st[:, 2:3]))
                dve.tensor_scalar(mp[:, u % 3, 0:n], mp[:, u % 3, 0:n], st[:, 3:4], None, ALU.mult).then_inc(mprobs, 1)

            probs_m(0)
            for u in range(len(UNITS_M)):
                if u + 1 < len(UNITS_M):
                    probs_m(u + 1)
                if u + 2 < len(UNITS_M):
                    stats_m(u + 2)

            def level_difference(h, n):
                s = LEVELS[n - 1]
                b = bc[h % 2][:, 0:T].rearrange("p (b x) -> p b x", x=2 * s)
                mid = b[:, :, s - 1:s].to_broadcast([P, T // (2 * s), 2 * s])
                dve.tensor_tensor(wl[n % 2].rearrange("p (b x) -> p b x", x=2 * s), b, mid,
                                  ALU.subtract).then_inc(level_diff, 1)

            att = attT.rearrange("p (c t) -> p c t", c=TT)

            def mask(n):
                return C("levels", n * P, (n + 1) * P).unsqueeze(1).to_broadcast([P, TT, P])

            def choose(h, n):
                key = ("lev", h, n)
                when_filled(dve, key)
                src = flat(key)[:, 0:T].rearrange("p (c t) -> p c t", c=TT)
                if n == 0:
                    if h:
                        when_filled(dve, ("go", h - 1))
                    empties(dve.tensor_tensor(att, src, mask(0), ALU.mult), key)
                else:
                    when_emptied(dve, ("lev", h, n - 1))
                    empties(dve.copy_predicated(att, mask(n).bitcast(U32), src), key)

            when_emptied(dve, ("gk", HG - 1))

            def cumulate(h):
                b = bc[h % 2]
                dve.wait_ge(zbias, h + 1)
                link(dve.scalar_tensor_tensor(la, la, 0.0, b, ALU.min, ALU.subtract))
                dve.tensor_tensor_scan(b, C("reset"), la, 0.0, ALU.mult, ALU.add).then_inc(cumulated, 1)

            cumulate(0)
            for h in range(HG):
                dve.wait_ge(cumulated, h + 1)
                if h:
                    dve.wait_ge(level_qk, 7 * h)
                level_difference(h, 1)
                level_difference(h, 2)
                choose(h, 0)
                dve.wait_ge(decays, h + 1)
                dve.tensor_tensor(qb, qb, gq[:, h, :], ALU.mult).then_inc(qb_ready, 1)
                for n in range(1, 8):
                    dve.wait_ge(level_exp, 7 * h + n)
                    if n > 2:
                        when_filled(dve, ("lev", h, n - 2))
                    elif h:
                        when_filled(dve, ("kd", h - 1))
                    dve.tensor_tensor(ql[n % 2], gq[:, h, :], wl[n % 2], ALU.mult)
                    dve.tensor_tensor(kl[n % 2][:, 0:T], gk[:, h, 0:T], wl[n % 2], ALU.mult).then_inc(level_qk, 1)
                    dve.wait_ge(level_qk, 7 * h + n)
                    if n < 6:
                        level_difference(h, n + 2)
                    if n > 1:
                        choose(h, n - 1)
                    if n == 6 and h + 1 < HG:
                        cumulate(h + 1)
                when_filled(dve, ("lev", h, 6))
                b = bc[h % 2]
                b4 = b[:, 0:T].rearrange("p (c t) -> p c t", c=TT)
                dve.tensor_tensor(kl[0][:, 0:T].rearrange("p (c t) -> p c t", c=TT),
                                  b4[:, :, P - 1:P].to_broadcast([P, TT, P]), b4, ALU.subtract)
                dve.tensor_tensor(kl[0][:, T:TM], b[:, TM - 1:TM].to_broadcast([P, META]), b[:, T:TM],
                                  ALU.subtract).then_inc(kd_diff, 1)
                choose(h, 7)
                dve.wait_ge(kd_exp, h + 1)
                dve.tensor_tensor(kl[0], kl[0], gk[:, h, :], ALU.mult).then_inc(kd_ready, 1)
                when_filled(dve, ("oa", h))
                when_emptied(dve, ("ta", h))
                empties(dve.tensor_tensor(mixT[:, 2 * h:2 * h + 2, :], gate_a[:, h % 2, :, :], pair(("oa", h)),
                                          ALU.mult), ("oa", h))
                if h:
                    when_filled(dve, ("go", h - 1))
                dve.wait_ge(decays, h + 1)
                for c in range(TT):
                    key = ("st", h, c)
                    when_filled(dve, key)
                    src = flat(key)[:, 0:HV]
                    if c == 0:
                        empties(dve.tensor_copy(state[:, 0, :], src), key)
                    else:
                        when_emptied(dve, ("st", h, c - 1))
                        empties(dve.scalar_tensor_tensor(state[:, c, :], state[:, c - 1, :], dec[:, c - 1:c], src,
                                                         ALU.mult, ALU.add), key)
            for h in range(HG):
                r = inverse(f"g{h}", T)
                for e in range(2):
                    scale_by(oT[:, 2 * h + e, :], oT[:, 2 * h + e, :], V("gnorm", e), r, e == 1)
            dve.wait_ge(normed, NORM[f"g{HG - 1}"] + 1)
            for h in range(HG):
                when_emptied(dve, ("gg", h))
                o = oT[:, 2 * h:2 * h + 2, :]
                dve.tensor_tensor(o, o, gate_s[:, h % 2, :, :], ALU.mult).then_inc(pair_made, 1)
                if h:
                    split_pair(7 + h, O_PARTS, 2 * h - 2, oT)
            split_pair(11, O_PARTS, 6, oT)
            for m in range(4):
                when_filled(dve, ("ob", m))
                when_emptied(dve, ("tb", m))
                if m:
                    dve.wait_ge(pair_made, 12 + m)
                empties(dve.tensor_tensor(mix_tmp, gate_s[:, m % 2, :, :], pair(("ob", m)), ALU.mult), ("ob", m))
                when_emptied(dve, ("ob", m))
                x = mixT[:, 2 * m:2 * m + 2, :]
                dve.tensor_tensor(x, x, mix_tmp, ALU.add).then_inc(pair_made, 1)
                split_pair(12 + m, MIX_PARTS, 2 * m, mixT)
            dve.wait_ge(x2_in, 16)
            for m in range(4):
                when_filled(dve, ("w2", m))
                x = resid[:, 2 * m:2 * m + 2, 0:T]
                empties(dve.tensor_tensor(x, x, pair(("w2", m)), ALU.add), ("w2", m))
            when_emptied(dve, ("w2", 3))
            r = inverse("ffn", T)
            for k in range(KD):
                ins = dve.scalar_tensor_tensor(hs[:, k, :], xs[:, k, :], V("ffn", k), r, ALU.mult, ALU.mult)
                if k % 2:
                    ins.then_inc(pair_made, 1)
                    if k > 1:
                        split_pair(16 + k // 2 - 1, Q_PARTS, k - 3, hs)
            split_pair(19, Q_PARTS, 6, hs)

            iota16 = C("iota", 0, TOPK)
            n_ent = TT * TOPK

            def best16(vals, index, src, n):
                for part in (slice(0, 8), slice(8, 16)):
                    for f in range(n):
                        ins = dve.max(vals[:, f, part], src[:, f, :])
                    link(ins)
                    for f in range(n):
                        ins = dve.max_index(index[:, f, part], vals[:, f, part], src[:, f, :])
                    link(ins)
                    if part.start == 0:
                        for f in range(n):
                            ins = dve.match_replace(src[:, f, :], vals[:, f, part], src[:, f, :], -3.0e38)
                        link(ins)

            def sum_places(h):
                heads = slice(h * TOPK, (h + 1) * TOPK)
                for a in range(2):
                    dve.wait_ge(places_weighed, 2 * h + a + 1)
                    ins = dve.tensor_reduce(ent[:, :, a, heads],
                                            hot_places[a].rearrange("p (t k) n -> p t k n", t=TT), AX_X, ALU.add)
                link(ins)

            for h in range(HP):
                when_emptied(dve, ("ps", h))
                best16(topv, topi_u, sc[:, h], 2 * TT)
                if h == 0:
                    dve.wait_ge(h_rounded, 1)
                    dve.tensor_tensor(h_hl[1], hs, h_hl[0], ALU.subtract).then_inc(h_split, 1)
                else:
                    sum_places(h - 1)
                v4 = topv.rearrange("p (t a) k -> p t a k", a=2)
                for lo, hi, at, n in ((0, 4, 0, TOPK), (4, TOPK, CA, 4)):
                    ins = dve.tensor_tensor(cand[:, :, at:at + (hi - lo) * n].rearrange("p t (a b) -> p t a b", b=n),
                                            v4[:, :, 0, lo:hi].unsqueeze(3).to_broadcast([P, TT, hi - lo, n]),
                                            v4[:, :, 1, 0:n].unsqueeze(2).to_broadcast([P, TT, hi - lo, n]), ALU.add)
                link(ins)
                best16(best, bpos_u, cand, TT)
                heads = slice(h * TOPK, (h + 1) * TOPK)
                ins = dve.tensor_tensor(ent[:, :, 2, heads], best, best[:, :, 0:1].to_broadcast([P, TT, TOPK]),
                                        ALU.subtract)
                if h == HP - 1:
                    ins.then_inc(soft_diff, 1)
                pos = bpos_u.rearrange("p t k -> p (t k)")
                for n, (by, op) in enumerate(((4, ALU.logical_shift_right), (15, ALU.bitwise_and),
                                              (2, ALU.logical_shift_right), (3, ALU.bitwise_and))):
                    dve.tensor_scalar(parts_u[:, n, :], pos, by, None, op)
                link(dve.tensor_copy(topi, topi_u))
                link(dve.tensor_copy(parts_f, parts_u))
                dve.tensor_scalar(low_rows, parts_f[:, 0, :], float(CA // TOPK), None, ALU.is_ge)
                dve.tensor_tensor(turn_ij[:, 1, :], parts_f[:, 3, :], parts_f[:, 1, :], ALU.subtract)
                link(dve.scalar_tensor_tensor(turn_ij[:, 0, :], parts_f[:, 2, :], float(4 - CA // 4),
                                              parts_f[:, 0, :], ALU.add, ALU.subtract))
                link(dve.tensor_tensor(turn_ij, turn_ij, low_rows.unsqueeze(1).to_broadcast([P, 2, n_ent]), ALU.mult))
                link(dve.tensor_tensor(turn_ij, turn_ij, parts_f[:, 0:2, :], ALU.add))
                for a in range(2):
                    dve.tensor_tensor(hot_places[a], turn_ij[:, a, :].unsqueeze(2).to_broadcast([P, n_ent, TOPK]),
                                      iota16.unsqueeze(1).to_broadcast([P, n_ent, TOPK]),
                                      ALU.is_equal).then_inc(places_hot, 1)
            sum_places(HP - 1)
            dve.wait_ge(soft_exp, 1)
            for t in range(TT):
                e3 = ent[:, t, 2, :].rearrange("p (h k) -> p h k", h=HP)
                ins = dve.tensor_reduce(bsum[:, t, :], e3, AX_X, ALU.add)
            link(ins)
            link(dve.reciprocal(bsum, bsum))
            for t in range(TT):
                e3 = ent[:, t, 2, :].rearrange("p (h k) -> p h k", h=HP)
                ins = dve.tensor_tensor(e3, e3, bsum[:, t, :].unsqueeze(2).to_broadcast([P, HP, TOPK]), ALU.mult)
            ins.then_inc(entries, 1)
            when_emptied(dve, ("tr", TT - 1))

            def one_hots(step):
                for q in range(4):
                    at_least(dve, spread, 4 * step + q - 3)
                    for one, key, done in ((oneA, 0, hot_n1), (oneB, 1, hot_n2)):
                        dve.tensor_tensor(one[:, 4 * q:4 * q + 4, :],
                                          C("iota").unsqueeze(1).to_broadcast([P, 4, P]),
                                          entT[:, key, bass.ds(16 * step + 4 * q, 4)].unsqueeze(2)
                                          .to_broadcast([P, 4, P]), ALU.is_equal).then_inc(done, 1)

            def split_u(g, s):
                dve.wait_ge(u_rounded, g + 1)
                dve.tensor_tensor(u_hl[s][1], u_raw, u_hl[s][0], ALU.subtract).then_inc(u_split, 1)

            def split_v(g, s):
                dve.wait_ge(v_rounded, g + 1)
                dve.tensor_tensor(v_hl[s][1], v_raw, v_hl[s][0], ALU.subtract).then_inc(v_split, 1)

            one_hots(0)
            with dve.Fori(1, T // 16) as step:
                one_hots(step)

            def coefs(g, s, turn, src=None):
                dve.wait_ge(g_in[s], 16 * turn)
                src = coef if src is None else src

                def multiply(j):
                    if src is coef:
                        dve.wait_ge(gelu_done, EG * (g - EARLY) + j + 1)
                    c = src[:, j, :].rearrange("p (n t) -> p n t", t=HALF)
                    dve.tensor_tensor(c, c, gslot[s][:, :, j, :], ALU.mult).then_inc(coef_mult, 1)

                def split(j):
                    dve.wait_ge(coef_rounded, EG * g + j + 1)
                    dve.tensor_tensor(c_hl[s][1][:, j, :], src[:, j, :], c_hl[s][0][:, j, :],
                                      ALU.subtract).then_inc(coef_done, 1)

                multiply(0)
                for j in range(1, EG):
                    multiply(j)
                    split(j - 1)
                split(EG - 1)

            def add(g):
                at_least(dve, added, KD * g)
                for m in range(KD):
                    dve.wait_ge(out_done, KD * g + m + 1)
                    x = resid[:, m, 0:T]
                    dve.tensor_tensor(x, x, ps[:, 4 + m % 4, :], ALU.add).then_inc(added, 1)

            def period(g, s, turn, last=0):
                if last < 2:
                    split_u(g + 2, s)
                if last < 3:
                    split_v(g + 1, 1 - s)
                    coefs(g + 1, 1 - s, turn)
                add(g)

            split_v(0, 0)
            coefs(0, 0, 1, early[:, 0])
            for g in range(1, EARLY):
                split_v(g, g % 2)
                coefs(g, g % 2, g // 2 + 1, early[:, g])
                add(g - 1)
            period(EARLY - 1, 1, EARLY // 2 + 1)
            with dve.Fori(EARLY // 2, GROUPS // 2 - 1) as it:
                period(2 * it, 0, it + 1)
                period(2 * it + 1, 1, it + 2)
            period(GROUPS - 2, 0, GROUPS // 2, last=2)
            period(GROUPS - 1, 1, 0, last=3)

        @block.gpsimd
        def _(pool):
            pool.wait_ge(first_consts, 32)
            def split_group(i):
                name = SPLIT[i]
                g = WN[name]
                _, k, n, _ = WEIGHTS[g]
                pool.wait_ge(w_in[g % NW], 16 * (g // NW + 1))
                if i >= NU:
                    when_filled(pool, last_job(SPLIT[i - NU]))
                up, low = W_parts(name)
                nc.gpsimd.tensor_tensor(up, W(name), C("ones", 0, 1).unsqueeze(1).to_broadcast([P, k, n]),
                                        ALU.mult).then_inc(part_rounded, 1)
                pool.wait_ge(part_rounded, i + 1)
                nc.gpsimd.tensor_tensor(low, W(name), up, ALU.subtract).then_inc(weights_split, 1)

            for i in range(len(SPLIT) - 2):
                split_group(i)

            def weigh(step):
                for q in range(4):
                    pool.wait_ge(hot_n1, 4 * step + q + 1)
                    one = oneA[:, 4 * q:4 * q + 4, :]
                    nc.gpsimd.tensor_tensor(one, one, entT[:, 2, bass.ds(16 * step + 4 * q, 4)].unsqueeze(2)
                                            .to_broadcast([P, 4, P]), ALU.mult).then_inc(hot, 1)

            def weigh_places(h):
                i4 = topi.rearrange("p (t a) k -> p t a k", a=2)
                for a in range(2):
                    pool.wait_ge(places_hot, 2 * h + a + 1)
                    places = hot_places[a].rearrange("p (t k) n -> p t k n", t=TT)
                    nc.gpsimd.tensor_tensor(places, places, i4[:, :, a, :].unsqueeze(2)
                                            .to_broadcast([P, TT, TOPK, TOPK]), ALU.mult).then_inc(places_weighed, 1)

            for h in range(HP):
                weigh_places(h)
                if h < 2:
                    split_group(len(SPLIT) - 2 + h)
                g = h - (HP - EARLY - 1)
                if g >= 0:
                    pool.wait_ge(u_rounded, g + 1)
                    nc.gpsimd.tensor_tensor(early_u_hl[g % 2][1], u_raw, early_u_hl[g % 2][0],
                                            ALU.subtract).then_inc(u_split, 1)
            when_emptied(pool, ("tr", TT - 1))
            weigh(0)
            with pool.Fori(1, T // 16) as step:
                weigh(step)


def at_least(eng, s, value):
    if not isinstance(value, int) or value > 0:
        eng.wait_ge(s, value)


def tables():
    c = np.zeros((P, NCONST), np.float32)

    def put(name, m):
        at, n = CONST[name]
        c[:, at:at + n] = m

    r = np.arange(P)
    put("ident", np.eye(P))
    put("ones", 1.0)
    put("heads64", (r[:, None] // 64 == r[None, :] // 64))
    rot = np.zeros((P, P), np.float32)
    for m in range(P):
        low = m % ROPE < ROPE // 2
        rot[m + 32 if low else m - 32, m] = -1.0 if low else 1.0
    put("rot", rot)
    put("iota", r[None, :])
    col = np.arange(T)
    at = T - P + r[:, None]
    seen = col[None, :] // CHUNK <= at // CHUNK
    put("dist", np.where(seen, np.abs(at - col[None, :]), 1e30))
    j, i = r[:, None], r[None, :]
    levels = [j == i]
    for s in LEVELS:
        levels.append((j // (2 * s) == i // (2 * s)) & (j % (2 * s) < s) & (i % (2 * s) >= s))
    put("levels", np.concatenate(levels, 1))
    reset = np.ones(TM)
    reset[0::P] = 0.0
    put("reset", reset[None, :])
    half = ROPE // 2
    inv = (np.float32(10000.0) ** (-np.arange(half, dtype=np.float32) / np.float32(half))).astype(np.float32)
    pos = np.concatenate([np.arange(META, TM), np.arange(META)]).astype(np.float32)
    ang = (inv[r % half][:, None] * pos[None, :]).astype(np.float32)
    put("cos", np.cos(ang))
    put("sin", np.sin(ang))
    return c


def kernel(**inputs):
    import concourse.bacc as _bacc
    from concourse.bass_utils import run_bass_kernel_spmd as _run

    x = {n: np.asarray(a) for n, a in inputs.items()}
    f = np.float32

    def cols(a):
        return np.asarray(a).reshape(-1, P).T

    def feature_major(a):
        return np.ascontiguousarray(a.T.reshape(-1, P, a.shape[0]).transpose(1, 0, 2))

    vecs = np.zeros((P, NVEC), f)

    def put(name, m):
        at, n = VEC[name]
        vecs[:m.shape[0], at:at + n] = m

    put("pre", cols(x["pre_norm_gain"][0]))
    put("mix", cols(x["norm_mix_2"][0]))
    put("subln", cols(x["subln_gain"][0]))
    put("conv", x["conv_w"][0].reshape(3, 4, P).transpose(2, 0, 1).reshape(P, 12))
    put("post", cols(x["post_norm_gain"][0]))
    put("ple", cols(x["ple_norm_gain"][0]))
    put("qnorm", cols(x["mla_q_norm_2"][0]))
    put("kvnorm", cols(x["mla_kv_norm_2"][0]))
    put("qn", cols(x["qn_nope_2"][0]))
    put("kn", cols(x["kn_nope_2"][0]))
    put("qp", np.concatenate([x["qn_pe_2"][0], x["qn_pe_2"][0]])[:, None])
    put("kp", np.concatenate([x["kn_pe_2"][0], x["kn_pe_2"][0]])[:, None])
    put("ba", cols(x["gla_b_a_2"][0]))
    put("gnorm", cols(x["gla_norm_2"][0]))
    put("ffn", cols(x["norm_ffn_2"][0]))
    put("lam", np.stack([x["lambda_q1"][0], x["lambda_q2"][0], x["lambda_k1"][0], x["lambda_k2"][0]], 1))
    put("eps", np.full((P, 1), EPS, f))
    put("subeps", np.full((P, 1), SUBLN_EPS, f))

    w1, w2 = x["w_in"][0], x["w_in_2"][0]
    part = {}

    def cut(name, m, width=256):
        for n in range(m.shape[1] // width):
            part[f"{name}{n}"] = m[:, n * width:(n + 1) * width]

    for n, g in enumerate(("q", "k", "v", "za", "b", "c", "u", "zc")):
        cut(g, w1[:, n * 512:(n + 1) * 512])
    at = 0
    two = {}
    for g, n in (("cq", 384), ("ckv", 256), ("kpe", 64), ("gq", 512), ("gk", 512), ("gv", 1024), ("ga", 16),
                 ("gg", 1024), ("ta", 1024), ("tb", 1024)):
        two[g] = w2[:, at:at + n]
        at += n
    part["cq0"], part["cq1"] = two["cq"][:, 0:256], two["cq"][:, 256:384]
    cut("ckv", two["ckv"], 128)
    part["kpe0"] = np.concatenate([two["kpe"], two["kpe"]], 1)
    part["ga0"] = two["ga"]
    cut("gk", two["gk"], 128)
    uq = x["mla_w_uq_2"][0].reshape(384, HM, 192)
    cut("uqn", uq[:, :, 0:128].reshape(384, 1024), 512)
    part["uqp"] = uq[:, :, 128:192].reshape(384, 512)
    ukv = x["mla_w_ukv_2"][0].reshape(256, HM, 256)
    part["ukv0"], part["ukv1"] = ukv[:, :, 0:128].reshape(256, 1024), ukv[:, :, 128:256].reshape(256, 1024)
    part["ple"] = x["w_ple_proj"][0]
    for g, m in (("wo", x["w_out"][0]), ("pg", x["w_ple_gate"][0]), ("gq", two["gq"]), ("gv", two["gv"]),
                 ("gg", two["gg"]), ("ta", two["ta"]), ("tb", two["tb"]), ("oa", x["w_o_mla_2"][0]),
                 ("ob", x["w_o_gla_2"][0]), ("w2", x["w_out_2"][0]), ("pq", x["peer_w_q_2"][0])):
        cut(g, m)
    weights = np.concatenate([part[n].reshape(k, P, c).transpose(1, 0, 2).reshape(P, k * c) for n, k, c, _ in WEIGHTS],
                             1)

    u = x["peer_u_2"][0].reshape(P, GROUPS, EG, KD, P)
    v = x["peer_v_2"][0].reshape(P, GROUPS, EG, D)
    arrays = {
        "xT": feature_major(x["x"][0]), "metaT": feature_major(x["meta_2"]), "pT": feature_major(x["p"][0, 0]),
        "consts": tables(), "vecs": vecs, "weights": np.ascontiguousarray(weights),
        "wa2": x["gla_w_a2_2"][0], "keysT": np.ascontiguousarray(x["peer_keys_2"][0].transpose(2, 0, 1)),
        "uT": np.ascontiguousarray(u.transpose(1, 4, 3, 2, 0)).reshape(GROUPS, P, KD * EG * P),
        "vT": np.ascontiguousarray(v.transpose(1, 0, 2, 3)).reshape(GROUPS, P, EG * D),
    }
    nc = _bacc.Bacc("TRN2", target_bir_lowering=False, num_devices=1,
                    dynamic_dma_scratch_size=256)
    A, ins = {}, {}
    for name, a in arrays.items():
        ins[f"in_{name}_dram"] = np.ascontiguousarray(a)
        A[name] = nc.dram_tensor(f"in_{name}_dram", a.shape, F32, kind="ExternalInput").ap()
    A["gates"] = nc.dram_tensor("gate_table", (P, PIECES, GROUPS, EG * HALF), F32, kind="Internal").ap()
    A["x2"] = nc.dram_tensor("x_after_first_block", (P, KD, T), F32, kind="Internal").ap()
    A["out"] = nc.dram_tensor("out_0_dram", (D, T), F32, kind="ExternalOutput").ap()
    build(nc, A)
    r = _run(nc, [ins], core_ids=[0])
    return np.ascontiguousarray(r.results[0]["out_0_dram"].T)[None]
```
